# Optimizing a Trainium2 kernel written in Bass

```python
import math
import jax, jax.numpy as jnp
from jax import lax
import numpy as np

D_MODEL = 1024
BATCH = 1
SEQ = 512
DEPTH = 2

N_A = DEPTH // 2
N_B = DEPTH - N_A
PLE_DIM = 256
SSM_WIDTH = D_MODEL
SSM_GROUP = 16
SSM_GROUPS = SSM_WIDTH // SSM_GROUP
SSM_STATE = 64
SSM_CHUNK = 128
DT_MIN = 0.001
DT_MAX = 0.1
HEAD_DIM = 64
V_DIM = 2 * HEAD_DIM
N_HEADS = D_MODEL // V_DIM
ATTN_WIDTH = N_HEADS * V_DIM
Q_BLOCK = 128
REL_BUCKETS = 32
REL_MAX_EXACT = REL_BUCKETS // 2
REL_MAX_DIST = 128
EPS = 1e-6
NEG_INF = -1e30

kernel_name = "yoco_s5_diffattn_hybrid"

def rmsnorm(x, g=None):
    xf = x.astype(jnp.float32)
    y = xf * lax.rsqrt(jnp.mean(xf * xf, axis=-1, keepdims=True) + EPS)
    if g is not None:
        y = y * g.astype(jnp.float32)
    return y.astype(x.dtype)

def cmul(ar, ai, br, bi):
    return ar * br - ai * bi, ar * bi + ai * br

def s5_scan(u, lam_re, lam_im, log_dt, b_re, b_im, c_re, c_im, d):
    f32 = jnp.float32
    bsz, seq, _ = u.shape
    uf = u.astype(f32).reshape(bsz, seq, SSM_GROUPS, SSM_GROUP)
    dt = jnp.exp(log_dt.astype(f32))[:, None]
    lr, li = lam_re.astype(f32), lam_im.astype(f32)
    mag = jnp.exp(lr * dt)
    ab_re, ab_im = mag * jnp.cos(li * dt), mag * jnp.sin(li * dt)
    den = lr * lr + li * li
    nr, ni = ab_re - 1.0, ab_im
    f_re = (nr * lr + ni * li) / den
    f_im = (ni * lr - nr * li) / den
    bb_re, bb_im = cmul(f_re[..., None], f_im[..., None], b_re.astype(f32), b_im.astype(f32))
    cr, ci = c_re.astype(f32), c_im.astype(f32)
    n_chunks = seq // SSM_CHUNK
    u_chunks = uf.reshape(bsz, n_chunks, SSM_CHUNK, SSM_GROUPS, SSM_GROUP).transpose(1, 0, 2, 3, 4)
    a_shape = (bsz, SSM_CHUNK, SSM_GROUPS, SSM_STATE)
    a_re = jnp.broadcast_to(ab_re, a_shape)
    a_im = jnp.broadcast_to(ab_im, a_shape)

    def combine(e1, e2):
        a1r, a1i, b1r, b1i = e1
        a2r, a2i, b2r, b2i = e2
        ar, ai = cmul(a2r, a2i, a1r, a1i)
        br, bi = cmul(a2r, a2i, b1r, b1i)
        return ar, ai, br + b2r, bi + b2i

    def chunk_step(carry, uc):
        h_re, h_im = carry
        bu_re = jnp.einsum('btgc,gpc->btgp', uc, bb_re)
        bu_im = jnp.einsum('btgc,gpc->btgp', uc, bb_im)
        pr, pi, sr, si = lax.associative_scan(combine, (a_re, a_im, bu_re, bu_im), axis=1)
        hr, hi = cmul(pr, pi, h_re[:, None], h_im[:, None])
        sr, si = sr + hr, si + hi
        y = jnp.einsum('btgp,gcp->btgc', sr, cr) - jnp.einsum('btgp,gcp->btgc', si, ci)
        return (sr[:, -1], si[:, -1]), y

    init = (jnp.zeros((bsz, SSM_GROUPS, SSM_STATE), f32), jnp.zeros((bsz, SSM_GROUPS, SSM_STATE), f32))
    _, ys = lax.scan(chunk_step, init, u_chunks)
    y = ys.transpose(1, 0, 2, 3, 4).reshape(bsz, seq, SSM_WIDTH)
    y = y + d.astype(f32) * uf.reshape(bsz, seq, SSM_WIDTH)
    return y.astype(u.dtype)

def ssm_layer(x, norm_g, w_in, lam_re, lam_im, log_dt, b_re, b_im, c_re, c_im, d, w_glu, w_out):
    h = rmsnorm(x, norm_g)
    u, z = jnp.split(h @ w_in, 2, axis=-1)
    y = jax.nn.gelu(s5_scan(u, lam_re, lam_im, log_dt, b_re, b_im, c_re, c_im, d))
    ga, gb = jnp.split(y @ w_glu, 2, axis=-1)
    y = ga * jax.nn.sigmoid(gb)
    return (y * jax.nn.silu(z)) @ w_out

def shared_kv(x, kv_norm_g, w_k, w_v, k_norm_g):
    bsz, seq, _ = x.shape
    h = rmsnorm(x, kv_norm_g)
    k = rmsnorm((h @ w_k).reshape(bsz, seq, N_HEADS, 2, HEAD_DIM), k_norm_g)
    v = (h @ w_v).reshape(bsz, seq, N_HEADS, V_DIM)
    return k, v

def rel_bucket(rel):
    n = jnp.maximum(rel, 0)
    nf = jnp.maximum(n, 1).astype(jnp.float32)
    large = REL_MAX_EXACT + (jnp.log(nf / REL_MAX_EXACT) / math.log(REL_MAX_DIST / REL_MAX_EXACT)
                             * (REL_BUCKETS - REL_MAX_EXACT)).astype(jnp.int32)
    large = jnp.minimum(large, REL_BUCKETS - 1)
    return jnp.where(n < REL_MAX_EXACT, n, large)

def diff_attn_layer(x, k, v, rel_bias, layer_idx, norm_g, w_in, q_norm_g,
                    lam_q1, lam_k1, lam_q2, lam_k2, subln_g, w_out):
    f32 = jnp.float32
    bsz, seq, _ = x.shape
    h = rmsnorm(x, norm_g)
    q, z = jnp.split(h @ w_in, 2, axis=-1)
    q = rmsnorm(q.reshape(bsz, seq, N_HEADS, 2, HEAD_DIM), q_norm_g)
    lam_init = 0.8 - 0.6 * math.exp(-0.3 * layer_idx)
    lam = (jnp.exp(jnp.sum(lam_q1.astype(f32) * lam_k1.astype(f32)))
           - jnp.exp(jnp.sum(lam_q2.astype(f32) * lam_k2.astype(f32))) + lam_init)
    n_blocks = seq // Q_BLOCK
    qb = q.reshape(bsz, n_blocks, Q_BLOCK, N_HEADS, 2, HEAD_DIM).transpose(1, 0, 2, 3, 4, 5)
    k_pos = jnp.arange(seq, dtype=jnp.int32)
    scale = HEAD_DIM ** -0.5
    table = rel_bias.astype(f32)

    def block(args):
        q_blk, blk = args
        q_pos = blk * Q_BLOCK + jnp.arange(Q_BLOCK, dtype=jnp.int32)
        rel = q_pos[:, None] - k_pos[None, :]
        bias = table[rel_bucket(rel)].transpose(2, 0, 1)
        s = jnp.einsum('bqhcd,bkhcd->bchqk', q_blk, k, preferred_element_type=f32) * scale + bias
        s = jnp.where(rel >= 0, s, NEG_INF)
        pm = jax.nn.softmax(s, axis=-1)
        attn = pm[:, 0] - lam * pm[:, 1]
        return jnp.einsum('bhqk,bkhe->bqhe', attn.astype(v.dtype), v)

    o = lax.map(block, (qb, jnp.arange(n_blocks, dtype=jnp.int32)))
    o = o.transpose(1, 0, 2, 3, 4).reshape(bsz, seq, N_HEADS, V_DIM)
    o = (rmsnorm(o, subln_g) * (1.0 - lam_init)).reshape(bsz, seq, ATTN_WIDTH)
    return (o * jax.nn.silu(z)) @ w_out

def per_layer_embed(x, p_i, w_proj, w_gate):
    return x + jax.nn.sigmoid(rmsnorm(x) @ w_gate) * (p_i @ w_proj)

def setup_inputs(seed: int = 0) -> dict:
    key = jax.random.key(seed)
    ks = iter(jax.random.split(key, 40))

    def nrm(shape, std):
        return jax.random.normal(next(ks), shape, jnp.float32) * std

    def gain(shape):
        return 1.0 + nrm(shape, 0.02)

    E, G, P, C = SSM_WIDTH, SSM_GROUPS, SSM_STATE, SSM_GROUP
    inp = {}
    inp['x'] = nrm((BATCH, SEQ, D_MODEL), 1.0)
    inp['p'] = nrm((DEPTH, BATCH, SEQ, PLE_DIM), 1.0)
    inp['a_norm_g'] = gain((N_A, D_MODEL))
    inp['a_w_in'] = nrm((N_A, D_MODEL, 2 * E), D_MODEL ** -0.5)
    inp['a_lam_re'] = -0.5 + nrm((N_A, G, P), 0.01)
    inp['a_lam_im'] = jnp.float32(math.pi) * jnp.arange(P, dtype=jnp.float32) + nrm((N_A, G, P), 0.01)
    inp['a_log_dt'] = jax.random.uniform(next(ks), (N_A, G), jnp.float32, math.log(DT_MIN), math.log(DT_MAX))
    inp['a_b_re'] = nrm((N_A, G, P, C), (2 * C) ** -0.5)
    inp['a_b_im'] = nrm((N_A, G, P, C), (2 * C) ** -0.5)
    inp['a_c_re'] = nrm((N_A, G, C, P), 0.5)
    inp['a_c_im'] = nrm((N_A, G, C, P), 0.5)
    inp['a_d'] = nrm((N_A, E), 1.0)
    inp['a_w_glu'] = nrm((N_A, E, 2 * E), E ** -0.5)
    inp['a_w_out'] = nrm((N_A, E, D_MODEL), E ** -0.5)
    inp['kv_norm_g'] = gain((D_MODEL,))
    inp['w_k'] = nrm((D_MODEL, N_HEADS * 2 * HEAD_DIM), D_MODEL ** -0.5)
    inp['w_v'] = nrm((D_MODEL, N_HEADS * V_DIM), D_MODEL ** -0.5)
    inp['k_norm_g'] = gain((HEAD_DIM,))
    inp['b_norm_g'] = gain((N_B, D_MODEL))
    inp['b_w_in'] = nrm((N_B, D_MODEL, N_HEADS * 2 * HEAD_DIM + ATTN_WIDTH), D_MODEL ** -0.5)
    inp['b_q_norm_g'] = gain((N_B, HEAD_DIM))
    inp['b_lam_q1'] = nrm((N_B, HEAD_DIM), 0.1)
    inp['b_lam_k1'] = nrm((N_B, HEAD_DIM), 0.1)
    inp['b_lam_q2'] = nrm((N_B, HEAD_DIM), 0.1)
    inp['b_lam_k2'] = nrm((N_B, HEAD_DIM), 0.1)
    inp['b_subln_g'] = gain((N_B, V_DIM))
    inp['b_w_out'] = nrm((N_B, ATTN_WIDTH, D_MODEL), ATTN_WIDTH ** -0.5)
    inp['rel_bias'] = nrm((REL_BUCKETS, N_HEADS), 0.5)
    inp['ple_w_proj'] = nrm((DEPTH, PLE_DIM, D_MODEL), 0.5 * PLE_DIM ** -0.5)
    inp['ple_w_gate'] = nrm((DEPTH, D_MODEL, D_MODEL), D_MODEL ** -0.5)
    return inp

def reference(x, p, a_norm_g, a_w_in, a_lam_re, a_lam_im, a_log_dt, a_b_re, a_b_im,
              a_c_re, a_c_im, a_d, a_w_glu, a_w_out, kv_norm_g, w_k, w_v, k_norm_g,
              b_norm_g, b_w_in, b_q_norm_g, b_lam_q1, b_lam_k1, b_lam_q2, b_lam_k2,
              b_subln_g, b_w_out, rel_bias, ple_w_proj, ple_w_gate):
    k = v = None
    for i in range(DEPTH):
        if i < N_A:
            j = i
            x = x + ssm_layer(x, a_norm_g[j], a_w_in[j], a_lam_re[j], a_lam_im[j], a_log_dt[j],
                              a_b_re[j], a_b_im[j], a_c_re[j], a_c_im[j], a_d[j], a_w_glu[j], a_w_out[j])
        else:
            if i == N_A:
                k, v = shared_kv(x, kv_norm_g, w_k, w_v, k_norm_g)
            j = i - N_A
            x = x + diff_attn_layer(x, k, v, rel_bias, i, b_norm_g[j], b_w_in[j], b_q_norm_g[j],
                                    b_lam_q1[j], b_lam_k1[j], b_lam_q2[j], b_lam_k2[j],
                                    b_subln_g[j], b_w_out[j])
        x = per_layer_embed(x, p[i], ple_w_proj[i], ple_w_gate[i])
    return x


_drawn_inputs = setup_inputs


def setup_inputs(seed=0):
    import zlib

    import numpy as np

    out = dict(_drawn_inputs(seed))
    spreads = {}
    factors = {'a_norm_g': 7.872,
     'a_lam_re': 8.0,
     'kv_norm_g': 5.733,
     'k_norm_g': 8.0,
     'b_norm_g': 5.893,
     'b_q_norm_g': 8.0,
     'b_lam_q1': 5.462,
     'b_lam_k1': 8.0,
     'b_subln_g': 8.0}
    for name, (base, spread) in spreads.items():
        noise = np.random.default_rng([zlib.crc32(name.encode()), seed]).standard_normal(out[name].shape)
        drawn = base * np.exp(spread * noise) if base else spread * noise
        out[name] = __import__('jax').numpy.asarray(drawn.astype(out[name].dtype))
    for name, factor in factors.items():
        out[name] = (out[name] * factor).astype(out[name].dtype)
    return out
```

```python
import math
from contextlib import ExitStack

import numpy as np
import concourse.bass as bass
from concourse import mybir

F32 = mybir.dt.float32
F32R = mybir.dt.float32r
ACT = mybir.ActivationFunctionType
ALU = mybir.AluOpType
AX = mybir.AxisListType

P = 128
D = 1024
T = 512
KT = D // P
CH = 8
NC = T // CH
G = 64
GC = 16
ST = 64
GT = P // GC
PADJ = 2 * CH - 1
H = 8
HD = 64
QB = T // P
PLE = 256
PK = PLE // P
EPS = 1e-6
LAM_INIT = 0.8 - 0.6 * math.exp(-0.3 * 1)
NEG = -1e30
BUCKETS = 32
REV = 640

RAW, RING = 2, 4

C_ID, C_J1, C_J2, C_ONE, C_BLK, C_HOT = 0, P, 2 * P, 3 * P, 4 * P, 5 * P
C_SGN = C_HOT + REV
C_END = C_SGN + 1

V_AG, V_D, V_KVG, V_BG, V_QG, V_KG, V_SUB, V_ROWS = 0, 8, 16, 24, 32, 33, 34, 35

TWO_PI = 2 * math.pi
PI_A = 6.28125
PI_B = float(np.float32(np.round((TWO_PI - PI_A) * 2 ** 20) / 2 ** 20))
PI_C = float(np.float32(TWO_PI - PI_A - PI_B))
MAGIC = 12582912.0

S_IN, S_GLU, S_P0, S_OUT, S_G0, S_K, S_V, S_Q, S_Z, S_BO, S_P1, S_G1, S_END = (
    0, 16, 32, 34, 42, 50, 58, 66, 74, 82, 90, 92, 100)


N_PAR = 8 + 4 + 1 + 1 + 4 + 2
T_MOVES = ((0, 128, 0), (32, 32, 0), (64, 32, 32), (96, 32, 64), (64, 64, 0), (96, 32, 0))
T_COPIES = len(T_MOVES)


def in_order():
    order = [("u", 0), ("u", 1)]
    for m in range(KT):
        order.append(("z", m))
        if m + 2 < KT:
            order.append(("u", m + 2))
    return order


IN_ORDER = in_order()
SLAB_OF = {x: i for i, x in enumerate(IN_ORDER)}


def build(nc, a, out):
    xd = nc.dram_tensor("xT_spill", (KT, P, T), F32, kind="Internal").ap()
    zd = nc.dram_tensor("gate_spill", (KT, P, T), F32, kind="Internal").ap()
    x1d = nc.dram_tensor("x1_spill", (KT, P, T), F32, kind="Internal").ap()
    ud = nc.dram_tensor("u_turn", (KT, P, T), F32, kind="Internal").ap()
    yd = nc.dram_tensor("y_turn", (KT, P, T), F32, kind="Internal").ap()
    bd = nc.dram_tensor("bias_rows", (H, P, REV), F32, kind="Internal").ap()

    def mk(name, shape, dt=F32):
        return nc.sbuf_tensor(name, shape, dt)

    with ExitStack() as keep:
        def sb(name, shape, dt=F32):
            return keep.enter_context(mk(name, shape, dt))

        def sem(name):
            return keep.enter_context(nc.semaphore(name))

        def sems(names):
            return [sem(name) for name in names.split()]

        raw = [sb(f"raw{i}", [P, D]) for i in range(RAW)]
        whi = [sb(f"whi{i}", [P, D], F32R) for i in range(RING)]
        wlo = [sb(f"wlo{i}", [P, D], F32R) for i in range(RING)]
        cst = sb("cst", [P, C_END])
        VT = sb("VT", [P, V_ROWS])
        R = sb("R", [P, T])
        small = sb("small", [P, 64])
        oss = small[:, 16:32]
        hi0 = sb("hi0", [P, KT, T], F32R)
        lo0 = sb("lo0", [P, KT, T], F32R)
        ident = cst[:, C_ID:C_ID + P]
        epsc, negl, lamc = small[:, 0:1], small[:, 1:2], small[:, 2:6]

        with ExitStack() as s5:
            def sa(name, shape, dt=F32):
                return s5.enter_context(mk(name, shape, dt))
            Y = sa("Y", [P, KT, T])
            Pp = sa("Pp", [P, GT, PADJ, GC])
            Win = sa("Win", [P, GT, P])
            Wsw = sa("Wsw", [P, GT, P])
            TT = sa("TT", [P, GT, CH, GC])
            M = sa("M", [P, GT, CH, GC])
            Msw = sa("Msw", [P, 2, GT, CH * GC])
            XB1 = sa("XB1", [P, G, GC])
            XB2 = sa("XB2", [P, G, GC])
            XC1 = sa("XC1", [P, G, GC])
            XC2 = sa("XC2", [P, G, GC])
            pw = [sa(f"pw{i}", [P, CH + 1, G]) for i in range(2)]
            gt = [sa(f"gt{i}", [P, CH + 1, G]) for i in range(2)]
            ft = [sa(f"ft{i}", [P, CH + 1, G]) for i in range(2)]
            r8 = sa("r8", [P, G])
            Ct = sa("Ct", [P, T])
            St = sa("St", [P, T])
            tmp = sa("tmp", [P, D])
            U = sa("U", [P, 2, GT, NC])
            w1 = sa("w1", [P, T])
            w2 = sa("w2", [P, T])
            gs = sa("gs", [P, T])
            p1 = sa("p1", [P, T])
            p2 = sa("p2", [P, T])
            ysb = sa("ysb", [P, 2, T])
            yT = sa("yT", [P, 2, T])
            uT = sa("uT", [P, 4, T])
            st = sa("st", [P, 2, T])
            r8x = sa("r8x", [P, T])
            tz = sa("tz", [P, T])
        xrow = Y[:, :, :].rearrange("p a b -> p (a b)")
        pt = ysb[:, :, :].rearrange("p a b -> p (a b)")
        yTf = yT[:, :, :].rearrange("p a b -> p (a b)")

        with ExitStack() as rest:
            def sc(name, shape, dt=F32, scope=rest):
                return scope.enter_context(mk(name, shape, dt))
            hi1 = sc("hi1", [P, KT, T], F32R)
            lo1 = sc("lo1", [P, KT, T], F32R)
            with ExitStack() as e:
                bias = sc("bias", [P, 2, T], F32, e)
                sco = [sc(f"sco{c}", [P, 2, T], F32, e) for c in range(2)]
                ab = sc("ab", [P, 2, T], F32, e)
                ath = sc("ath", [P, 2, T], F32R, e)
                atl = sc("atl", [P, 2, T], F32R, e)
                on = sc("on", [P, T], F32, e)
                stat = sc("stat", [P, 2, 16], F32, e)
            hi2 = sc("hi2", [P, KT, T], F32R)
            lo2 = sc("lo2", [P, KT, T], F32R)
            with ExitStack() as e:
                zz = sc("zz", [P, KT, T], F32, e)
                xT = sc("xT", [P, KT, T], F32, e)
                prow = sc("prow", [P, QB, PLE], F32, e)
                phi = sc("phi", [P, PK, T], F32R, e)
                plo = sc("plo", [P, PK, T], F32R, e)
                tb = [sc(f"tb{i}", [P, 2, T], F32, e) for i in range(4)]
            with ExitStack() as e:
                Vhi = sc("Vhi", [P, H, T], F32R, e)
                Vlo = sc("Vlo", [P, H, T], F32R, e)
                ta = [sc(f"ta{i}", [P, 2, T], F32, e) for i in range(3)]
                sz = sc("sz", [P, H, T], F32, e)
            with ExitStack() as e:
                x1b = sc("x1b", [P, KT, T], F32, e)
                pr2 = sc("pr2", [P, KT, T], F32, e)
                prow2 = sc("prow2", [P, QB, PLE], F32, e)
                phi2 = sc("phi2", [P, PK, T], F32R, e)
                plo2 = sc("plo2", [P, PK, T], F32R, e)
                tc = [sc(f"tc{i}", [P, 2, T], F32, e) for i in range(4)]
        bk = [keep.enter_context(nc.psum_tensor(f"bank{i}", [P, T], F32)) for i in range(8)]

        class s:
            cst_in, par_in, b_in, hot_in, par_T, par_read = sems("cst_in par_in b_in hot_in par_T par_read")
            vt, dt, xr, mag, lam_dot, lam_e = sems("vt dt xr mag lam_dot lam_e")
            rr, sin, hot, rows_mm, row0, rows_ev = sems("rr sin hot rows_mm row0 rows_ev")
            rows_out, zeroed, dve_step = sems("rows_out zeroed dve_step")
            c_T, xc1, xc2, xc2_mm, xb1, xb2 = sems("c_T xc1 xc2 xc2_mm xb1 xb2")
            xb2_mm, r8 = sems("xb2_mm r8")
            w_hi, w_split, w_used = sems("w_hi w_split w_used")
            x_T, x_copied, x_hi, x_lo, x_sq, summed = sems("x_T x_copied x_hi x_lo x_sq summed")
            r_ln, r_norm, r1 = sems("r_ln r_norm r1")
            u_ev, u_out, z_ev, z_tanh, zz = sems("u_ev u_out z_ev z_tanh zz")
            p_built, p_T, win, t_mm, t_built, m_built = sems("p_built p_T win t_mm t_built m_built")
            ratio, ssm_w, rot, scan, p_rot, ssm_y = sems("ratio ssm_w rot scan p_rot ssm_y")
            y_ev, y_out, comb, gelu, y_hi, y_lo = sems("y_ev y_out comb gelu y_hi y_lo")
            zz_in, xT_in, glu_tanh, glu_y, glu_y3, glu_hi = sems("zz_in xT_in glu_tanh glu_y glu_y3 glu_hi")
            glu_lo, p_in, p2_in, pT, p_hi, p_lo = sems("glu_lo p_in p2_in pT p_hi p_lo")
            pr_ev, pr2_ev = sems("pr_ev pr2_ev")
            xa, xa_hi, xa_lo, xa_sq, g_ev, g_tanh = sems("xa xa_hi xa_lo xa_sq g_ev g_tanh")
            g_pr, x1, x1_sq, n1_hi, n1_lo, n2_hi = sems("g_pr x1 x1_sq n1_hi n1_lo n2_hi")
            n2_lo, x1_in, x2, out_T, out_ev = sems("n2_lo x1_in x2 out_T out_ev")
            k_ev, k_sq, k_bs, k_ln, k_r, k_n = sems("k_ev k_sq k_bs k_ln k_r k_n")
            k_hi, k_lo, v_ev, v_T, v_hi, v_lo = sems("k_hi k_lo v_ev v_T v_hi v_lo")
            b_z, b_tanh, sz = sems("b_z b_tanh sz")
            sc, sc_read, neg, exp, soft, at = sems("sc sc_read neg exp soft at")
            at_hi, at_lo, pv, o_sq, o_ln, o_r = sems("at_hi at_lo pv o_sq o_ln o_r")
            on, o_T, o_ev, o_hi, o_lo = sems("on o_T o_ev o_hi o_lo")
        raw_in = [sem(f"raw_in{i}") for i in range(RAW)]
        x_in = [sem(f"x_in{i}") for i in range(QB)]
        xs_out = [sem(f"xs_out{i}") for i in range(4)]
        u_in = [sem(f"u_in{i}") for i in range(2)]
        y_in = [sem(f"y_in{i}") for i in range(2)]
        msw_in = [sem(f"msw_in{i}") for i in range(2)]
        z_out = [sem(f"z_out{i}") for i in range(2)]
        x1_out = [sem(f"x1_out{i}") for i in range(2)]
        bias_in = [sem(f"bias_in{i}") for i in range(2)]
        o_out = [sem(f"o_out{i}") for i in range(2)]

        def after(eng, which, n):
            if n > 0:
                eng.wait_ge(which, n)

        def view(t, off, dims, p0=0, np_=P):
            pitch = int(np.prod(t.shape[1:]))
            return bass.AP(t, p0 * pitch + off, [[pitch, np_]] + [list(d) for d in dims])

        def cols(t, m):
            return t[:, m, :]

        def ps(b, n=T, o=0):
            return bk[b][:, o:o + n]

        def vcol(r):
            return VT[:, r:r + 1]

        def pt(i, n=1):
            return view(ysb, i * 64, [[1, 64 * n]])
        LR_, LI_, DT_, XR_, TH_, KQ_, RR_, SN_, SH_, CO_, MG_, T1_, T2_, FR_, FI_, DN_ = range(16)

        lam_v = view(yT, 448, [[64, 4], [1, 64]])
        block = keep.enter_context(nc.Block())

        @block.sync
        def _(sp):
            sent = [0]

            def slab_source(S):
                def w(t, c, n=P):
                    return t[:, c:c + n].rearrange("(k p) c -> p k c", p=P)
                if S < S_GLU:
                    kind, m = IN_ORDER[S]
                    return w(a["a_w_in"][0], m * P + (D if kind == "z" else 0))
                if S < S_P0:
                    m, half = divmod(S - S_GLU, 2)
                    return w(a["a_w_glu"][0], m * P + (0 if half else D))
                for base, end, t, c0, n in (
                        (S_P0, S_OUT, a["ple_w_proj"][0], 0, T), (S_OUT, S_G0, a["a_w_out"][0], 0, P),
                        (S_G0, S_K, a["ple_w_gate"][0], 0, P), (S_K, S_V, a["w_k"], 0, P),
                        (S_V, S_Q, a["w_v"], 0, P), (S_Q, S_Z, a["b_w_in"][0], 0, P),
                        (S_Z, S_BO, a["b_w_in"][0], D, P), (S_BO, S_P1, a["b_w_out"][0], 0, P),
                        (S_P1, S_G1, a["ple_w_proj"][1], 0, T), (S_G1, S_END, a["ple_w_gate"][1], 0, P)):
                    if base <= S < end:
                        return w(t, c0 + (S - base) * n, n)

            def slabs(upto):
                while sent[0] <= min(upto, S_END - 1):
                    S = sent[0]
                    after(sp, s.w_split, S - RAW + 1)
                    src = slab_source(S)
                    dst = raw[S % RAW][:].rearrange("p (k c) -> p k c", c=src.shape[2])
                    sp.dma_start(dst, src).then_inc(raw_in[S % RAW], 16)
                    sent[0] += 1

            sp.dma_start(cst[:], a["consts"]).then_inc(s.cst_in, 16)
            xv = a["x"][0].rearrange("(n s) d -> s n d", s=CH)
            for j in range(QB):
                for i in range(2):
                    sp.dma_start(xrow[i * NC:(i + 1) * NC, j * D:(j + 1) * D], xv[2 * j + i]).then_inc(x_in[j], 16)
            slabs(1)
            for k in range(KT):
                sp.wait_ge(s.x_copied, k + 1)
                sp.dma_start(xd[k], uT[:, k % 4, :]).then_inc(xs_out[k % 4], 16)
            slabs(5)
            sp.wait_ge(s.rows_ev, 1)
            sp.dma_start(bd[:, :, 0:T], view(p1, 0, [[0, P], [1, T]], np_=H)).then_inc(s.rows_out, 16)
            sp.dma_start(bd[:, :, T:REV], view(p2, 0, [[0, P], [1, REV - T]], np_=H)).then_inc(s.rows_out, 16)

            def turn_u(m):
                slabs(SLAB_OF["u", m] + 5)
                sp.wait_ge(s.u_ev, m + 1)
                sp.dma_start(ud[m], uT[:, m % 4, :]).then_inc(s.u_out, 16)
                sp.wait_ge(s.u_out, 16 * (m + 1))
                after(sp, s.ssm_y, m - 1)
                v = ud[m].rearrange("(g c) (s n) -> s c g n", c=GC, s=CH)
                for i in range(CH):
                    sp.dma_start(U[i * GC:(i + 1) * GC, m % 2, :, :], v[i]).then_inc(u_in[m % 2], 16)

            def swap_m(m):
                sp.wait_ge(s.m_built, m + 1)
                after(sp, s.ssm_y, m - 1)
                for i in range(2):
                    sp.dma_start(Msw[ST * i:ST * (i + 1), m % 2],
                                 M[ST * (1 - i):ST * (2 - i)].rearrange("p g t c -> p g (t c)")
                                 ).then_inc(msw_in[m % 2], 16)

            def turn_y(m):
                sp.wait_ge(s.y_ev, m + 1)
                sp.dma_start(yd[m], ysb[:, m % 2, :]).then_inc(s.y_out, 16)
                sp.wait_ge(s.y_out, 16 * (m + 1))
                after(sp, s.gelu, m - 1)
                v = yd[m].rearrange("(t c) (g n) -> g c t n", c=GC, g=GT)
                for i in range(GT):
                    sp.dma_start(yT[i * GC:(i + 1) * GC, m % 2, :].rearrange("p (t n) -> p t n", t=CH),
                                 v[i]).then_inc(y_in[m % 2], 16)

            def spill_z(m):
                sp.wait_ge(s.zz, m + 1)
                sp.dma_start(zd[m], st[:, m % 2, :]).then_inc(z_out[m % 2], 16)

            turn_u(0)
            turn_u(1)
            swap_m(0)
            for m in range(KT):
                if m + 1 < KT:
                    slabs(SLAB_OF["z", m + 1] + 2)
                turn_y(m)
                if m + 2 < KT:
                    turn_u(m + 2)
                if m + 1 < KT:
                    swap_m(m + 1)
                spill_z(m)
            slabs(S_GLU + 4)
            sp.wait_ge(s.y_lo, KT)
            for i in range(2):
                sp.wait_ge(z_out[i], 16 * KT // 2)
            sp.dma_start(zz[:], zd.rearrange("k p t -> p k t")).then_inc(s.zz_in, 16)
            sp.dma_start(xT[:], xd.rearrange("k p t -> p k t")).then_inc(s.xT_in, 16)
            pv = a["p"][0, 0].rearrange("(n s) d -> s n d", s=CH)
            for j in range(QB):
                for i in range(2):
                    sp.dma_start(prow[i * NC:(i + 1) * NC, j, :], pv[2 * j + i]).then_inc(s.p_in, 16)
            for m in range(KT):
                slabs(S_G0 + m + 5)
                sp.wait_ge(s.x1, m + 1)
                sp.dma_start(x1d[m], tb[2][:, m % 2, :]).then_inc(x1_out[m % 2], 16)
            slabs(S_BO)
            sp.wait_ge(s.rows_out, 32)
            for m in range(H):
                after(sp, s.soft, QB * (m - 1))
                if m == 0:
                    sp.wait_ge(s.sz, H)
                src = bass.AP(bd.tensor, m * P * REV + P - 1, [[REV - 1, P], [1, T]])
                sp.dma_start(bias[:, m % 2, :], src).then_inc(bias_in[m % 2], 16)
            slabs(S_BO + 3)
            sp.wait_ge(s.pv, H * QB)
            for i in range(2):
                sp.wait_ge(x1_out[i], 16 * KT // 2)
            sp.dma_start(x1b[:], x1d.rearrange("k p t -> p k t")).then_inc(s.x1_in, 16)
            sp.wait_ge(s.o_lo, H)
            sp.dma_start(prow2[:], a["p"][1, 0].rearrange("(j p) d -> p j d", p=P)).then_inc(s.p2_in, 16)
            ov = out[0].rearrange("(j p) d -> p j d", p=P)
            for m in range(KT):
                slabs(S_G1 + m)
            for m in range(KT):
                sp.wait_ge(s.out_ev, m + 1)
                sp.dma_start(ov[:, :, m * P:(m + 1) * P],
                             tc[3][:, m % 2, :].rearrange("p (j c) -> p j c", c=P)).then_inc(o_out[m % 2], 16)
            for i in range(2):
                sp.wait_ge(o_out[i], 16 * KT // 2)

        @block.gpsimd
        def _(pool):
            nc.gpsimd.memset(Pp[:], 0.0).then_inc(s.zeroed, 1)
            nc.gpsimd.memset(TT[:], 0.0).then_inc(s.zeroed, 1)
            nc.gpsimd.memset(r8x[:], 0.0).then_inc(s.zeroed, 1)
            nc.gpsimd.memset(epsc, EPS).then_inc(s.zeroed, 1)
            for S in range(S_END):
                pool.wait_ge(raw_in[S % RAW], 16 * (S // RAW + 1))
                after(pool, s.w_used, S - RING + 1)
                nc.gpsimd.tensor_scalar(whi[S % RING][:], raw[S % RAW][:], 1.0, 0.0, ALU.mult,
                                        ALU.add).then_inc(s.w_hi, 1)
                pool.wait_ge(s.w_hi, S + 1)
                nc.gpsimd.tensor_tensor(wlo[S % RING][:], raw[S % RAW][:], whi[S % RING][:].bitcast(F32),
                                        ALU.subtract).then_inc(s.w_split, 1)

        @block.tensor
        def _(pe):
            mm = nc.tensor.matmul

            def exact(dst, wh, wl, xh, xl, first, last):
                mm(dst, wh, xh, start=first, stop=False)
                mm(dst, wh, xl, start=False, stop=False)
                return mm(dst, wl, xh, start=False, stop=last)

            def dense(S, xh, xl, b, ready, before=0):
                pe.wait_ge(s.w_split, S + 1)
                for k in range(KT):
                    for r in ready:
                        pe.wait_ge(r, before + k + 1)
                    c = slice(k * P, (k + 1) * P)
                    last = exact(ps(b), whi[S % RING][:, c], wlo[S % RING][:, c], xh[:, k, :], xl[:, k, :],
                                 k == 0, k == KT - 1)
                last.then_inc(s.w_used, 1)

            def turn(b, src, np_=P, n=P, o=0):
                return nc.tensor.transpose(bk[b][0:n, o:o + np_], src, ident[0:np_, 0:np_])

            def sum_squares(b, sq, k, done, before=0):
                pe.wait_ge(done, before + k + 1)
                mm(ps(b), cst[:, C_ONE:C_ONE + P], sq, start=k == 0, stop=k == KT - 1).then_inc(s.summed, 1)

            pe.wait_ge(s.cst_in, 16)
            pe.wait_ge(s.par_in, 16 * N_PAR)
            turn(4, view(yT, 0, [[1, P]], np_=G), np_=G)
            turn(4, view(yT, P, [[1, P]], np_=G), np_=G, o=ST)
            turn(4, view(yT, 2 * P, [[1, P]], np_=V_ROWS), np_=V_ROWS, o=P).then_inc(s.par_T, 1)
            for k in range(KT):
                last = turn(5 + k // 4, view(Msw, k * P, [[1, P]]), o=(k % 4) * P)
            last.then_inc(s.c_T, 1)
            for k in range(KT + 2):
                if k < KT:
                    after(pe, s.x_copied, k - 3)
                    for j in range(QB):
                        if k == 0:
                            pe.wait_ge(x_in[j], 32)
                        last = turn(k % 4, xrow[:, j * D + k * P:j * D + (k + 1) * P], o=j * P)
                    last.then_inc(s.x_T, 1)
                if k >= 2:
                    sum_squares(7, (w1, w2)[k % 2][:], k - 2, s.x_sq)

            after(pe, s.x_copied, KT)
            dense(SLAB_OF["u", 0], hi0, lo0, 0, (s.x_hi, s.x_lo))
            pe.wait_ge(s.xc1, 2)
            for h in range(2):
                last = mm(ps(5 + h), cst[:, C_J2:C_J2 + P], view(XC1, h * T, [[1, T]]), start=True, stop=True)
            last.then_inc(s.xc2_mm, 1)
            pe.wait_ge(s.b_in, 32)
            for h in range(2):
                last = mm(ps(2 + h), cst[:, C_J1:C_J1 + P], view(XB1, h * T, [[1, T]]), start=True, stop=True)
            last.then_inc(s.xb2_mm, 1)
            dense(SLAB_OF["u", 1], hi0, lo0, 1, ())
            pe.wait_ge(s.par_read, 1)
            pe.wait_ge(s.hot, 2)
            mm(bk[4][0:H, 0:T], small[0:BUCKETS + 1, 8:16], cst[0:BUCKETS + 1, C_HOT:C_HOT + T],
               start=True, stop=True)
            pe.wait_ge(s.r1, 1)
            mm(bk[7][0:H, 0:REV - T], small[0:BUCKETS + 1, 8:16], cst[0:BUCKETS + 1, C_HOT + T:C_HOT + REV],
               start=True, stop=True).then_inc(s.rows_mm, 1)
            pe.wait_ge(s.xb1, 2)
            pe.wait_ge(s.xc2, 2)
            for h in range(2):
                last = mm(ps(5 + h), cst[:, C_J1:C_J1 + P], view(XB1, h * T, [[1, T]]), start=True, stop=True)
            last.then_inc(s.xb2_mm, 1)

            def ssm_weights(m):
                pe.wait_ge(s.p_built, m + 1)
                after(pe, s.win, 4 * m)
                if m == 0:
                    pe.wait_ge(s.xb2, 4)
                for g in range(GT):
                    last = turn(2 + g // 4, view(Pp, g * PADJ * GC, [[1, P]]), o=(g % 4) * P)
                last.then_inc(s.p_T, 1)
                after(pe, s.t_built, T_COPIES * m)
                if m == 0:
                    pe.wait_ge(s.rows_ev, 1)
                for g in range(GT):
                    for i in range(2):
                        last = mm(ps(4, GC, (2 * g + i) * GC),
                                  view(Pp, g * PADJ * GC + (1 - i) * GC, [[1, P]]),
                                  XC1[:, m * GT + g, :], start=True, stop=True)
                last.then_inc(s.t_mm, 1)

            def ssm_in(m):
                pe.wait_ge(s.win, 4 * (m + 1))
                pe.wait_ge(u_in[m % 2], 16 * CH * (m // 2 + 1))
                after(pe, s.rot, m)
                if m == 0:
                    pe.wait_ge(s.xb2, 4)
                for g in range(GT):
                    mm(ps(5, NC, g * NC), Win[:, g, :], U[:, m % 2, g, :], start=True, stop=True)
                    last = mm(ps(6, NC, g * NC), Wsw[:, g, :], U[:, m % 2, g, :], start=True, stop=True)
                last.then_inc(s.ssm_w, 1)

            def ssm_out(m):
                pe.wait_ge(s.p_rot, m + 1)
                pe.wait_ge(s.t_built, T_COPIES * (m + 1))
                pe.wait_ge(s.m_built, m + 1)
                pe.wait_ge(msw_in[m % 2], 32 * (m // 2 + 1))
                after(pe, s.y_ev, m)
                for g in range(GT):
                    o = ps(7, NC, g * NC)
                    mm(o, view(TT, g * P, [[1, P]]), U[:, m % 2, g, :], start=True, stop=False)
                    mm(o, view(M, g * P, [[1, P]]), p1[:, g * NC:(g + 1) * NC], start=False, stop=False)
                    last = mm(o, Msw[:, m % 2, g, :], p2[:, g * NC:(g + 1) * NC], start=False, stop=True)
                last.then_inc(s.ssm_y, 1)

            ssm_weights(0)
            for m in range(KT):
                ssm_in(m)
                S = SLAB_OF["z", m]
                after(pe, s.u_ev, len([x for x in IN_ORDER[:S] if x[0] == "u"]))
                after(pe, s.z_ev, m)
                dense(S, hi0, lo0, S % 2, ())
                ssm_out(m)
                if m + 2 < KT:
                    S = SLAB_OF["u", m + 2]
                    pe.wait_ge(s.u_ev, m + 2)
                    after(pe, s.z_ev, m)
                    dense(S, hi0, lo0, S % 2, ())
                if m + 1 < KT:
                    ssm_weights(m + 1)

            def turn_p(rows, src, arrived, b):
                pe.wait_ge(arrived, rows)
                for k in range(PK):
                    for j in range(QB):
                        last = turn(b + k, src[:, j, k * P:(k + 1) * P], o=j * P)
                last.then_inc(s.pT, 1)

            for m in range(KT):
                if m < 2:
                    pe.wait_ge(s.z_ev, KT)
                else:
                    pe.wait_ge(s.glu_tanh, m - 1)
                    pe.wait_ge(s.glu_y, m - 1)
                dense(S_GLU + 2 * m, hi0, lo0, 2 * (m % 2), (s.y_hi, s.y_lo) if m == 0 else ())
                dense(S_GLU + 2 * m + 1, hi0, lo0, 2 * (m % 2) + 1, ())
                if m == 3:
                    turn_p(16 * 8, prow, s.p_in, 4)

            def project(S, ph, pl, b, n):
                pe.wait_ge(s.w_split, S + 1)
                pe.wait_ge(s.p_hi, n)
                pe.wait_ge(s.p_lo, n)
                for o in range(4):
                    for k in range(PK):
                        c = slice(k * T + o * P, k * T + (o + 1) * P)
                        last = exact(ps(b + o), whi[S % RING][:, c], wlo[S % RING][:, c], ph[:, k, :],
                                     pl[:, k, :], k == 0, k == PK - 1)
                last.then_inc(s.w_used, 1)

            project(S_P0, phi, plo, 4, PK)
            pe.wait_ge(s.glu_tanh, KT)
            pe.wait_ge(s.glu_y, KT)
            project(S_P0 + 1, phi, plo, 0, PK)

            for m in range(KT):
                if m < 2:
                    pe.wait_ge(s.pr_ev, 4)
                else:
                    pe.wait_ge(s.xa, m - 1)
                dense(S_OUT + m, hi1, lo1, 4 + m % 2, (s.glu_hi, s.glu_lo) if m == 0 else ())
                if m >= 2:
                    sum_squares(6, tb[3][:, m % 2, :], m - 2, s.xa_sq)
            for m in range(KT):
                pe.wait_ge(*((s.xa, KT - 1 + m) if m < 2 else (s.g_ev, m - 1)))
                dense(S_G0 + m, hi0, lo0, 4 + m % 2, (s.xa_hi, s.xa_lo) if m == 0 else ())
                if m == 0:
                    sum_squares(6, tb[3][:, 0, :], 6, s.xa_sq)
                    sum_squares(6, tb[3][:, 1, :], 7, s.xa_sq)
                if m >= 2:
                    sum_squares(7, tb[3][:, m % 2, :], m - 2, s.x1_sq)

            def qk(base, xh, xl, ready, o):
                for m in range(KT + 1):
                    if m < KT:
                        if m < 2:
                            if base == S_K:
                                pe.wait_ge(s.g_ev, KT)
                            else:
                                pe.wait_ge(s.v_ev, KT)
                        else:
                            pe.wait_ge(s.k_ev, o + m - 1)
                        dense(base + m, xh, xl, 4 + m % 2, ready if m == 0 else ())
                        if base == S_K and m == 0:
                            sum_squares(7, tb[3][:, 0, :], 6, s.x1_sq)
                            sum_squares(7, tb[3][:, 1, :], 7, s.x1_sq)
                    if m >= 1:
                        pe.wait_ge(s.k_sq, o + m)
                        if m >= 3:
                            pe.wait_ge(s.k_r, o + m - 2)
                        elif base == S_K:
                            pe.wait_ge(s.r_norm, 3)
                        else:
                            pe.wait_ge(s.v_lo, KT)
                        mm(ps(6 + (m - 1) % 2), cst[:, C_BLK:C_BLK + P], ta[1][:, (m - 1) % 2, :],
                           start=True, stop=True).then_inc(s.k_bs, 1)

            qk(S_K, hi1, lo1, (s.n1_hi, s.n1_lo), 0)
            for m in range(KT + 1):
                if m < KT:
                    pe.wait_ge(*((s.k_ev, KT) if m < 2 else (s.v_ev, m - 1)))
                    dense(S_V + m, hi1, lo1, 4 + m % 2, ())
                if m >= 1:
                    pe.wait_ge(s.v_ev, m)
                    if m >= 3:
                        pe.wait_ge(s.v_lo, m - 2)
                    else:
                        pe.wait_ge(s.k_r, KT)
                    for j in range(QB):
                        last = turn(6 + (m - 1) % 2, ta[0][:, (m - 1) % 2, j * P:(j + 1) * P], o=j * P)
                    last.then_inc(s.v_T, 1)
            qk(S_Q, hi2, lo2, (s.n2_hi, s.n2_lo), KT)
            for m in range(KT):
                pe.wait_ge(*((s.k_ev, 2 * KT) if m < 2 else (s.b_z, m - 1)))
                dense(S_Z + m, hi2, lo2, 4 + m % 2, ())

            def scores(j):
                m, I = divmod(j, QB)
                if j == 0:
                    pe.wait_ge(s.k_lo, 2 * KT)
                for c in range(2):
                    n = 2 * j + c
                    after(pe, s.sc_read, n - 2)
                    r = slice(c * HD, (c + 1) * HD)
                    q = slice(I * P, (I + 1) * P)
                    w = (I + 1) * P
                    exact(ps(n % 3, w), hi1[r, m, q], lo1[r, m, q], hi0[r, m, 0:w], lo0[r, m, 0:w],
                          True, True).then_inc(s.sc, 1)

            def apply(j):
                m, I = divmod(j, QB)
                pe.wait_ge(s.soft, j + 1)
                if j >= 2:
                    pe.wait_ge(s.at_lo, j - 1)
                else:
                    pe.wait_ge(s.b_z, KT)
                for t in range(I + 1):
                    last = turn(4 + j % 2, ab[:, j % 2, t * P:(t + 1) * P], o=t * P)
                last.then_inc(s.at, 1)

            def values(j):
                m, I = divmod(j, QB)
                pe.wait_ge(s.at_lo, j + 1)
                if I == 0:
                    after(pe, s.on, m - 1)
                    if m == 0:
                        pe.wait_ge(s.k_r, 2 * KT)
                for t in range(I + 1):
                    last = exact(ps(6 + m % 2, P, I * P), ath[:, j % 2, t * P:(t + 1) * P],
                                 atl[:, j % 2, t * P:(t + 1) * P], Vhi[:, m, t * P:(t + 1) * P],
                                 Vlo[:, m, t * P:(t + 1) * P], t == 0, t == I)
                last.then_inc(s.pv, 1)

            def turn_o(m):
                pe.wait_ge(s.on, m + 1)
                after(pe, s.o_ev, m)
                for I in range(QB):
                    last = turn(3, on[:, I * P:(I + 1) * P], o=I * P)
                last.then_inc(s.o_T, 1)

            steps = H * QB
            scores(0)
            for j in range(steps + 2):
                if j + 1 < steps:
                    scores(j + 1)
                if j < steps:
                    apply(j)
                if 1 <= j <= steps:
                    values(j - 1)
                if j >= 5 and (j - 5) % QB == 0:
                    turn_o((j - 5) // QB)

            for m in range(KT):
                pe.wait_ge(*((s.at_lo, steps) if m < 2 else (s.xa, KT + m - 1)))
                dense(S_BO + m, hi1, lo1, 4 + m % 2, (s.o_hi, s.o_lo) if m == 0 else ())
                if m >= 2:
                    sum_squares(6, tc[3][:, m % 2, :], m - 2, s.xa_sq, KT)
                if m == 4:
                    turn_p(16, prow2, s.p2_in, 0)
            project(S_P1, phi2, plo2, 0, 2 * PK)
            sum_squares(6, tc[3][:, 0, :], 6, s.xa_sq, KT)
            sum_squares(6, tc[3][:, 1, :], 7, s.xa_sq, KT)
            pe.wait_ge(s.pr2_ev, 4)
            project(S_P1 + 1, phi2, plo2, 0, 2 * PK)
            for m in range(KT + 1):
                if m < KT:
                    pe.wait_ge(*((s.xa, 2 * KT - 1 + m) if m < 2 else (s.g_ev, KT + m - 1)))
                    dense(S_G1 + m, hi2, lo2, 4 + m % 2, (s.xa_hi, s.xa_lo) if m == 0 else (), KT)
                if m >= 1:
                    pe.wait_ge(s.x2, m)
                    if m >= 3:
                        pe.wait_ge(s.out_ev, m - 2)
                    else:
                        pe.wait_ge(s.pr2_ev, KT)
                    for j in range(QB):
                        last = turn((m - 1) % 2, tc[2][:, (m - 1) % 2, j * P:(j + 1) * P], o=j * P)
                    last.then_inc(s.out_T, 1)

        @block.scalar
        def _(act):
            fn = nc.scalar.activation
            def dma(dst, src, which=s.par_in):
                act.dma_start(dst, src).then_inc(which, 16)
            for i in range(2):
                for n, t in ((0, a["a_lam_re"][0]), (P, a["a_lam_im"][0])):
                    dma(view(yT, n + i * ST, [[1, ST]], np_=G), t)
                dma(view(yT, 2 * P + i * HD, [[1, HD]], p0=V_QG, np_=1), a["b_q_norm_g"])
                dma(view(yT, 2 * P + i * HD, [[1, HD]], p0=V_KG, np_=1), a["k_norm_g"].rearrange("(a n) -> a n", a=1))
            for r, t in ((V_AG, a["a_norm_g"][0]), (V_D, a["a_d"][0]), (V_KVG, a["kv_norm_g"]),
                         (V_BG, a["b_norm_g"][0])):
                dma(view(yT, 2 * P, [[1, P]], p0=r, np_=KT), t.rearrange("(k p) -> k p", p=P))
            dma(view(yT, 2 * P, [[1, P]], p0=V_SUB, np_=1), a["b_subln_g"])
            dma(view(yT, 384, [[1, G]]), bass.AP(a["a_log_dt"].tensor, 0, [[0, P], [1, G]]))
            for i, n in enumerate(("b_lam_q1", "b_lam_k1", "b_lam_q2", "b_lam_k2")):
                dma(view(yT, 448 + i * 64, [[1, HD]]), bass.AP(a[n].tensor, 0, [[0, P], [1, HD]]))
            for i, t in enumerate((a["a_c_re"][0], a["a_c_im"][0])):
                dma(view(Msw, i * ST, [[P, KT], [1, ST]]), t.rearrange("(k g) c p -> (g c) k p", k=KT))
            for i, t in enumerate((a["a_b_re"][0], a["a_b_im"][0])):
                dma(XB1[i * ST:(i + 1) * ST], t.rearrange("g p c -> p g c"), s.b_in)
            dma(small[0:BUCKETS, 8:16], a["rel_bias"], s.hot_in)

            act.wait_ge(s.par_in, 16 * N_PAR)
            fn(pt(DT_), view(yT, 384, [[1, G]]), ACT.Exp).then_inc(s.dt, 1)
            act.wait_ge(s.xr, 1)
            fn(pt(MG_), pt(XR_), ACT.Exp).then_inc(s.mag, 1)
            act.wait_ge(s.lam_dot, 2)
            fn(small[:, 4:6], small[:, 2:4], ACT.Exp).then_inc(s.lam_e, 1)
            act.wait_ge(s.rr, 1)
            fn(pt(SN_), pt(RR_), ACT.Sin).then_inc(s.sin, 1)
            fn(pt(SH_), pt(RR_), ACT.Sin, scale=0.5).then_inc(s.sin, 1)

            act.wait_ge(s.vt, 1)
            for k in range(KT + 1):
                if k < KT:
                    act.wait_ge(s.x_T, k + 1)
                    fn(cols(hi0, k), ps(k % 4), ACT.Identity, scale=vcol(V_AG + k)).then_inc(s.x_hi, 1)
                if k >= 1:
                    act.wait_ge(s.x_copied, k)
                    after(act, s.summed, k - 2)
                    fn((w1, w2)[(k - 1) % 2][:], uT[:, (k - 1) % 4, :], ACT.Square).then_inc(s.x_sq, 1)

            def inverse_rms(n, b, version):
                act.wait_ge(s.summed, n)
                fn(R[:], ps(b), ACT.Ln, scale=1.0 / D, bias=epsc).then_inc(s.r_ln, 1)
                act.wait_ge(s.r_ln, version)
                fn(R[:], R[:], ACT.Exp, scale=-0.5).then_inc(s.r_norm, 1)

            act.wait_ge(s.zeroed, 4)
            inverse_rms(KT, 7, 1)
            act.wait_ge(s.r_norm, 1)
            fn(small[:, 6:7], epsc, ACT.Copy).then_inc(s.r1, 1)
            act.wait_ge(s.rows_mm, 1)
            fn(p1[0:H, :], bk[4][0:H, 0:T], ACT.Copy).then_inc(s.row0, 1)
            fn(p2[0:H, 0:REV - T], bk[7][0:H, 0:REV - T], ACT.Copy).then_inc(s.rows_ev, 1)
            
            def scan_ratio(m):
                if m == 0:
                    act.wait_ge(s.r8, 1)
                fn(view(r8x, 1, [[NC, GT], [1, NC - 1]]), view(r8, m * GT, [[1, GT], [0, NC - 1]]),
                   ACT.Copy).then_inc(s.ratio, 1)

            def input_weights(m):
                act.wait_ge(s.p_T, m + 1)
                after(act, s.ssm_w, m)
                for h in range(2):
                    fn(Win[:, 4 * h:4 * h + 4, :], ps(2 + h).rearrange("p (g s) -> p g s", g=4),
                       ACT.Copy).then_inc(s.win, 1)
                    fn(view(Wsw, 4 * h * P, [[P, 4], [ST, 2], [1, ST]]),
                       bass.AP(bk[2 + h], ST, [[T, P], [P, 4], [-ST, 2], [1, ST]]),
                       ACT.Copy).then_inc(s.win, 1)

            scan_ratio(0)
            input_weights(0)

            def gelu(m):
                act.wait_ge(s.comb, m + 1)
                fn(Y[:, m, :], yT[:, m % 2, :], ACT.Gelu_apprx_tanh).then_inc(s.gelu, 1)

            for m in range(KT):
                act.wait_ge(s.z_ev, m + 1)
                after(act, s.zz, m)
                fn(tz[:], st[:, m % 2, :], ACT.Tanh, scale=0.5).then_inc(s.z_tanh, 1)
                act.wait_ge(s.ssm_y, m + 1)
                if m >= 2:
                    act.wait_ge(s.y_out, 16 * (m - 1))
                fn(ysb[:, m % 2, :], ps(7), ACT.Copy).then_inc(s.y_ev, 1)
                if m >= 1:
                    gelu(m - 1)
                if m + 1 < KT:
                    act.wait_ge(s.scan, m + 1)
                    scan_ratio(m + 1)
                    input_weights(m + 1)
                if m == KT - 1:
                    act.wait_ge(s.w_used, S_GLU)
                    for k in range(KT - 1):
                        act.wait_ge(s.gelu, k + 1)
                        fn(cols(hi0, k), cols(Y, k), ACT.Copy).then_inc(s.y_hi, 1)
                    gelu(m)
                    act.wait_ge(s.gelu, KT)
                    fn(cols(hi0, m), cols(Y, m), ACT.Copy).then_inc(s.y_hi, 1)

            def split_p(ph, psb):
                for k in range(PK):
                    fn(ph[:, k, :], ps(psb + k), ACT.Copy).then_inc(s.p_hi, 1)

            for m in range(KT + 1):
                if m < KT:
                    act.wait_ge(s.w_used, S_GLU + 2 * m + 1)
                    after(act, s.glu_y, m - 1)
                    if m == 0:
                        act.wait_ge(s.y_lo, KT)
                    fn(tb[1][:, m % 2, :], ps(2 * (m % 2)), ACT.Tanh, scale=0.5).then_inc(s.glu_tanh, 1)
                if m >= 1:
                    act.wait_ge(s.glu_y3, m)
                    fn(cols(hi1, m - 1), tb[2][:, (m - 1) % 2, :], ACT.Copy).then_inc(s.glu_hi, 1)
                if m == 4:
                    act.wait_ge(s.pT, 1)
                    split_p(phi, 4)
            for i in range(2):
                act.wait_ge(s.w_used, S_P0 + i + 1)
                for o in range(4):
                    fn(cols(zz, 4 * i + o), ps(4 * (1 - i) + o), ACT.Copy).then_inc(s.pr_ev, 1)
            for m in range(KT):
                act.wait_ge(s.xa, m + 1)
                fn(cols(hi0, m), cols(xT, m), ACT.Copy).then_inc(s.xa_hi, 1)
                after(act, s.summed, KT + m - 1)
                fn(tb[3][:, m % 2, :], cols(xT, m), ACT.Square).then_inc(s.xa_sq, 1)
            inverse_rms(2 * KT, 6, 2)
            for m in range(KT):
                act.wait_ge(s.g_ev, m + 1)
                after(act, s.g_pr, m - 1)
                fn(tb[1][:, m % 2, :], tb[0][:, m % 2, :], ACT.Tanh, scale=0.5).then_inc(s.g_tanh, 1)
                act.wait_ge(s.x1, m + 1)
                fn(cols(hi1, m), tb[2][:, m % 2, :], ACT.Identity, scale=vcol(V_KVG + m)).then_inc(s.n1_hi, 1)
                fn(cols(hi2, m), tb[2][:, m % 2, :], ACT.Identity, scale=vcol(V_BG + m)).then_inc(s.n2_hi, 1)
                after(act, s.summed, 2 * KT + m - 1)
                fn(tb[3][:, m % 2, :], tb[2][:, m % 2, :], ACT.Square).then_inc(s.x1_sq, 1)
            inverse_rms(3 * KT, 7, 3)

            def qk(hi, o):
                for m in range(KT + 1):
                    if m < KT:
                        act.wait_ge(s.k_ev, o + m + 1)
                        if m >= 2:
                            act.wait_ge(s.k_n, o + m - 1)
                        fn(ta[1][:, m % 2, :], ta[0][:, m % 2, :], ACT.Square).then_inc(s.k_sq, 1)
                    if m >= 1:
                        n = m - 1
                        act.wait_ge(s.k_bs, o + n + 1)
                        t = ta[1][:, n % 2, :]
                        fn(t, ps(6 + n % 2), ACT.Ln, scale=1.0 / HD, bias=epsc).then_inc(s.k_ln, 1)
                        act.wait_ge(s.k_ln, o + n + 1)
                        fn(t, t, ACT.Exp, scale=-0.5).then_inc(s.k_r, 1)
                        act.wait_ge(s.k_n, o + n + 1)
                        fn(cols(hi, n), ta[2][:, n % 2, :], ACT.Copy).then_inc(s.k_hi, 1)

            qk(hi0, 0)
            for m in range(KT):
                act.wait_ge(s.v_T, m + 1)
                fn(cols(Vhi, m), ps(6 + m % 2), ACT.Copy).then_inc(s.v_hi, 1)
            qk(hi1, KT)
            for m in range(KT):
                act.wait_ge(s.b_z, m + 1)
                after(act, s.sz, m - 1)
                fn(ta[1][:, m % 2, :], ta[0][:, m % 2, :], ACT.Tanh, scale=0.5).then_inc(s.b_tanh, 1)

            steps = H * QB

            def exps(j):
                w = (j % QB + 1) * P
                act.wait_ge(s.neg, j + 1)
                for c in range(2):
                    e = sco[c][:, j % 2, 0:w]
                    fn(e, e, ACT.Exp, bias=stat[:, j % 2, 4 + c:5 + c],
                       accum_out=stat[:, j % 2, 6 + c:7 + c]).then_inc(s.exp, 1)

            def at_hi(j):
                w = (j % QB + 1) * P
                act.wait_ge(s.at, j + 1)
                after(act, s.pv, j - 1)
                fn(ath[:, j % 2, 0:w], ps(4 + j % 2, w), ACT.Copy).then_inc(s.at_hi, 1)

            def o_norm(m):
                act.wait_ge(s.pv, QB * (m + 1))
                after(act, s.o_T, m)
                for I in range(QB):
                    fn(on[:, I * P:(I + 1) * P], ps(6 + m % 2, P, I * P), ACT.Square,
                       accum_out=oss[:, I:I + 1]).then_inc(s.o_sq, 1)
                act.wait_ge(s.o_sq, QB * (m + 1))
                fn(oss[:, 4:8], oss[:, 0:4], ACT.Ln, scale=1.0 / P, bias=epsc).then_inc(s.o_ln, 1)
                act.wait_ge(s.o_ln, m + 1)
                fn(oss[:, 8:12], oss[:, 4:8], ACT.Exp, scale=-0.5).then_inc(s.o_r, 1)

            def o_hi(m):
                act.wait_ge(s.o_ev, m + 1)
                fn(cols(hi1, m), ta[2][:, m % 2, :], ACT.Copy).then_inc(s.o_hi, 1)

            for j in range(steps + 3):
                if j < steps:
                    exps(j)
                if 1 <= j <= steps:
                    at_hi(j - 1)
                if j >= 5 and (j - 5) % QB == 0 and (j - 5) // QB < H - 1:
                    o_norm((j - 5) // QB)
                if j >= 6 and (j - 6) % QB == 0 and (j - 6) // QB < H - 1:
                    o_hi((j - 6) // QB)
            o_norm(H - 1)
            o_hi(H - 1)

            for m in range(KT):
                act.wait_ge(s.xa, KT + m + 1)
                fn(cols(hi2, m), cols(x1b, m), ACT.Copy).then_inc(s.xa_hi, 1)
                after(act, s.summed, 3 * KT + m - 1)
                fn(tc[3][:, m % 2, :], cols(x1b, m), ACT.Square).then_inc(s.xa_sq, 1)
                if m == 4:
                    act.wait_ge(s.pT, 2)
                    split_p(phi2, 0)
            act.wait_ge(s.w_used, S_P1 + 1)
            for o in range(4):
                fn(cols(pr2, o), ps(o), ACT.Copy).then_inc(s.pr2_ev, 1)
            inverse_rms(4 * KT, 6, 4)
            act.wait_ge(s.w_used, S_P1 + 2)
            for o in range(4):
                fn(cols(pr2, 4 + o), ps(o), ACT.Copy).then_inc(s.pr2_ev, 1)
            for m in range(KT + 1):
                if m < KT:
                    act.wait_ge(s.g_ev, KT + m + 1)
                    after(act, s.g_pr, KT + m - 1)
                    fn(tc[1][:, m % 2, :], tc[0][:, m % 2, :], ACT.Tanh, scale=0.5).then_inc(s.g_tanh, 1)
                if m >= 1:
                    n = m - 1
                    act.wait_ge(s.out_T, n + 1)
                    if n >= 2:
                        act.wait_ge(o_out[n % 2], 16 * (n // 2))
                    fn(tc[3][:, n % 2, :], ps(n % 2), ACT.Copy).then_inc(s.out_ev, 1)

        @block.vector
        def _(dve):
            v = nc.vector
            tt, ts, stt, cp = v.tensor_tensor, v.tensor_scalar, v.scalar_tensor_tensor, v.tensor_copy
            MUL, ADD, SUB = ALU.mult, ALU.add, ALU.subtract
            steps_done = [0]

            def link(ins):
                steps_done[0] += 1
                ins.then_inc(s.dve_step, 1)
                dve.wait_ge(s.dve_step, steps_done[0])

            dve.wait_ge(s.par_T, 1)
            link(cp(pt(LR_), bk[4][:, 0:ST]))
            link(cp(pt(LI_), bk[4][:, ST:P]))
            cp(VT[:], bk[4][:, P:P + V_ROWS]).then_inc(s.par_read, 1)
            dve.wait_ge(s.par_read, 1)
            link(ts(vcol(V_QG), vcol(V_QG), HD ** -0.5, None, MUL))
            ts(vcol(V_SUB), vcol(V_SUB), 0.5 * (1 - LAM_INIT), None, MUL).then_inc(s.vt, 1)
            dve.wait_ge(s.dt, 1)
            tt(pt(XR_), pt(LR_), pt(DT_), MUL).then_inc(s.xr, 1)
            link(tt(pt(TH_), pt(LI_), pt(DT_), MUL))
            link(ts(pt(KQ_), pt(TH_), 1 / TWO_PI, MAGIC, MUL, ADD))
            link(ts(pt(KQ_), pt(KQ_), -MAGIC, None, ADD))
            link(stt(out=pt(RR_), in0=pt(KQ_), scalar=-PI_A, in1=pt(TH_), op0=MUL, op1=ADD))
            link(stt(out=pt(RR_), in0=pt(KQ_), scalar=-PI_B, in1=pt(RR_), op0=MUL, op1=ADD))
            link(stt(out=pt(RR_), in0=pt(KQ_), scalar=-PI_C, in1=pt(RR_), op0=MUL, op1=ADD))
            ts(pt(RR_), pt(RR_), 3.1415925, -3.1415925, ALU.min, ALU.max).then_inc(s.rr, 1)
            for i in range(2):
                v.tensor_tensor_reduce(view(tmp, i * 64, [[1, 64]]), lam_v[:, 2 * i, :], lam_v[:, 2 * i + 1, :],
                                       1.0, 0.0, MUL, ADD, small[:, 2 + i:3 + i]).then_inc(s.lam_dot, 1)
            dve.wait_ge(s.lam_e, 1)
            link(tt(small[:, 1:2], small[:, 5:6], small[:, 4:5], SUB))
            link(ts(small[:, 1:2], small[:, 1:2], -LAM_INIT, None, ADD))
            dve.wait_ge(s.hot_in, 16)
            v.memset(small[BUCKETS:BUCKETS + 1, 8:16], NEG).then_inc(s.hot, 2)

            for k in range(KT):
                dve.wait_ge(s.x_hi, k + 1)
                if k >= 4:
                    dve.wait_ge(xs_out[k % 4], 16)
                    dve.wait_ge(s.x_sq, k - 3)
                cp(uT[:, k % 4, :], ps(k % 4)).then_inc(s.x_copied, 1)
                dve.wait_ge(s.x_copied, k + 1)
                stt(out=cols(lo0, k), in0=uT[:, k % 4, :], scalar=vcol(V_AG + k), in1=cols(hi0, k).bitcast(F32),
                    op0=MUL, op1=SUB).then_inc(s.x_lo, 1)

            dve.wait_ge(s.c_T, 1)
            dve.wait_ge(s.cst_in, 16)
            sgn = cst[:, C_SGN:C_SGN + 1]
            for h in range(2):
                ts(view(XC1, h * T, [[1, T]]), ps(5 + h), sgn, None, MUL).then_inc(s.xc1, 1)
            dve.wait_ge(s.sin, 2)
            dve.wait_ge(s.mag, 1)
            link(tt(pt(CO_), pt(SH_), pt(SH_), MUL))
            link(ts(pt(CO_), pt(CO_), -2.0, 1.0, MUL, ADD))
            re, im = pw
            link(v.memset(re[:, 0, :], 1.0))
            link(v.memset(im[:, 0, :], 0.0))
            link(tt(re[:, 1, :], pt(MG_), pt(CO_), MUL))
            link(tt(im[:, 1, :], pt(MG_), pt(SN_), MUL))
            link(ts(pt(T1_), re[:, 1, :], -1.0, None, ADD))
            link(tt(pt(DN_), pt(LR_), pt(LR_), MUL))
            link(tt(pt(T2_), pt(LI_), pt(LI_), MUL))
            link(tt(pt(DN_), pt(DN_), pt(T2_), ADD))
            link(v.reciprocal(pt(DN_), pt(DN_)))
            link(tt(pt(FR_), pt(T1_), pt(LR_), MUL))
            link(tt(pt(T2_), im[:, 1, :], pt(LI_), MUL))
            link(tt(pt(FR_), pt(FR_), pt(T2_), ADD))
            link(tt(pt(FR_), pt(FR_), pt(DN_), MUL))
            link(tt(pt(FI_), im[:, 1, :], pt(LR_), MUL))
            link(tt(pt(T2_), pt(T1_), pt(LI_), MUL))
            link(tt(pt(FI_), pt(FI_), pt(T2_), SUB))
            link(tt(pt(FI_), pt(FI_), pt(DN_), MUL))

            def cmul(t, dst, n, i, j):
                r, q = t
                d0, x0 = slice(dst, dst + n), slice(i, i + n)
                bc = [view(z, j * G, [[0, n], [1, G]]) for z in t]
                A = view(tmp, 0, [[G, n], [1, G]])
                B = view(tmp, 4 * G, [[G, n], [1, G]])
                link(tt(A, r[:, x0, :], bc[0], MUL))
                link(tt(B, q[:, x0, :], bc[1], MUL))
                link(tt(r[:, d0, :], A, B, SUB))
                link(tt(A, r[:, x0, :], bc[1], MUL))
                link(tt(B, q[:, x0, :], bc[0], MUL))
                link(tt(q[:, d0, :], A, B, ADD))

            def powers(t):
                for dst, n, j in ((2, 1, 1), (3, 2, 2), (5, 4, 4)):
                    cmul(t, dst, n, 1, j)

            powers(pw)
            link(tt(pt(MG_), pt(MG_), pt(MG_), MUL))
            link(tt(pt(MG_), pt(MG_), pt(MG_), MUL))
            tt(r8[:], pt(MG_), pt(MG_), MUL).then_inc(s.r8, 1)
            dve.wait_ge(s.xb2_mm, 1)
            dve.wait_ge(s.b_in, 32)
            for h in range(2):
                gsl = slice(h * G // 2, (h + 1) * G // 2)
                x1 = XB1[:, gsl, :]
                x2 = XB2[:, gsl, :]
                fr = view(ysb, FR_ * 64 + h * G // 2, [[1, G // 2], [0, GC]])
                fi = view(ysb, FI_ * 64 + h * G // 2, [[1, G // 2], [0, GC]])
                link(tt(x2, ps(2 + h).rearrange("p (g c) -> p g c", c=GC), fi, MUL))
                link(tt(x1, x1, fr, MUL))
                tt(x1, x1, x2, ADD).then_inc(s.xb1, 1)
            dve.wait_ge(s.xc2_mm, 1)
            for h in range(2):
                cp(view(XC2, h * T, [[1, T]]), ps(5 + h)).then_inc(s.xc2, 1)

            for t in (gt, ft):
                link(v.memset(t[0][:, 0, :], 1.0))
                link(v.memset(t[1][:, 0, :], 0.0))
            link(cp(gt[0][:, 1, :], pt(CO_)))
            link(ts(gt[1][:, 1, :], pt(SN_), sgn, None, MUL))
            for _ in range(3):
                cmul(gt, 2, 1, 1, 1)
                link(cp(gt[0][:, 1, :], gt[0][:, 2, :]))
                link(cp(gt[1][:, 1, :], gt[1][:, 2, :]))
            powers(gt)
            link(cp(ft[0][:, 1, :], gt[0][:, CH, :]))
            link(cp(ft[1][:, 1, :], gt[1][:, CH, :]))
            powers(ft)
            dve.wait_ge(s.xb2_mm, 2)
            for h in range(2):
                cp(view(XB2, h * T, [[1, T]]), ps(5 + h)).then_inc(s.xb2, 2)
            dve.wait_ge(s.xb2, 4)

            dve.wait_ge(s.zeroed, 4)
            tmp4 = view(tmp, 0, [[P, GT], [GC, CH], [1, GC]])

            def powers_of(t, m, k0, step):
                return view(t, k0 * G + m * GT, [[1, GT], [step * G, CH], [0, GC]])

            def build_p(m):
                after(dve, s.t_mm, m)
                o = view(Pp, 0, [[PADJ * GC, GT], [GC, CH], [1, GC]])
                x1 = view(XB1, m * P, [[GC, GT], [0, CH], [1, GC]])
                x2 = view(XB2, m * P, [[GC, GT], [0, CH], [1, GC]])
                link(tt(tmp4, x2, powers_of(pw[1], m, CH - 1, -1), MUL))
                link(tt(o, x1, powers_of(pw[0], m, CH - 1, -1), MUL))
                tt(o, o, tmp4, ADD).then_inc(s.p_built, 1)

            def build_m(m):
                after(dve, s.ssm_y, m)
                x1 = view(XC1, m * P, [[GC, GT], [0, CH], [1, GC]])
                x2 = view(XC2, m * P, [[GC, GT], [0, CH], [1, GC]])
                dve.wait_ge(s.p_built, m + 1)
                link(tt(tmp4, x2, powers_of(pw[1], m, 1, 1), MUL))
                link(tt(M[:], x1, powers_of(pw[0], m, 1, 1), MUL))
                tt(M[:], M[:], tmp4, ADD).then_inc(s.m_built, 1)

            def phase_table(m):
                o = [[NC, GT], [8, 8], [1, 8]]
                fr, fi = [view(t, m * GT, [[1, GT], [G, 8], [0, 8]]) for t in ft]
                gr, gi = [view(t, m * GT, [[1, GT], [0, 8], [G, 8]]) for t in gt]
                C, S_, A, B = view(Ct, 0, o), view(St, 0, o), view(tmp, 0, o), view(tmp, T, o)
                if m > 0:
                    dve.wait_ge(s.p_rot, m)
                dve.wait_ge(s.p_built, m + 1)
                dve.wait_ge(s.m_built, max(m, 1))
                link(tt(A, fr, gr, MUL))
                link(tt(B, fi, gi, MUL))
                link(tt(C, A, B, SUB))
                link(tt(A, fr, gi, MUL))
                link(tt(B, fi, gr, MUL))
                link(tt(S_, A, B, ADD))

            def copy_t(m):
                dve.wait_ge(s.t_mm, m + 1)
                after(dve, s.ssm_y, m)
                for q, (src, n, dst) in enumerate(T_MOVES):
                    t0 = CH - 2 - 2 * ((src - dst) // 32)
                    cp(view(TT, t0 * GC, [[P, GT], [1, 2 * GC]], p0=dst, np_=n),
                       bass.AP(bk[4], src * T, [[T, n], [2 * GC, GT], [1, 2 * GC]])).then_inc(s.t_built, 1)

            def rotate(m):
                dve.wait_ge(s.ssm_w, m + 1)
                cut = [[NC, GT], [1, NC - 1]]
                A, B = view(w1, 1, cut), view(w2, 1, cut)
                C, S_ = view(Ct, 1, cut), view(St, 1, cut)
                link(tt(A, bass.AP(bk[5], 0, [[T, P]] + cut), C, MUL))
                tt(B, bass.AP(bk[6], 0, [[T, P]] + cut), S_, MUL).then_inc(s.rot, 1)
                dve.wait_ge(s.rot, m + 1)
                link(tt(A, A, B, ADD))
                dve.wait_ge(s.ratio, m + 1)
                v.tensor_tensor_scan(gs[:], r8x[:], w1[:], 0.0, MUL, ADD).then_inc(s.scan, 1)
                dve.wait_ge(s.scan, m + 1)
                after(dve, s.ssm_y, m)
                if m == 0:
                    dve.wait_ge(s.rows_out, 32)
                link(tt(p1[:], gs[:], Ct[:], MUL))
                tt(p2[:], gs[:], St[:], MUL).then_inc(s.p_rot, 1)

            def u_out(m):
                S = SLAB_OF["u", m]
                dve.wait_ge(s.w_used, S + 1)
                if m < 4:
                    dve.wait_ge(xs_out[m], 32)
                tt(uT[:, m % 4, :], ps(S % 2), R[:], MUL).then_inc(s.u_ev, 1)

            def combine(m):
                dve.wait_ge(y_in[m % 2], 16 * GT * (m // 2 + 1))
                stt(out=yT[:, m % 2, :], in0=uT[:, m % 4, :], scalar=vcol(V_D + m), in1=yT[:, m % 2, :],
                    op0=MUL, op1=ADD).then_inc(s.comb, 1)

            dve.wait_ge(s.x_sq, KT)
            dve.wait_ge(s.summed, KT)
            link(v.memset(w1[:], 0.0))
            dve.wait_ge(s.r_norm, 1)
            u_out(0)
            build_p(0)
            u_out(1)
            copy_t(0)
            build_m(0)
            phase_table(0)
            for m in range(KT):
                rotate(m)
                if m + 1 < KT:
                    build_p(m + 1)
                S = SLAB_OF["z", m]
                dve.wait_ge(s.w_used, S + 1)
                if m >= 2:
                    dve.wait_ge(z_out[m % 2], 16 * (m // 2))
                tt(st[:, m % 2, :], ps(S % 2), R[:], MUL).then_inc(s.z_ev, 1)
                if m >= 1:
                    combine(m - 1)
                dve.wait_ge(s.z_tanh, m + 1)
                stt(out=st[:, m % 2, :], in0=tz[:], scalar=1.0, in1=st[:, m % 2, :], op0=ADD,
                    op1=MUL).then_inc(s.zz, 1)
                if m + 2 < KT:
                    u_out(m + 2)
                if m + 1 < KT:
                    phase_table(m + 1)
                    copy_t(m + 1)
                    build_m(m + 1)
            for k in range(KT - 1):
                dve.wait_ge(s.y_hi, k + 1)
                tt(cols(lo0, k), cols(Y, k), cols(hi0, k).bitcast(F32), SUB).then_inc(s.y_lo, 1)
            combine(KT - 1)
            dve.wait_ge(s.y_hi, KT)
            tt(cols(lo0, KT - 1), cols(Y, KT - 1), cols(hi0, KT - 1).bitcast(F32), SUB).then_inc(s.y_lo, 1)

            for m in range(KT):
                dve.wait_ge(s.w_used, S_GLU + 2 * m + 2)
                dve.wait_ge(s.glu_tanh, m + 1)
                y = tb[0][:, m % 2, :]
                stt(out=y, in0=tb[1][:, m % 2, :], scalar=1.0, in1=ps(2 * (m % 2) + 1), op0=ADD,
                    op1=MUL).then_inc(s.glu_y, 1)
                dve.wait_ge(s.glu_y, m + 1)
                if m == 0:
                    dve.wait_ge(s.zz_in, 16)
                after(dve, s.glu_hi, m - 1)
                stt(out=tb[2][:, m % 2, :], in0=y, scalar=0.25, in1=cols(zz, m), op0=MUL,
                    op1=MUL).then_inc(s.glu_y3, 1)
                dve.wait_ge(s.glu_hi, m + 1)
                tt(cols(lo1, m), tb[2][:, m % 2, :], cols(hi1, m).bitcast(F32), SUB).then_inc(s.glu_lo, 1)
                if m == 4:
                    for k in range(PK):
                        dve.wait_ge(s.p_hi, k + 1)
                        tt(plo[:, k, :], ps(4 + k), phi[:, k, :].bitcast(F32), SUB).then_inc(s.p_lo, 1)
            dve.wait_ge(s.xT_in, 16)
            for m in range(KT):
                dve.wait_ge(s.w_used, S_OUT + m + 1)
                tt(cols(xT, m), cols(xT, m), ps(4 + m % 2), ADD).then_inc(s.xa, 1)
                dve.wait_ge(s.xa_hi, m + 1)
                tt(cols(lo0, m), cols(xT, m), cols(hi0, m).bitcast(F32), SUB).then_inc(s.xa_lo, 1)
            dve.wait_ge(s.r_norm, 2)
            dve.wait_ge(s.pr_ev, KT)
            for m in range(KT):
                dve.wait_ge(s.w_used, S_G0 + m + 1)
                tt(tb[0][:, m % 2, :], ps(4 + m % 2), R[:], MUL).then_inc(s.g_ev, 1)
                dve.wait_ge(s.g_tanh, m + 1)
                t = tb[1][:, m % 2, :]
                stt(out=t, in0=t, scalar=1.0, in1=cols(zz, m), op0=ADD, op1=MUL).then_inc(s.g_pr, 1)
                dve.wait_ge(s.g_pr, m + 1)
                if m >= 2:
                    dve.wait_ge(x1_out[m % 2], 16 * (m // 2))
                    dve.wait_ge(s.x1_sq, m - 1)
                stt(out=view(tb[2], (m % 2) * T, [[1, CH], [CH, NC]]),
                    in0=view(tb[1], (m % 2) * T, [[NC, CH], [1, NC]]), scalar=0.5,
                    in1=view(xT, m * T, [[NC, CH], [1, NC]]), op0=MUL, op1=ADD).then_inc(s.x1, 1)
                for hi, lo, g, hd, ld in ((hi1, lo1, V_KVG, s.n1_hi, s.n1_lo), (hi2, lo2, V_BG, s.n2_hi, s.n2_lo)):
                    dve.wait_ge(hd, m + 1)
                    stt(out=cols(lo, m), in0=tb[2][:, m % 2, :], scalar=vcol(g + m),
                        in1=cols(hi, m).bitcast(F32), op0=MUL, op1=SUB).then_inc(ld, 1)

            def qk(base, hi, lo, g, o):
                for m in range(KT + 1):
                    if m < KT:
                        dve.wait_ge(s.w_used, base + m + 1)
                        tt(ta[0][:, m % 2, :], ps(4 + m % 2), R[:], MUL).then_inc(s.k_ev, 1)
                    if m >= 1:
                        n = m - 1
                        dve.wait_ge(s.k_r, o + n + 1)
                        t = ta[2][:, n % 2, :]
                        stt(out=t, in0=ta[0][:, n % 2, :], scalar=vcol(g), in1=ta[1][:, n % 2, :], op0=MUL,
                            op1=MUL).then_inc(s.k_n, 1)
                        dve.wait_ge(s.k_hi, o + n + 1)
                        tt(cols(lo, n), t, cols(hi, n).bitcast(F32), SUB).then_inc(s.k_lo, 1)

            dve.wait_ge(s.r_norm, 3)
            for i in range(2):
                dve.wait_ge(x1_out[i], 16 * KT // 2)
            qk(S_K, hi0, lo0, V_KG, 0)
            for m in range(KT + 1):
                if m < KT:
                    dve.wait_ge(s.w_used, S_V + m + 1)
                    after(dve, s.v_T, m - 1)
                    tt(ta[0][:, m % 2, :], ps(4 + m % 2), R[:], MUL).then_inc(s.v_ev, 1)
                if m >= 1:
                    n = m - 1
                    dve.wait_ge(s.v_hi, n + 1)
                    tt(cols(Vlo, n), ps(6 + n % 2), cols(Vhi, n).bitcast(F32), SUB).then_inc(s.v_lo, 1)
            dve.wait_ge(s.v_T, KT)
            qk(S_Q, hi1, lo1, V_QG, KT)
            for m in range(KT):
                dve.wait_ge(s.w_used, S_Z + m + 1)
                tt(ta[0][:, m % 2, :], ps(4 + m % 2), R[:], MUL).then_inc(s.b_z, 1)
                dve.wait_ge(s.b_tanh, m + 1)
                stt(out=cols(sz, m), in0=ta[1][:, m % 2, :], scalar=1.0, in1=ta[0][:, m % 2, :], op0=ADD,
                    op1=MUL).then_inc(s.sz, 1)

            steps = H * QB

            def soft_in(j):
                m, I = divmod(j, QB)
                w = (I + 1) * P
                if I == 0:
                    dve.wait_ge(bias_in[m % 2], 16 * (m // 2 + 1))
                after(dve, s.soft, j - 1)
                for c in range(2):
                    n = 2 * j + c
                    dve.wait_ge(s.sc, n + 1)
                    v.tensor_tensor_reduce(sco[c][:, j % 2, 0:w], ps(n % 3, w), bias[:, m % 2, T - w:T], 1.0,
                                           -3e38, ADD, ALU.max,
                                           stat[:, j % 2, 2 + c:3 + c]).then_inc(s.sc_read, 1)
                dve.wait_ge(s.sc_read, 2 * j + 2)
                ts(stat[:, j % 2, 4:6], stat[:, j % 2, 2:4], -1.0, None, MUL).then_inc(s.neg, 1)

            def soft_out(j):
                w = (j % QB + 1) * P
                dve.wait_ge(s.exp, 2 * j + 2)
                r = stat[:, j % 2, 8:10]
                link(v.reciprocal(r, stat[:, j % 2, 6:8]))
                link(tt(stat[:, j % 2, 10:11], stat[:, j % 2, 9:10], negl, MUL))
                link(ts(sco[0][:, j % 2, 0:w], sco[0][:, j % 2, 0:w], stat[:, j % 2, 8:9], None, MUL))
                after(dve, s.at, j - 1)
                stt(out=ab[:, j % 2, 0:w], in0=sco[1][:, j % 2, 0:w], scalar=stat[:, j % 2, 10:11],
                    in1=sco[0][:, j % 2, 0:w], op0=MUL, op1=ADD).then_inc(s.soft, 1)

            def at_lo(j):
                w = (j % QB + 1) * P
                dve.wait_ge(s.at_hi, j + 1)
                tt(atl[:, j % 2, 0:w], ps(4 + j % 2, w), ath[:, j % 2, 0:w].bitcast(F32), SUB).then_inc(s.at_lo, 1)

            def o_scale(m):
                dve.wait_ge(s.o_r, m + 1)
                for I in range(QB):
                    last = ts(on[:, I * P:(I + 1) * P], ps(6 + m % 2, P, I * P), oss[:, 8 + I:9 + I], None, MUL)
                last.then_inc(s.on, 1)

            def o_out_(m):
                dve.wait_ge(s.o_T, m + 1)
                stt(out=ta[2][:, m % 2, :], in0=ps(3), scalar=vcol(V_SUB), in1=cols(sz, m), op0=MUL,
                    op1=MUL).then_inc(s.o_ev, 1)

            def o_lo_(m):
                dve.wait_ge(s.o_hi, m + 1)
                tt(cols(lo1, m), ta[2][:, m % 2, :], cols(hi1, m).bitcast(F32), SUB).then_inc(s.o_lo, 1)

            soft_in(0)
            for j in range(steps + 3):
                if j + 1 < steps:
                    soft_in(j + 1)
                if j < steps:
                    soft_out(j)
                if 1 <= j <= steps:
                    at_lo(j - 1)
                if j >= 5 and (j - 5) % QB == 0 and (j - 5) // QB < H - 1:
                    o_scale((j - 5) // QB)
                if j >= 6 and (j - 6) % QB == 0 and (j - 6) // QB < H - 1:
                    o_out_((j - 6) // QB)
                if j >= 7 and (j - 7) % QB == 0 and (j - 7) // QB < H - 1:
                    o_lo_((j - 7) // QB)
            o_scale(H - 1)
            o_out_(H - 1)
            o_lo_(H - 1)

            dve.wait_ge(s.x1_in, 16)
            for m in range(KT):
                dve.wait_ge(s.w_used, S_BO + m + 1)
                tt(cols(x1b, m), cols(x1b, m), ps(4 + m % 2), ADD).then_inc(s.xa, 1)
                dve.wait_ge(s.xa_hi, KT + m + 1)
                tt(cols(lo2, m), cols(x1b, m), cols(hi2, m).bitcast(F32), SUB).then_inc(s.xa_lo, 1)
                if m == 4:
                    for k in range(PK):
                        dve.wait_ge(s.p_hi, PK + k + 1)
                        tt(plo2[:, k, :], ps(k), phi2[:, k, :].bitcast(F32), SUB).then_inc(s.p_lo, 1)
            dve.wait_ge(s.r_norm, 4)
            for m in range(KT):
                dve.wait_ge(s.w_used, S_G1 + m + 1)
                tt(tc[0][:, m % 2, :], ps(4 + m % 2), R[:], MUL).then_inc(s.g_ev, 1)
                dve.wait_ge(s.g_tanh, KT + m + 1)
                dve.wait_ge(s.pr2_ev, KT)
                t = tc[1][:, m % 2, :]
                stt(out=t, in0=t, scalar=1.0, in1=cols(pr2, m), op0=ADD, op1=MUL).then_inc(s.g_pr, 1)
                dve.wait_ge(s.g_pr, KT + m + 1)
                after(dve, s.out_T, m - 1)
                stt(out=tc[2][:, m % 2, :], in0=t, scalar=0.5, in1=cols(x1b, m), op0=MUL,
                    op1=ADD).then_inc(s.x2, 1)


_INS = ["x", "p", "a_norm_g", "a_w_in", "a_lam_re", "a_lam_im", "a_log_dt", "a_b_re", "a_b_im", "a_c_re",
        "a_c_im", "a_d", "a_w_glu", "a_w_out", "kv_norm_g", "w_k", "w_v", "k_norm_g", "b_norm_g", "b_w_in",
        "b_q_norm_g", "b_lam_q1", "b_lam_k1", "b_lam_q2", "b_lam_k2", "b_subln_g", "b_w_out", "rel_bias",
        "ple_w_proj", "ple_w_gate"]


def constants():
    c = np.zeros((P, C_END), np.float32)
    c[:, C_ID:C_ID + P] = np.eye(P)
    i = np.arange(ST)
    c[i, C_J1 + ST + i] = 1.0
    c[ST + i, C_J1 + i] = -1.0
    c[i, C_J2 + ST + i] = -1.0
    c[ST + i, C_J2 + i] = 1.0
    c[:, C_ONE:C_ONE + P] = 1.0
    c[:HD, C_BLK:C_BLK + HD] = 1.0
    c[HD:, C_BLK + HD:C_BLK + P] = 1.0
    rel = T - 1 - np.arange(REV)
    n = np.maximum(rel, 1).astype(np.float32)
    exact = BUCKETS // 2
    large = exact + (np.log(n / np.float32(exact)) / np.float32(math.log(128 / exact))
                     * np.float32(BUCKETS - exact)).astype(np.int32)
    bucket = np.where(rel < exact, rel, np.minimum(large, BUCKETS - 1))
    bucket = np.where(rel < 0, BUCKETS, bucket)
    c[bucket, C_HOT + np.arange(REV)] = 1.0
    c[:ST, C_SGN] = 1.0
    c[ST:, C_SGN] = -1.0
    return c


def kernel(**inputs):
    import concourse.bacc as _bacc
    from concourse.bass_utils import run_bass_kernel_spmd as _run

    nc = _bacc.Bacc("TRN2", target_bir_lowering=False, num_devices=1)
    arrays, args = {}, {}
    for name in _INS + ["consts"]:
        v = constants() if name == "consts" else np.ascontiguousarray(inputs[name])
        arrays[f"in_{name}"] = v
        args[name] = nc.dram_tensor(f"in_{name}", v.shape, mybir.dt.from_np(v.dtype), kind="ExternalInput").ap()
    out = nc.dram_tensor("out_x", (1, T, D), F32, kind="ExternalOutput").ap()
    build(nc, args, out)
    r = _run(nc, [arrays], core_ids=[0])
    return r.results[0]["out_x"]
```

```python
import math
from contextlib import ExitStack

import numpy as np
import concourse.bass as bass
from concourse import mybir

F32 = mybir.dt.float32
F32R = mybir.dt.float32r
ACT = mybir.ActivationFunctionType
ALU = mybir.AluOpType
AX = mybir.AxisListType

P = 128
D = 1024
T = 512
KT = D // P
CH = 8
NC = T // CH
G = 64
GC = 16
ST = 64
GT = P // GC
PADJ = 2 * CH - 1
H = 8
HD = 64
QB = T // P
PLE = 256
PK = PLE // P
EPS = 1e-6
LAM_INIT = 0.8 - 0.6 * math.exp(-0.3 * 1)
NEG = -1e30
BUCKETS = 32
REV = 640

RAW, RING = 2, 4

C_ID, C_J1, C_J2, C_ONE, C_BLK, C_HOT = 0, P, 2 * P, 3 * P, 4 * P, 5 * P
C_SGN = C_HOT + REV
C_END = C_SGN + 1

V_AG, V_D, V_KVG, V_BG, V_QG, V_KG, V_SUB, V_ROWS = 0, 8, 16, 24, 32, 33, 34, 35

TWO_PI = 2 * math.pi
PI_A = 6.28125
PI_B = float(np.float32(np.round((TWO_PI - PI_A) * 2 ** 20) / 2 ** 20))
PI_C = float(np.float32(TWO_PI - PI_A - PI_B))
MAGIC = 12582912.0

S_IN, S_GLU, S_P0, S_OUT, S_G0, S_H, S_P1, S_BO, S_G1, S_END = (
    0, 16, 32, 34, 42, 50, 82, 84, 92, 100)


N_PAR = 8 + 4 + 1 + 1 + 4 + 2
T_MOVES = ((0, 128, 0), (32, 32, 0), (64, 32, 32), (96, 32, 64), (64, 64, 0), (96, 32, 0))
T_COPIES = len(T_MOVES)


def in_order():
    order = [("u", 0), ("u", 1)]
    for m in range(KT):
        order.append(("z", m))
        if m + 2 < KT:
            order.append(("u", m + 2))
    return order


IN_ORDER = in_order()
SLAB_OF = {x: i for i, x in enumerate(IN_ORDER)}


def head_order():
    order = [("k", 0), ("q", 0), ("v", 0)]
    for m in range(H):
        if m + 1 < H:
            order += [("k", m + 1), ("q", m + 1), ("v", m + 1)]
        order.append(("z", m))
    return order


HEAD_ORDER = head_order()
LEAD = 4


def build(nc, a, out):
    xd = nc.dram_tensor("xT_spill", (KT, P, T), F32, kind="Internal").ap()
    zd = nc.dram_tensor("gate_spill", (KT, P, T), F32, kind="Internal").ap()
    x1d = nc.dram_tensor("x1_spill", (KT, P, T), F32, kind="Internal").ap()
    ud = nc.dram_tensor("u_turn", (KT, P, T), F32, kind="Internal").ap()
    yd = nc.dram_tensor("y_turn", (KT, P, T), F32, kind="Internal").ap()
    bd = nc.dram_tensor("bias_rows", (H, P, REV), F32, kind="Internal").ap()

    def mk(name, shape, dt=F32):
        return nc.sbuf_tensor(name, shape, dt)

    with ExitStack() as keep:
        def sb(name, shape, dt=F32):
            return keep.enter_context(mk(name, shape, dt))

        def sem(name):
            return keep.enter_context(nc.semaphore(name))

        def sems(names):
            return [sem(name) for name in names.split()]

        raw = [sb(f"raw{i}", [P, D]) for i in range(RAW)]
        whi = [sb(f"whi{i}", [P, D], F32R) for i in range(RING)]
        wlo = [sb(f"wlo{i}", [P, D], F32R) for i in range(RING)]
        cst = sb("cst", [P, C_END])
        VT = sb("VT", [P, V_ROWS])
        R = sb("R", [P, T])
        small = sb("small", [P, 64])
        oss = small[:, 16:32]
        hi0 = sb("hi0", [P, KT, T], F32R)
        lo0 = sb("lo0", [P, KT, T], F32R)
        ident = cst[:, C_ID:C_ID + P]
        epsc, negl, lamc = small[:, 0:1], small[:, 1:2], small[:, 2:6]

        with ExitStack() as s5:
            def sa(name, shape, dt=F32):
                return s5.enter_context(mk(name, shape, dt))
            Y = sa("Y", [P, KT, T])
            Pp = sa("Pp", [P, GT, PADJ, GC])
            Win = sa("Win", [P, GT, P])
            Wsw = sa("Wsw", [P, GT, P])
            TT = sa("TT", [P, GT, CH, GC])
            M = sa("M", [P, GT, CH, GC])
            Msw = sa("Msw", [P, 2, GT, CH * GC])
            XB1 = sa("XB1", [P, G, GC])
            XB2 = sa("XB2", [P, G, GC])
            XC1 = sa("XC1", [P, G, GC])
            XC2 = sa("XC2", [P, G, GC])
            pw = [sa(f"pw{i}", [P, CH + 1, G]) for i in range(2)]
            gt = [sa(f"gt{i}", [P, CH + 1, G]) for i in range(2)]
            ft = [sa(f"ft{i}", [P, CH + 1, G]) for i in range(2)]
            r8 = sa("r8", [P, G])
            Ct = sa("Ct", [P, T])
            St = sa("St", [P, T])
            tmp = sa("tmp", [P, D])
            U = sa("U", [P, 2, GT, NC])
            w1 = sa("w1", [P, T])
            w2 = sa("w2", [P, T])
            gs = sa("gs", [P, T])
            p1 = sa("p1", [P, T])
            p2 = sa("p2", [P, T])
            ysb = sa("ysb", [P, 2, T])
            yT = sa("yT", [P, 2, T])
            uT = sa("uT", [P, 4, T])
            st = sa("st", [P, 2, T])
            r8x = sa("r8x", [P, T])
            tz = sa("tz", [P, T])
        xrow = Y[:, :, :].rearrange("p a b -> p (a b)")
        pt = ysb[:, :, :].rearrange("p a b -> p (a b)")
        yTf = yT[:, :, :].rearrange("p a b -> p (a b)")

        with ExitStack() as rest:
            def sc(name, shape, dt=F32, scope=rest):
                return scope.enter_context(mk(name, shape, dt))
            with ExitStack() as e:
                hi1 = sc("hi1", [P, KT, T], F32R, e)
            with ExitStack() as e:
                prow2 = sc("prow2", [P, QB, PLE], F32, e)
                phi2 = sc("phi2", [P, PK, T], F32R, e)
                plo2 = sc("plo2", [P, PK, T], F32R, e)
            sc("hi1_place", [P, KT, T], F32R)
            lo1 = sc("lo1", [P, KT, T], F32R)
            with ExitStack() as e:
                hi2 = sc("hi2", [P, KT, T], F32R, e)
                lo2 = sc("lo2", [P, KT, T], F32R, e)
            with ExitStack() as e:
                x1b = sc("x1b", [P, KT, T], F32, e)
                pr2 = sc("pr2", [P, KT, T], F32, e)
            sc("pair2_place", [P, 2, KT, T], F32R)
            with ExitStack() as e:
                zz = sc("zz", [P, KT, T], F32, e)
                xT = sc("xT", [P, KT, T], F32, e)
                prow = sc("prow", [P, QB, PLE], F32, e)
                phi = sc("phi", [P, PK, T], F32R, e)
                plo = sc("plo", [P, PK, T], F32R, e)
                tb = [sc(f"tb{i}", [P, 2, T], F32, e) for i in range(4)]
                acc = sc("acc", [P, T], F32, e)
            with ExitStack() as e:
                kh, kl, qh, ql, vh, vl = [sc(n, [P, 2, T], F32R, e) for n in ("kh", "kl", "qh", "ql", "vh", "vl")]
                ta = [sc(f"ta{i}", [P, 2, T], F32, e) for i in range(3)]
                sz = sc("sz", [P, 2, T], F32, e)
                bias = sc("bias", [P, 2, T], F32, e)
                sco = [sc(f"sco{c}", [P, 2, T], F32, e) for c in range(2)]
                ath = sc("ath", [P, 2, T], F32R, e)
                atl = sc("atl", [P, 2, T], F32R, e)
                on = sc("on", [P, T], F32, e)
                stat = sc("stat", [P, 2, 16], F32, e)
            with ExitStack() as e:
                tc = [sc(f"tc{i}", [P, 2, T], F32, e) for i in range(4)]
                acc2 = sc("acc2", [P, T], F32, e)
        bk = [keep.enter_context(nc.psum_tensor(f"bank{i}", [P, T], F32)) for i in range(8)]

        class s:
            cst_in, par_in, b_in, hot_in, par_T, par_read = sems("cst_in par_in b_in hot_in par_T par_read")
            vt, dt, xr, mag, lam_dot, lam_e = sems("vt dt xr mag lam_dot lam_e")
            rr, sin, hot, rows_mm, row0, rows_ev = sems("rr sin hot rows_mm row0 rows_ev")
            rows_out, zeroed, dve_step = sems("rows_out zeroed dve_step")
            c_T, xc1, xc2, xc2_mm, xb1, xb2 = sems("c_T xc1 xc2 xc2_mm xb1 xb2")
            xb2_mm, r8 = sems("xb2_mm r8")
            w_hi, w_split, w_used = sems("w_hi w_split w_used")
            x_T, x_copied, x_hi, x_lo, x_sq, summed = sems("x_T x_copied x_hi x_lo x_sq summed")
            r_ln, r_norm, r1 = sems("r_ln r_norm r1")
            u_ev, u_out, z_ev, z_tanh, zz = sems("u_ev u_out z_ev z_tanh zz")
            p_built, p_T, win, t_mm, t_built, m_built = sems("p_built p_T win t_mm t_built m_built")
            ratio, ssm_w, rot, scan, p_rot, ssm_y = sems("ratio ssm_w rot scan p_rot ssm_y")
            y_ev, y_out, comb, gelu, y_hi, y_lo = sems("y_ev y_out comb gelu y_hi y_lo")
            zz_in, xT_in, glu_tanh, glu_y, glu_y3, glu_hi = sems("zz_in xT_in glu_tanh glu_y glu_y3 glu_hi")
            glu_lo, p_in, p2_in, pT, p_hi, p_lo = sems("glu_lo p_in p2_in pT p_hi p_lo")
            pr_ev, pr2_mm, pr2_ev = sems("pr_ev pr2_mm pr2_ev")
            xa, xa_hi, xa_lo, xa_sq, g_ev, g_tanh = sems("xa xa_hi xa_lo xa_sq g_ev g_tanh")
            g_pr, x1, x1_sq, n1_hi, n1_lo, n2_hi = sems("g_pr x1 x1_sq n1_hi n1_lo n2_hi")
            n2_lo, x1_in, x2, out_T, out_ev = sems("n2_lo x1_in x2 out_T out_ev")
            h_ev, k_sq, k_bs, k_ln, k_r, k_n = sems("h_ev k_sq k_bs k_ln k_r k_n")
            k_hi, k_lo, v_T, v_hi, v_lo = sems("k_hi k_lo v_T v_hi v_lo")
            b_tanh, sz = sems("b_tanh sz")
            sc, sc_read, neg, exp, soft, at = sems("sc sc_read neg exp soft at")
            at_hi, at_lo, pv, o_sq, o_ln, o_r = sems("at_hi at_lo pv o_sq o_ln o_r")
            on, o_T, o_ev, o_hi, o_lo = sems("on o_T o_ev o_hi o_lo")
        s.acc = sem("acc_ready")
        raw_in = [sem(f"raw_in{i}") for i in range(RAW)]
        x_in = [sem(f"x_in{i}") for i in range(QB)]
        xs_out = [sem(f"xs_out{i}") for i in range(4)]
        u_in = [sem(f"u_in{i}") for i in range(2)]
        y_in = [sem(f"y_in{i}") for i in range(2)]
        msw_in = [sem(f"msw_in{i}") for i in range(2)]
        z_out = [sem(f"z_out{i}") for i in range(2)]
        x1_out = [sem(f"x1_out{i}") for i in range(2)]
        bias_in = [sem(f"bias_in{i}") for i in range(2)]
        o_out = [sem(f"o_out{i}") for i in range(2)]

        def after(eng, which, n):
            if n > 0:
                eng.wait_ge(which, n)

        def view(t, off, dims, p0=0, np_=P):
            pitch = int(np.prod(t.shape[1:]))
            return bass.AP(t, p0 * pitch + off, [[pitch, np_]] + [list(d) for d in dims])

        def cols(t, m):
            return t[:, m, :]

        def ps(b, n=T, o=0):
            return bk[b][:, o:o + n]

        def vcol(r):
            return VT[:, r:r + 1]

        def pt(i, n=1):
            return view(ysb, i * 64, [[1, 64 * n]])
        LR_, LI_, DT_, XR_, TH_, KQ_, RR_, SN_, SH_, CO_, MG_, T1_, T2_, FR_, FI_, DN_ = range(16)

        lam_v = view(yT, 448, [[64, 4], [1, 64]])
        block = keep.enter_context(nc.Block())

        @block.sync
        def _(sp):
            sent = [0]

            def slab_source(S):
                def w(t, c, n=P):
                    return t[:, c:c + n].rearrange("(k p) c -> p k c", p=P)
                if S < S_GLU:
                    kind, m = IN_ORDER[S]
                    return w(a["a_w_in"][0], m * P + (D if kind == "z" else 0))
                if S < S_P0:
                    m, half = divmod(S - S_GLU, 2)
                    return w(a["a_w_glu"][0], m * P + (0 if half else D))
                if S_H <= S < S_P1:
                    kind, m = HEAD_ORDER[S - S_H]
                    t = {"k": a["w_k"], "v": a["w_v"]}.get(kind, a["b_w_in"][0])
                    return w(t, m * P + (D if kind == "z" else 0))
                for base, end, t, c0, n in (
                        (S_P0, S_OUT, a["ple_w_proj"][0], 0, T), (S_OUT, S_G0, a["a_w_out"][0], 0, P),
                        (S_G0, S_H, a["ple_w_gate"][0], 0, P), (S_P1, S_BO, a["ple_w_proj"][1], 0, T),
                        (S_BO, S_G1, a["b_w_out"][0], 0, P), (S_G1, S_END, a["ple_w_gate"][1], 0, P)):
                    if base <= S < end:
                        return w(t, c0 + (S - base) * n, n)

            def slabs(upto):
                while sent[0] <= min(upto, S_END - 1):
                    S = sent[0]
                    after(sp, s.w_split, S - RAW + 1)
                    src = slab_source(S)
                    dst = raw[S % RAW][:].rearrange("p (k c) -> p k c", c=src.shape[2])
                    sp.dma_start(dst, src).then_inc(raw_in[S % RAW], 16)
                    sent[0] += 1

            sp.dma_start(cst[:], a["consts"]).then_inc(s.cst_in, 16)
            xv = a["x"][0].rearrange("(n s) d -> s n d", s=CH)
            for j in range(QB):
                for i in range(2):
                    sp.dma_start(xrow[i * NC:(i + 1) * NC, j * D:(j + 1) * D], xv[2 * j + i]).then_inc(x_in[j], 16)
            slabs(1)
            for k in range(KT):
                sp.wait_ge(s.x_copied, k + 1)
                sp.dma_start(xd[k], uT[:, k % 4, :]).then_inc(xs_out[k % 4], 16)
            slabs(5)
            sp.wait_ge(s.rows_ev, 1)
            sp.dma_start(bd[:, :, 0:T], view(p1, 0, [[0, P], [1, T]], np_=H)).then_inc(s.rows_out, 16)
            sp.dma_start(bd[:, :, T:REV], view(p2, 0, [[0, P], [1, REV - T]], np_=H)).then_inc(s.rows_out, 16)

            def turn_u(m):
                slabs(SLAB_OF["u", m] + 5)
                sp.wait_ge(s.u_ev, m + 1)
                sp.dma_start(ud[m], uT[:, m % 4, :]).then_inc(s.u_out, 16)
                sp.wait_ge(s.u_out, 16 * (m + 1))
                after(sp, s.ssm_y, m - 1)
                v = ud[m].rearrange("(g c) (s n) -> s c g n", c=GC, s=CH)
                for i in range(CH):
                    sp.dma_start(U[i * GC:(i + 1) * GC, m % 2, :, :], v[i]).then_inc(u_in[m % 2], 16)

            def swap_m(m):
                sp.wait_ge(s.m_built, m + 1)
                after(sp, s.ssm_y, m - 1)
                for i in range(2):
                    sp.dma_start(Msw[ST * i:ST * (i + 1), m % 2],
                                 M[ST * (1 - i):ST * (2 - i)].rearrange("p g t c -> p g (t c)")
                                 ).then_inc(msw_in[m % 2], 16)

            def turn_y(m):
                sp.wait_ge(s.y_ev, m + 1)
                sp.dma_start(yd[m], ysb[:, m % 2, :]).then_inc(s.y_out, 16)
                sp.wait_ge(s.y_out, 16 * (m + 1))
                after(sp, s.gelu, m - 1)
                v = yd[m].rearrange("(t c) (g n) -> g c t n", c=GC, g=GT)
                for i in range(GT):
                    sp.dma_start(yT[i * GC:(i + 1) * GC, m % 2, :].rearrange("p (t n) -> p t n", t=CH),
                                 v[i]).then_inc(y_in[m % 2], 16)

            def spill_z(m):
                sp.wait_ge(s.zz, m + 1)
                sp.dma_start(zd[m], st[:, m % 2, :]).then_inc(z_out[m % 2], 16)

            turn_u(0)
            turn_u(1)
            swap_m(0)
            for m in range(KT):
                if m + 1 < KT:
                    slabs(SLAB_OF["z", m + 1] + 2)
                turn_y(m)
                if m + 2 < KT:
                    turn_u(m + 2)
                if m + 1 < KT:
                    swap_m(m + 1)
                spill_z(m)
            slabs(S_GLU + 4)
            sp.wait_ge(s.y_lo, KT)
            for i in range(2):
                sp.wait_ge(z_out[i], 16 * KT // 2)
            sp.dma_start(zz[:], zd.rearrange("k p t -> p k t")).then_inc(s.zz_in, 16)
            sp.dma_start(xT[:], xd.rearrange("k p t -> p k t")).then_inc(s.xT_in, 16)
            pv = a["p"][0, 0].rearrange("(n s) d -> s n d", s=CH)
            for j in range(QB):
                for i in range(2):
                    sp.dma_start(prow[i * NC:(i + 1) * NC, j, :], pv[2 * j + i]).then_inc(s.p_in, 16)
            for m in range(KT):
                slabs(S_G0 + m + 5)
                sp.wait_ge(s.x1, m + 1)
                sp.dma_start(x1d[m], tb[2][:, m % 2, :]).then_inc(x1_out[m % 2], 16)
            sp.wait_ge(s.rows_out, 32)
            for m in range(H):
                slabs(S_H + 4 * m + 3)
                if m < 2:
                    sp.wait_ge(s.h_ev, 1)
                else:
                    sp.wait_ge(s.sc_read, 2 * QB * (m - 1))
                src = bass.AP(bd.tensor, m * P * REV + P - 1, [[REV - 1, P], [1, T]])
                sp.dma_start(bias[:, m % 2, :], src).then_inc(bias_in[m % 2], 16)
            slabs(S_H + 33)
            sp.wait_ge(s.w_used, S_H + 30)
            sp.dma_start(prow2[:], a["p"][1, 0].rearrange("(j p) d -> p j d", p=P)).then_inc(s.p2_in, 16)
            slabs(S_H + 35)
            sp.wait_ge(s.w_used, S_P1)
            for i in range(2):
                sp.wait_ge(x1_out[i], 16 * KT // 2)
            sp.dma_start(x1b[:], x1d.rearrange("k p t -> p k t")).then_inc(s.x1_in, 16)
            ov = out[0].rearrange("(j p) d -> p j d", p=P)
            for m in range(KT):
                slabs(S_G1 + m)
            for m in range(KT):
                sp.wait_ge(s.out_ev, m + 1)
                sp.dma_start(ov[:, :, m * P:(m + 1) * P],
                             tc[3][:, m % 2, :].rearrange("p (j c) -> p j c", c=P)).then_inc(o_out[m % 2], 16)
            for i in range(2):
                sp.wait_ge(o_out[i], 16 * KT // 2)

        @block.gpsimd
        def _(pool):
            nc.gpsimd.memset(Pp[:], 0.0).then_inc(s.zeroed, 1)
            nc.gpsimd.memset(TT[:], 0.0).then_inc(s.zeroed, 1)
            nc.gpsimd.memset(r8x[:], 0.0).then_inc(s.zeroed, 1)
            nc.gpsimd.memset(epsc, EPS).then_inc(s.zeroed, 1)
            for S in range(S_END):
                pool.wait_ge(raw_in[S % RAW], 16 * (S // RAW + 1))
                after(pool, s.w_used, S - RING + 1)
                nc.gpsimd.tensor_scalar(whi[S % RING][:], raw[S % RAW][:], 1.0, 0.0, ALU.mult,
                                        ALU.add).then_inc(s.w_hi, 1)
                pool.wait_ge(s.w_hi, S + 1)
                nc.gpsimd.tensor_tensor(wlo[S % RING][:], raw[S % RAW][:], whi[S % RING][:].bitcast(F32),
                                        ALU.subtract).then_inc(s.w_split, 1)

        @block.tensor
        def _(pe):
            mm = nc.tensor.matmul

            def exact(dst, wh, wl, xh, xl, first, last):
                mm(dst, wh, xh, start=first, stop=False)
                mm(dst, wh, xl, start=False, stop=False)
                return mm(dst, wl, xh, start=False, stop=last)

            def dense(S, xh, xl, b, ready, before=0):
                pe.wait_ge(s.w_split, S + 1)
                for k in range(KT):
                    for r in ready:
                        pe.wait_ge(r, before + k + 1)
                    c = slice(k * P, (k + 1) * P)
                    last = exact(ps(b), whi[S % RING][:, c], wlo[S % RING][:, c], xh[:, k, :], xl[:, k, :],
                                 k == 0, k == KT - 1)
                last.then_inc(s.w_used, 1)

            def turn(b, src, np_=P, n=P, o=0):
                return nc.tensor.transpose(bk[b][0:n, o:o + np_], src, ident[0:np_, 0:np_])

            def sum_squares(b, sq, k, done, before=0):
                pe.wait_ge(done, before + k + 1)
                mm(ps(b), cst[:, C_ONE:C_ONE + P], sq, start=k == 0, stop=k == KT - 1).then_inc(s.summed, 1)

            def square_sum(b, t, n):
                pe.wait_ge(s.acc, n)
                mm(ps(b), cst[:, C_ONE:C_ONE + P], t[:], start=True, stop=True).then_inc(s.summed, 1)

            pe.wait_ge(s.cst_in, 16)
            pe.wait_ge(s.par_in, 16 * N_PAR)
            turn(4, view(yT, 0, [[1, P]], np_=G), np_=G)
            turn(4, view(yT, P, [[1, P]], np_=G), np_=G, o=ST)
            turn(4, view(yT, 2 * P, [[1, P]], np_=V_ROWS), np_=V_ROWS, o=P).then_inc(s.par_T, 1)
            for k in range(KT):
                last = turn(5 + k // 4, view(Msw, k * P, [[1, P]]), o=(k % 4) * P)
            last.then_inc(s.c_T, 1)
            for k in range(KT + 2):
                if k < KT:
                    after(pe, s.x_copied, k - 3)
                    for j in range(QB):
                        if k == 0:
                            pe.wait_ge(x_in[j], 32)
                        last = turn(k % 4, xrow[:, j * D + k * P:j * D + (k + 1) * P], o=j * P)
                    last.then_inc(s.x_T, 1)
                if k >= 2:
                    sum_squares(7, (w1, w2)[k % 2][:], k - 2, s.x_sq)

            after(pe, s.x_copied, KT)
            dense(SLAB_OF["u", 0], hi0, lo0, 0, (s.x_hi, s.x_lo))
            pe.wait_ge(s.xc1, 2)
            for h in range(2):
                last = mm(ps(5 + h), cst[:, C_J2:C_J2 + P], view(XC1, h * T, [[1, T]]), start=True, stop=True)
            last.then_inc(s.xc2_mm, 1)
            pe.wait_ge(s.b_in, 32)
            for h in range(2):
                last = mm(ps(2 + h), cst[:, C_J1:C_J1 + P], view(XB1, h * T, [[1, T]]), start=True, stop=True)
            last.then_inc(s.xb2_mm, 1)
            dense(SLAB_OF["u", 1], hi0, lo0, 1, ())
            pe.wait_ge(s.par_read, 1)
            pe.wait_ge(s.hot, 2)
            mm(bk[4][0:H, 0:T], small[0:BUCKETS + 1, 8:16], cst[0:BUCKETS + 1, C_HOT:C_HOT + T],
               start=True, stop=True)
            pe.wait_ge(s.r1, 1)
            mm(bk[7][0:H, 0:REV - T], small[0:BUCKETS + 1, 8:16], cst[0:BUCKETS + 1, C_HOT + T:C_HOT + REV],
               start=True, stop=True).then_inc(s.rows_mm, 1)
            pe.wait_ge(s.xb1, 2)
            pe.wait_ge(s.xc2, 2)
            for h in range(2):
                last = mm(ps(5 + h), cst[:, C_J1:C_J1 + P], view(XB1, h * T, [[1, T]]), start=True, stop=True)
            last.then_inc(s.xb2_mm, 1)

            def ssm_weights(m):
                pe.wait_ge(s.p_built, m + 1)
                after(pe, s.win, 4 * m)
                if m == 0:
                    pe.wait_ge(s.xb2, 4)
                for g in range(GT):
                    last = turn(2 + g // 4, view(Pp, g * PADJ * GC, [[1, P]]), o=(g % 4) * P)
                last.then_inc(s.p_T, 1)
                after(pe, s.t_built, T_COPIES * m)
                if m == 0:
                    pe.wait_ge(s.rows_ev, 1)
                for g in range(GT):
                    for i in range(2):
                        last = mm(ps(4, GC, (2 * g + i) * GC),
                                  view(Pp, g * PADJ * GC + (1 - i) * GC, [[1, P]]),
                                  XC1[:, m * GT + g, :], start=True, stop=True)
                last.then_inc(s.t_mm, 1)

            def ssm_in(m):
                pe.wait_ge(s.win, 4 * (m + 1))
                pe.wait_ge(u_in[m % 2], 16 * CH * (m // 2 + 1))
                after(pe, s.rot, m)
                if m == 0:
                    pe.wait_ge(s.xb2, 4)
                for g in range(GT):
                    mm(ps(5, NC, g * NC), Win[:, g, :], U[:, m % 2, g, :], start=True, stop=True)
                    last = mm(ps(6, NC, g * NC), Wsw[:, g, :], U[:, m % 2, g, :], start=True, stop=True)
                last.then_inc(s.ssm_w, 1)

            def ssm_out(m):
                pe.wait_ge(s.p_rot, m + 1)
                pe.wait_ge(s.t_built, T_COPIES * (m + 1))
                pe.wait_ge(s.m_built, m + 1)
                pe.wait_ge(msw_in[m % 2], 32 * (m // 2 + 1))
                after(pe, s.y_ev, m)
                for g in range(GT):
                    o = ps(7, NC, g * NC)
                    mm(o, view(TT, g * P, [[1, P]]), U[:, m % 2, g, :], start=True, stop=False)
                    mm(o, view(M, g * P, [[1, P]]), p1[:, g * NC:(g + 1) * NC], start=False, stop=False)
                    last = mm(o, Msw[:, m % 2, g, :], p2[:, g * NC:(g + 1) * NC], start=False, stop=True)
                last.then_inc(s.ssm_y, 1)

            ssm_weights(0)
            for m in range(KT):
                ssm_in(m)
                S = SLAB_OF["z", m]
                after(pe, s.u_ev, len([x for x in IN_ORDER[:S] if x[0] == "u"]))
                after(pe, s.z_ev, m)
                dense(S, hi0, lo0, S % 2, ())
                ssm_out(m)
                if m + 2 < KT:
                    S = SLAB_OF["u", m + 2]
                    pe.wait_ge(s.u_ev, m + 2)
                    after(pe, s.z_ev, m)
                    dense(S, hi0, lo0, S % 2, ())
                if m + 1 < KT:
                    ssm_weights(m + 1)

            def turn_p(rows, src, arrived, b):
                pe.wait_ge(arrived, rows)
                if arrived is s.p2_in:
                    pe.wait_ge(s.h_ev, len(HEAD_ORDER) - 1)
                    pe.wait_ge(s.v_lo, H)
                for k in range(PK):
                    for j in range(QB):
                        last = turn(b[k], src[:, j, k * P:(k + 1) * P], o=j * P)
                last.then_inc(s.pT, 1)

            for m in range(KT):
                if m < 2:
                    pe.wait_ge(s.z_ev, KT)
                else:
                    pe.wait_ge(s.glu_tanh, m - 1)
                    pe.wait_ge(s.glu_y, m - 1)
                dense(S_GLU + 2 * m, hi0, lo0, 2 * (m % 2), (s.y_hi, s.y_lo) if m == 0 else ())
                dense(S_GLU + 2 * m + 1, hi0, lo0, 2 * (m % 2) + 1, ())
                if m == 3:
                    turn_p(16 * 8, prow, s.p_in, (4, 5))

            def project(S, ph, pl, b, n):
                pe.wait_ge(s.w_split, S + 1)
                pe.wait_ge(s.p_hi, n)
                pe.wait_ge(s.p_lo, n)
                for o in range(4):
                    for k in range(PK):
                        c = slice(k * T + o * P, k * T + (o + 1) * P)
                        last = exact(ps(b + o), whi[S % RING][:, c], wlo[S % RING][:, c], ph[:, k, :],
                                     pl[:, k, :], k == 0, k == PK - 1)
                last.then_inc(s.w_used, 1)

            project(S_P0, phi, plo, 4, PK)
            pe.wait_ge(s.glu_tanh, KT)
            pe.wait_ge(s.glu_y, KT)
            project(S_P0 + 1, phi, plo, 0, PK)

            for m in range(KT):
                if m < 2:
                    pe.wait_ge(s.pr_ev, 4)
                else:
                    pe.wait_ge(s.xa, m - 1)
                dense(S_OUT + m, hi1, lo1, 4 + m % 2, (s.glu_hi, s.glu_lo) if m == 0 else ())
            for m in range(KT):
                pe.wait_ge(*((s.xa, KT - 1 + m) if m < 2 else (s.g_ev, m - 1)))
                dense(S_G0 + m, hi0, lo0, 4 + m % 2, (s.xa_hi, s.xa_lo) if m == 0 else ())
                if m == 0:
                    square_sum(6, acc, KT - 1)
            def project_head(e):
                kind, m = HEAD_ORDER[e]
                if e == 0:
                    pe.wait_ge(s.pr_ev, KT)
                else:
                    after(pe, s.h_ev, e - 1)
                xh, xl = (hi1, lo1) if kind in "kv" else (hi2, lo2)
                ready = (s.n1_hi, s.n1_lo) if e == 0 else (s.n2_hi, s.n2_lo) if e == 1 else ()
                dense(S_H + e, xh, xl, e % 2, ready)
                if e == 0:
                    square_sum(6, acc, 2 * (KT - 1))

            def after_project(e):
                kind, m = HEAD_ORDER[e]
                if kind == "z":
                    return
                if e > 0:
                    last_kind, n = [x for x in HEAD_ORDER[:e] if x[0] != "z"][-1]
                    if last_kind == "v":
                        pe.wait_ge(s.v_lo, n + 1)
                    else:
                        pe.wait_ge(s.k_ln, 2 * n + (last_kind == "q") + 1)
                if kind == "v":
                    pe.wait_ge(s.h_ev, e + 1)
                    for j in range(QB):
                        last = turn(7, ta[0][:, e % 2, j * P:(j + 1) * P], o=j * P)
                    last.then_inc(s.v_T, 1)
                else:
                    pe.wait_ge(s.k_sq, 2 * m + (kind == "q") + 1)
                    mm(ps(7), cst[:, C_BLK:C_BLK + P], ta[1][:, e % 2, :], start=True,
                       stop=True).then_inc(s.k_bs, 1)

            def scores(j):
                m, I = divmod(j, QB)
                if I == 0:
                    pe.wait_ge(s.k_lo, 2 * m + 2)
                for c in range(2):
                    n = 2 * j + c
                    after(pe, s.sc_read, n - 1)
                    r = slice(c * HD, (c + 1) * HD)
                    q = slice(I * P, (I + 1) * P)
                    w = (I + 1) * P
                    exact(ps(2 + c, w), qh[r, m % 2, q], ql[r, m % 2, q], kh[r, m % 2, 0:w], kl[r, m % 2, 0:w],
                          True, True).then_inc(s.sc, 1)

            def apply(j):
                m, I = divmod(j, QB)
                pe.wait_ge(s.soft, j + 1)
                after(pe, s.at_lo, j)
                for t in range(I + 1):
                    last = turn(4, sco[0][:, j % 2, t * P:(t + 1) * P], o=t * P)
                last.then_inc(s.at, 1)

            def values(j):
                m, I = divmod(j, QB)
                pe.wait_ge(s.at_lo, j + 1)
                if I == 0:
                    after(pe, s.o_ev, m - 1)
                    pe.wait_ge(s.v_lo, m + 1)
                for t in range(I + 1):
                    last = exact(ps(5 + m % 2, P, I * P), ath[:, j % 2, t * P:(t + 1) * P],
                                 atl[:, j % 2, t * P:(t + 1) * P], vh[:, m % 2, t * P:(t + 1) * P],
                                 vl[:, m % 2, t * P:(t + 1) * P], t == 0, t == I)
                last.then_inc(s.pv, 1)

            def turn_o(m):
                pe.wait_ge(s.on, m + 1)
                for I in range(QB):
                    last = turn(5 + m % 2, on[:, I * P:(I + 1) * P], o=I * P)
                last.then_inc(s.o_T, 1)

            def project_p2(i):
                S = S_P1 + i
                pe.wait_ge(s.w_split, S + 1)
                pe.wait_ge(s.p_hi, 2 * PK)
                pe.wait_ge(s.p_lo, 2 * PK)
                pe.wait_ge(s.h_ev, len(HEAD_ORDER))
                for o in range(4):
                    after(pe, s.pr2_ev, 4 * i + o - 1)
                    for k in range(PK):
                        c = slice(k * T + o * P, k * T + (o + 1) * P)
                        last = exact(ps(o % 2), whi[S % RING][:, c], wlo[S % RING][:, c], phi2[:, k, :],
                                     plo2[:, k, :], k == 0, k == PK - 1)
                    last.then_inc(*((s.w_used, 1) if o == 3 else (s.pr2_mm, 1)))

            steps = H * QB
            slabs_h = len(HEAD_ORDER)
            for e in range(LEAD + steps + 2):
                j = e - LEAD
                if e < slabs_h:
                    project_head(e)
                elif e - slabs_h in (1, 2):
                    project_p2(e - slabs_h - 1)
                if 1 <= e <= slabs_h:
                    after_project(e - 1)
                if e == slabs_h - 1:
                    turn_p(16, prow2, s.p2_in, (0, 7))
                if 0 <= j + 1 < steps:
                    scores(j + 1)
                if 0 <= j < steps:
                    apply(j)
                if 1 <= j <= steps:
                    values(j - 1)
                if j >= QB + 1 and (j - 1) % QB == 0:
                    turn_o((j - 1) // QB - 1)

            for m in range(KT):
                if m >= 2:
                    pe.wait_ge(s.xa, KT + m - 1)
                else:
                    pe.wait_ge(*((s.at_lo, steps) if m == 0 else (s.o_ev, H)))
                dense(S_BO + m, hi0, lo0, 4 + m % 2, (s.o_hi, s.o_lo) if m == 0 else ())
            for m in range(KT + 1):
                if m < KT:
                    pe.wait_ge(*((s.xa, 2 * KT - 1 + m) if m < 2 else (s.g_ev, KT + m - 1)))
                    dense(S_G1 + m, hi1, lo1, 4 + m % 2, (s.xa_hi, s.xa_lo) if m == 0 else (), KT)
                    if m == 0:
                        square_sum(6, acc2, 3 * (KT - 1))
                if m >= 1:
                    pe.wait_ge(s.x2, m)
                    if m >= 3:
                        pe.wait_ge(s.out_ev, m - 2)
                    else:
                        pe.wait_ge(s.pr2_ev, KT)
                    for j in range(QB):
                        last = turn((m - 1) % 2, tc[2][:, (m - 1) % 2, j * P:(j + 1) * P], o=j * P)
                    last.then_inc(s.out_T, 1)

        @block.scalar
        def _(act):
            fn = nc.scalar.activation
            def dma(dst, src, which=s.par_in):
                act.dma_start(dst, src).then_inc(which, 16)
            for i in range(2):
                for n, t in ((0, a["a_lam_re"][0]), (P, a["a_lam_im"][0])):
                    dma(view(yT, n + i * ST, [[1, ST]], np_=G), t)
                dma(view(yT, 2 * P + i * HD, [[1, HD]], p0=V_QG, np_=1), a["b_q_norm_g"])
                dma(view(yT, 2 * P + i * HD, [[1, HD]], p0=V_KG, np_=1), a["k_norm_g"].rearrange("(a n) -> a n", a=1))
            for r, t in ((V_AG, a["a_norm_g"][0]), (V_D, a["a_d"][0]), (V_KVG, a["kv_norm_g"]),
                         (V_BG, a["b_norm_g"][0])):
                dma(view(yT, 2 * P, [[1, P]], p0=r, np_=KT), t.rearrange("(k p) -> k p", p=P))
            dma(view(yT, 2 * P, [[1, P]], p0=V_SUB, np_=1), a["b_subln_g"])
            dma(view(yT, 384, [[1, G]]), bass.AP(a["a_log_dt"].tensor, 0, [[0, P], [1, G]]))
            for i, n in enumerate(("b_lam_q1", "b_lam_k1", "b_lam_q2", "b_lam_k2")):
                dma(view(yT, 448 + i * 64, [[1, HD]]), bass.AP(a[n].tensor, 0, [[0, P], [1, HD]]))
            for i, t in enumerate((a["a_c_re"][0], a["a_c_im"][0])):
                dma(view(Msw, i * ST, [[P, KT], [1, ST]]), t.rearrange("(k g) c p -> (g c) k p", k=KT))
            for i, t in enumerate((a["a_b_re"][0], a["a_b_im"][0])):
                dma(XB1[i * ST:(i + 1) * ST], t.rearrange("g p c -> p g c"), s.b_in)
            dma(small[0:BUCKETS, 8:16], a["rel_bias"], s.hot_in)

            act.wait_ge(s.par_in, 16 * N_PAR)
            fn(pt(DT_), view(yT, 384, [[1, G]]), ACT.Exp).then_inc(s.dt, 1)
            act.wait_ge(s.xr, 1)
            fn(pt(MG_), pt(XR_), ACT.Exp).then_inc(s.mag, 1)
            act.wait_ge(s.lam_dot, 2)
            fn(small[:, 4:6], small[:, 2:4], ACT.Exp).then_inc(s.lam_e, 1)
            act.wait_ge(s.rr, 1)
            fn(pt(SN_), pt(RR_), ACT.Sin).then_inc(s.sin, 1)
            fn(pt(SH_), pt(RR_), ACT.Sin, scale=0.5).then_inc(s.sin, 1)

            act.wait_ge(s.vt, 1)
            for k in range(KT + 1):
                if k < KT:
                    act.wait_ge(s.x_T, k + 1)
                    fn(cols(hi0, k), ps(k % 4), ACT.Identity, scale=vcol(V_AG + k)).then_inc(s.x_hi, 1)
                if k >= 1:
                    act.wait_ge(s.x_copied, k)
                    after(act, s.summed, k - 2)
                    fn((w1, w2)[(k - 1) % 2][:], uT[:, (k - 1) % 4, :], ACT.Square).then_inc(s.x_sq, 1)

            def inverse_rms(n, b, version):
                act.wait_ge(s.summed, n)
                fn(R[:], ps(b), ACT.Ln, scale=1.0 / D, bias=epsc).then_inc(s.r_ln, 1)
                act.wait_ge(s.r_ln, version)
                fn(R[:], R[:], ACT.Exp, scale=-0.5).then_inc(s.r_norm, 1)

            act.wait_ge(s.zeroed, 4)
            inverse_rms(KT, 7, 1)
            act.wait_ge(s.r_norm, 1)
            fn(small[:, 6:7], epsc, ACT.Copy).then_inc(s.r1, 1)
            act.wait_ge(s.rows_mm, 1)
            fn(p1[0:H, :], bk[4][0:H, 0:T], ACT.Copy).then_inc(s.row0, 1)
            fn(p2[0:H, 0:REV - T], bk[7][0:H, 0:REV - T], ACT.Copy).then_inc(s.rows_ev, 1)
            
            def scan_ratio(m):
                if m == 0:
                    act.wait_ge(s.r8, 1)
                fn(view(r8x, 1, [[NC, GT], [1, NC - 1]]), view(r8, m * GT, [[1, GT], [0, NC - 1]]),
                   ACT.Copy).then_inc(s.ratio, 1)

            def input_weights(m):
                act.wait_ge(s.p_T, m + 1)
                after(act, s.ssm_w, m)
                for h in range(2):
                    fn(Win[:, 4 * h:4 * h + 4, :], ps(2 + h).rearrange("p (g s) -> p g s", g=4),
                       ACT.Copy).then_inc(s.win, 1)
                    fn(view(Wsw, 4 * h * P, [[P, 4], [ST, 2], [1, ST]]),
                       bass.AP(bk[2 + h], ST, [[T, P], [P, 4], [-ST, 2], [1, ST]]),
                       ACT.Copy).then_inc(s.win, 1)

            scan_ratio(0)
            input_weights(0)

            def gelu(m):
                act.wait_ge(s.comb, m + 1)
                fn(Y[:, m, :], yT[:, m % 2, :], ACT.Gelu_apprx_tanh).then_inc(s.gelu, 1)

            for m in range(KT):
                act.wait_ge(s.z_ev, m + 1)
                after(act, s.zz, m)
                fn(tz[:], st[:, m % 2, :], ACT.Tanh, scale=0.5).then_inc(s.z_tanh, 1)
                act.wait_ge(s.ssm_y, m + 1)
                if m >= 2:
                    act.wait_ge(s.y_out, 16 * (m - 1))
                fn(ysb[:, m % 2, :], ps(7), ACT.Copy).then_inc(s.y_ev, 1)
                if m >= 1:
                    gelu(m - 1)
                if m + 1 < KT:
                    act.wait_ge(s.scan, m + 1)
                    scan_ratio(m + 1)
                    input_weights(m + 1)
                if m == KT - 1:
                    act.wait_ge(s.w_used, S_GLU)
                    for k in range(KT - 1):
                        act.wait_ge(s.gelu, k + 1)
                        fn(cols(hi0, k), cols(Y, k), ACT.Copy).then_inc(s.y_hi, 1)
                    gelu(m)
                    act.wait_ge(s.gelu, KT)
                    fn(cols(hi0, m), cols(Y, m), ACT.Copy).then_inc(s.y_hi, 1)

            def split_p(ph, psb):
                for k in range(PK):
                    fn(ph[:, k, :], ps(psb[k]), ACT.Copy).then_inc(s.p_hi, 1)

            for m in range(KT + 1):
                if m < KT:
                    act.wait_ge(s.w_used, S_GLU + 2 * m + 1)
                    after(act, s.glu_y, m - 1)
                    if m == 0:
                        act.wait_ge(s.y_lo, KT)
                    fn(tb[1][:, m % 2, :], ps(2 * (m % 2)), ACT.Tanh, scale=0.5).then_inc(s.glu_tanh, 1)
                if m >= 1:
                    act.wait_ge(s.glu_y3, m)
                    fn(cols(hi1, m - 1), tb[2][:, (m - 1) % 2, :], ACT.Copy).then_inc(s.glu_hi, 1)
                if m == 4:
                    act.wait_ge(s.pT, 1)
                    split_p(phi, (4, 5))
            for i in range(2):
                act.wait_ge(s.w_used, S_P0 + i + 1)
                for o in range(4):
                    fn(cols(zz, 4 * i + o), ps(4 * (1 - i) + o), ACT.Copy).then_inc(s.pr_ev, 1)
            for m in range(KT):
                act.wait_ge(s.xa, m + 1)
                fn(cols(hi0, m), cols(xT, m), ACT.Copy).then_inc(s.xa_hi, 1)
                if m >= 3:
                    act.wait_ge(s.acc, m - 2)
                fn(acc[:] if m == 0 else tb[3][:, m % 2, :], cols(xT, m), ACT.Square).then_inc(s.xa_sq, 1)
            inverse_rms(KT + 1, 6, 2)
            for m in range(KT):
                act.wait_ge(s.g_ev, m + 1)
                after(act, s.g_pr, m - 1)
                fn(tb[1][:, m % 2, :], tb[0][:, m % 2, :], ACT.Tanh, scale=0.5).then_inc(s.g_tanh, 1)
                act.wait_ge(s.x1, m + 1)
                fn(cols(hi1, m), tb[2][:, m % 2, :], ACT.Identity, scale=vcol(V_KVG + m)).then_inc(s.n1_hi, 1)
                fn(cols(hi2, m), tb[2][:, m % 2, :], ACT.Identity, scale=vcol(V_BG + m)).then_inc(s.n2_hi, 1)
                if m == 0:
                    act.wait_ge(s.summed, KT + 1)
                if m >= 3:
                    act.wait_ge(s.acc, KT - 1 + m - 2)
                fn(acc[:] if m == 0 else tb[3][:, m % 2, :], tb[2][:, m % 2, :], ACT.Square).then_inc(s.x1_sq, 1)
            inverse_rms(KT + 2, 6, 3)

            def project_first(e):
                kind, m = HEAD_ORDER[e]
                if kind == "v":
                    return
                act.wait_ge(s.h_ev, e + 1)
                for last_kind, n in [x for x in HEAD_ORDER[e % 2:e:2] if x[0] != "v"][-1:]:
                    if last_kind == "z":
                        act.wait_ge(s.sz, n + 1)
                    else:
                        act.wait_ge(s.k_n, 2 * n + (last_kind == "q") + 1)
                if kind == "z":
                    fn(ta[1][:, e % 2, :], ta[0][:, e % 2, :], ACT.Tanh, scale=0.5).then_inc(s.b_tanh, 1)
                else:
                    fn(ta[1][:, e % 2, :], ta[0][:, e % 2, :], ACT.Square).then_inc(s.k_sq, 1)

            def project_second(e):
                kind, m = HEAD_ORDER[e]
                n = 2 * m + (kind == "q")
                if kind in "kq":
                    act.wait_ge(s.k_bs, n + 1)
                    t = ta[1][:, e % 2, :]
                    fn(t, ps(7), ACT.Ln, scale=1.0 / HD, bias=epsc).then_inc(s.k_ln, 1)
                    act.wait_ge(s.k_ln, n + 1)
                    fn(t, t, ACT.Exp, scale=-0.5).then_inc(s.k_r, 1)
                elif kind == "v":
                    act.wait_ge(s.v_T, m + 1)
                    after(act, s.pv, QB * (m - 1))
                    fn(vh[:, m % 2, :], ps(7), ACT.Copy).then_inc(s.v_hi, 1)

            def project_hi(e):
                kind, m = HEAD_ORDER[e]
                if kind in "kq":
                    act.wait_ge(s.k_n, 2 * m + (kind == "q") + 1)
                    after(act, s.sc, 2 * QB * (m - 1))
                    fn((kh if kind == "k" else qh)[:, m % 2, :], ta[2][:, e % 2, :], ACT.Copy).then_inc(s.k_hi, 1)

            def exps(j):
                w = (j % QB + 1) * P
                act.wait_ge(s.neg, j + 1)
                for c in range(2):
                    e = sco[c][:, j % 2, 0:w]
                    fn(e, e, ACT.Exp, bias=stat[:, j % 2, 4 + c:5 + c],
                       accum_out=stat[:, j % 2, 6 + c:7 + c]).then_inc(s.exp, 1)

            def at_hi(j):
                w = (j % QB + 1) * P
                act.wait_ge(s.at, j + 1)
                after(act, s.pv, j - 1)
                fn(ath[:, j % 2, 0:w], ps(4, w), ACT.Copy).then_inc(s.at_hi, 1)

            def o_norm(m):
                act.wait_ge(s.pv, QB * (m + 1))
                after(act, s.o_lo, m)
                for I in range(QB):
                    fn(on[:, I * P:(I + 1) * P], ps(5 + m % 2, P, I * P), ACT.Square,
                       accum_out=oss[:, I:I + 1]).then_inc(s.o_sq, 1)
                act.wait_ge(s.o_sq, QB * (m + 1))
                fn(oss[:, 4:8], oss[:, 0:4], ACT.Ln, scale=1.0 / P, bias=epsc).then_inc(s.o_ln, 1)
                act.wait_ge(s.o_ln, m + 1)
                fn(oss[:, 8:12], oss[:, 4:8], ACT.Exp, scale=-0.5).then_inc(s.o_r, 1)

            def o_hi(m):
                act.wait_ge(s.o_ev, m + 1)
                fn(cols(hi0, m), on[:], ACT.Copy).then_inc(s.o_hi, 1)

            steps = H * QB
            slabs_h = len(HEAD_ORDER)
            for e in range(LEAD + steps + 3):
                j = e - LEAD
                if 1 <= e <= slabs_h:
                    project_first(e - 1)
                if 2 <= e <= slabs_h + 1:
                    project_second(e - 2)
                if 0 <= j < steps:
                    exps(j)
                if 2 <= e <= slabs_h + 1:
                    project_hi(e - 2)
                if e == slabs_h:
                    act.wait_ge(s.pT, 2)
                    split_p(phi2, (0, 7))
                if 1 <= j <= steps:
                    at_hi(j - 1)
                if e - slabs_h in (1, 2):
                    i = e - slabs_h - 1
                    for o in range(4):
                        act.wait_ge(*((s.w_used, S_P1 + i + 1) if o == 3 else (s.pr2_mm, 3 * i + o + 1)))
                        fn(cols(pr2, 4 * i + o), ps(o % 2), ACT.Copy).then_inc(s.pr2_ev, 1)
                if j >= QB + 1 and (j - 1) % QB == 0:
                    o_norm((j - 1) // QB - 1)
                if j >= QB + 2 and (j - 2) % QB == 0:
                    o_hi((j - 2) // QB - 1)

            for m in range(KT):
                act.wait_ge(s.xa, KT + m + 1)
                fn(cols(hi1, m), cols(x1b, m), ACT.Copy).then_inc(s.xa_hi, 1)
                if m >= 3:
                    act.wait_ge(s.acc, 2 * (KT - 1) + m - 2)
                fn(acc2[:] if m == 0 else tc[3][:, m % 2, :], cols(x1b, m), ACT.Square).then_inc(s.xa_sq, 1)
            inverse_rms(KT + 3, 6, 4)
            for m in range(KT + 1):
                if m < KT:
                    act.wait_ge(s.g_ev, KT + m + 1)
                    after(act, s.g_pr, KT + m - 1)
                    fn(tc[1][:, m % 2, :], tc[0][:, m % 2, :], ACT.Tanh, scale=0.5).then_inc(s.g_tanh, 1)
                if m >= 1:
                    n = m - 1
                    act.wait_ge(s.out_T, n + 1)
                    if n >= 2:
                        act.wait_ge(o_out[n % 2], 16 * (n // 2))
                    fn(tc[3][:, n % 2, :], ps(n % 2), ACT.Copy).then_inc(s.out_ev, 1)

        @block.vector
        def _(dve):
            v = nc.vector
            tt, ts, stt, cp = v.tensor_tensor, v.tensor_scalar, v.scalar_tensor_tensor, v.tensor_copy
            MUL, ADD, SUB = ALU.mult, ALU.add, ALU.subtract
            steps_done = [0]

            def link(ins):
                steps_done[0] += 1
                ins.then_inc(s.dve_step, 1)
                dve.wait_ge(s.dve_step, steps_done[0])

            dve.wait_ge(s.par_T, 1)
            link(cp(pt(LR_), bk[4][:, 0:ST]))
            link(cp(pt(LI_), bk[4][:, ST:P]))
            cp(VT[:], bk[4][:, P:P + V_ROWS]).then_inc(s.par_read, 1)
            dve.wait_ge(s.par_read, 1)
            link(ts(vcol(V_QG), vcol(V_QG), HD ** -0.5, None, MUL))
            ts(vcol(V_SUB), vcol(V_SUB), 0.5 * (1 - LAM_INIT), None, MUL).then_inc(s.vt, 1)
            dve.wait_ge(s.dt, 1)
            tt(pt(XR_), pt(LR_), pt(DT_), MUL).then_inc(s.xr, 1)
            link(tt(pt(TH_), pt(LI_), pt(DT_), MUL))
            link(ts(pt(KQ_), pt(TH_), 1 / TWO_PI, MAGIC, MUL, ADD))
            link(ts(pt(KQ_), pt(KQ_), -MAGIC, None, ADD))
            link(stt(out=pt(RR_), in0=pt(KQ_), scalar=-PI_A, in1=pt(TH_), op0=MUL, op1=ADD))
            link(stt(out=pt(RR_), in0=pt(KQ_), scalar=-PI_B, in1=pt(RR_), op0=MUL, op1=ADD))
            link(stt(out=pt(RR_), in0=pt(KQ_), scalar=-PI_C, in1=pt(RR_), op0=MUL, op1=ADD))
            ts(pt(RR_), pt(RR_), 3.1415925, -3.1415925, ALU.min, ALU.max).then_inc(s.rr, 1)
            for i in range(2):
                v.tensor_tensor_reduce(view(tmp, i * 64, [[1, 64]]), lam_v[:, 2 * i, :], lam_v[:, 2 * i + 1, :],
                                       1.0, 0.0, MUL, ADD, small[:, 2 + i:3 + i]).then_inc(s.lam_dot, 1)
            dve.wait_ge(s.lam_e, 1)
            link(tt(small[:, 1:2], small[:, 5:6], small[:, 4:5], SUB))
            link(ts(small[:, 1:2], small[:, 1:2], -LAM_INIT, None, ADD))
            dve.wait_ge(s.hot_in, 16)
            v.memset(small[BUCKETS:BUCKETS + 1, 8:16], NEG).then_inc(s.hot, 2)

            for k in range(KT):
                dve.wait_ge(s.x_hi, k + 1)
                if k >= 4:
                    dve.wait_ge(xs_out[k % 4], 16)
                    dve.wait_ge(s.x_sq, k - 3)
                cp(uT[:, k % 4, :], ps(k % 4)).then_inc(s.x_copied, 1)
                dve.wait_ge(s.x_copied, k + 1)
                stt(out=cols(lo0, k), in0=uT[:, k % 4, :], scalar=vcol(V_AG + k), in1=cols(hi0, k).bitcast(F32),
                    op0=MUL, op1=SUB).then_inc(s.x_lo, 1)

            dve.wait_ge(s.c_T, 1)
            dve.wait_ge(s.cst_in, 16)
            sgn = cst[:, C_SGN:C_SGN + 1]
            for h in range(2):
                ts(view(XC1, h * T, [[1, T]]), ps(5 + h), sgn, None, MUL).then_inc(s.xc1, 1)
            dve.wait_ge(s.sin, 2)
            dve.wait_ge(s.mag, 1)
            link(tt(pt(CO_), pt(SH_), pt(SH_), MUL))
            link(ts(pt(CO_), pt(CO_), -2.0, 1.0, MUL, ADD))
            re, im = pw
            link(v.memset(re[:, 0, :], 1.0))
            link(v.memset(im[:, 0, :], 0.0))
            link(tt(re[:, 1, :], pt(MG_), pt(CO_), MUL))
            link(tt(im[:, 1, :], pt(MG_), pt(SN_), MUL))
            link(ts(pt(T1_), re[:, 1, :], -1.0, None, ADD))
            link(tt(pt(DN_), pt(LR_), pt(LR_), MUL))
            link(tt(pt(T2_), pt(LI_), pt(LI_), MUL))
            link(tt(pt(DN_), pt(DN_), pt(T2_), ADD))
            link(v.reciprocal(pt(DN_), pt(DN_)))
            link(tt(pt(FR_), pt(T1_), pt(LR_), MUL))
            link(tt(pt(T2_), im[:, 1, :], pt(LI_), MUL))
            link(tt(pt(FR_), pt(FR_), pt(T2_), ADD))
            link(tt(pt(FR_), pt(FR_), pt(DN_), MUL))
            link(tt(pt(FI_), im[:, 1, :], pt(LR_), MUL))
            link(tt(pt(T2_), pt(T1_), pt(LI_), MUL))
            link(tt(pt(FI_), pt(FI_), pt(T2_), SUB))
            link(tt(pt(FI_), pt(FI_), pt(DN_), MUL))

            def cmul(t, dst, n, i, j):
                r, q = t
                d0, x0 = slice(dst, dst + n), slice(i, i + n)
                bc = [view(z, j * G, [[0, n], [1, G]]) for z in t]
                A = view(tmp, 0, [[G, n], [1, G]])
                B = view(tmp, 4 * G, [[G, n], [1, G]])
                link(tt(A, r[:, x0, :], bc[0], MUL))
                link(tt(B, q[:, x0, :], bc[1], MUL))
                link(tt(r[:, d0, :], A, B, SUB))
                link(tt(A, r[:, x0, :], bc[1], MUL))
                link(tt(B, q[:, x0, :], bc[0], MUL))
                link(tt(q[:, d0, :], A, B, ADD))

            def powers(t):
                for dst, n, j in ((2, 1, 1), (3, 2, 2), (5, 4, 4)):
                    cmul(t, dst, n, 1, j)

            powers(pw)
            link(tt(pt(MG_), pt(MG_), pt(MG_), MUL))
            link(tt(pt(MG_), pt(MG_), pt(MG_), MUL))
            tt(r8[:], pt(MG_), pt(MG_), MUL).then_inc(s.r8, 1)
            dve.wait_ge(s.xb2_mm, 1)
            dve.wait_ge(s.b_in, 32)
            for h in range(2):
                gsl = slice(h * G // 2, (h + 1) * G // 2)
                x1 = XB1[:, gsl, :]
                x2 = XB2[:, gsl, :]
                fr = view(ysb, FR_ * 64 + h * G // 2, [[1, G // 2], [0, GC]])
                fi = view(ysb, FI_ * 64 + h * G // 2, [[1, G // 2], [0, GC]])
                link(tt(x2, ps(2 + h).rearrange("p (g c) -> p g c", c=GC), fi, MUL))
                link(tt(x1, x1, fr, MUL))
                tt(x1, x1, x2, ADD).then_inc(s.xb1, 1)
            dve.wait_ge(s.xc2_mm, 1)
            for h in range(2):
                cp(view(XC2, h * T, [[1, T]]), ps(5 + h)).then_inc(s.xc2, 1)

            for t in (gt, ft):
                link(v.memset(t[0][:, 0, :], 1.0))
                link(v.memset(t[1][:, 0, :], 0.0))
            link(cp(gt[0][:, 1, :], pt(CO_)))
            link(ts(gt[1][:, 1, :], pt(SN_), sgn, None, MUL))
            for _ in range(3):
                cmul(gt, 2, 1, 1, 1)
                link(cp(gt[0][:, 1, :], gt[0][:, 2, :]))
                link(cp(gt[1][:, 1, :], gt[1][:, 2, :]))
            powers(gt)
            link(cp(ft[0][:, 1, :], gt[0][:, CH, :]))
            link(cp(ft[1][:, 1, :], gt[1][:, CH, :]))
            powers(ft)
            dve.wait_ge(s.xb2_mm, 2)
            for h in range(2):
                cp(view(XB2, h * T, [[1, T]]), ps(5 + h)).then_inc(s.xb2, 2)
            dve.wait_ge(s.xb2, 4)

            dve.wait_ge(s.zeroed, 4)
            tmp4 = view(tmp, 0, [[P, GT], [GC, CH], [1, GC]])

            def powers_of(t, m, k0, step):
                return view(t, k0 * G + m * GT, [[1, GT], [step * G, CH], [0, GC]])

            def build_p(m):
                after(dve, s.t_mm, m)
                o = view(Pp, 0, [[PADJ * GC, GT], [GC, CH], [1, GC]])
                x1 = view(XB1, m * P, [[GC, GT], [0, CH], [1, GC]])
                x2 = view(XB2, m * P, [[GC, GT], [0, CH], [1, GC]])
                link(tt(tmp4, x2, powers_of(pw[1], m, CH - 1, -1), MUL))
                link(tt(o, x1, powers_of(pw[0], m, CH - 1, -1), MUL))
                tt(o, o, tmp4, ADD).then_inc(s.p_built, 1)

            def build_m(m):
                after(dve, s.ssm_y, m)
                x1 = view(XC1, m * P, [[GC, GT], [0, CH], [1, GC]])
                x2 = view(XC2, m * P, [[GC, GT], [0, CH], [1, GC]])
                dve.wait_ge(s.p_built, m + 1)
                link(tt(tmp4, x2, powers_of(pw[1], m, 1, 1), MUL))
                link(tt(M[:], x1, powers_of(pw[0], m, 1, 1), MUL))
                tt(M[:], M[:], tmp4, ADD).then_inc(s.m_built, 1)

            def phase_table(m):
                o = [[NC, GT], [8, 8], [1, 8]]
                fr, fi = [view(t, m * GT, [[1, GT], [G, 8], [0, 8]]) for t in ft]
                gr, gi = [view(t, m * GT, [[1, GT], [0, 8], [G, 8]]) for t in gt]
                C, S_, A, B = view(Ct, 0, o), view(St, 0, o), view(tmp, 0, o), view(tmp, T, o)
                if m > 0:
                    dve.wait_ge(s.p_rot, m)
                dve.wait_ge(s.p_built, m + 1)
                dve.wait_ge(s.m_built, max(m, 1))
                link(tt(A, fr, gr, MUL))
                link(tt(B, fi, gi, MUL))
                link(tt(C, A, B, SUB))
                link(tt(A, fr, gi, MUL))
                link(tt(B, fi, gr, MUL))
                link(tt(S_, A, B, ADD))

            def copy_t(m):
                dve.wait_ge(s.t_mm, m + 1)
                after(dve, s.ssm_y, m)
                for q, (src, n, dst) in enumerate(T_MOVES):
                    t0 = CH - 2 - 2 * ((src - dst) // 32)
                    cp(view(TT, t0 * GC, [[P, GT], [1, 2 * GC]], p0=dst, np_=n),
                       bass.AP(bk[4], src * T, [[T, n], [2 * GC, GT], [1, 2 * GC]])).then_inc(s.t_built, 1)

            def rotate(m):
                dve.wait_ge(s.ssm_w, m + 1)
                cut = [[NC, GT], [1, NC - 1]]
                A, B = view(w1, 1, cut), view(w2, 1, cut)
                C, S_ = view(Ct, 1, cut), view(St, 1, cut)
                link(tt(A, bass.AP(bk[5], 0, [[T, P]] + cut), C, MUL))
                tt(B, bass.AP(bk[6], 0, [[T, P]] + cut), S_, MUL).then_inc(s.rot, 1)
                dve.wait_ge(s.rot, m + 1)
                link(tt(A, A, B, ADD))
                dve.wait_ge(s.ratio, m + 1)
                v.tensor_tensor_scan(gs[:], r8x[:], w1[:], 0.0, MUL, ADD).then_inc(s.scan, 1)
                dve.wait_ge(s.scan, m + 1)
                after(dve, s.ssm_y, m)
                if m == 0:
                    dve.wait_ge(s.rows_out, 32)
                link(tt(p1[:], gs[:], Ct[:], MUL))
                tt(p2[:], gs[:], St[:], MUL).then_inc(s.p_rot, 1)

            def u_out(m):
                S = SLAB_OF["u", m]
                dve.wait_ge(s.w_used, S + 1)
                if m < 4:
                    dve.wait_ge(xs_out[m], 32)
                tt(uT[:, m % 4, :], ps(S % 2), R[:], MUL).then_inc(s.u_ev, 1)

            def combine(m):
                dve.wait_ge(y_in[m % 2], 16 * GT * (m // 2 + 1))
                stt(out=yT[:, m % 2, :], in0=uT[:, m % 4, :], scalar=vcol(V_D + m), in1=yT[:, m % 2, :],
                    op0=MUL, op1=ADD).then_inc(s.comb, 1)

            dve.wait_ge(s.x_sq, KT)
            dve.wait_ge(s.summed, KT)
            link(v.memset(w1[:], 0.0))
            dve.wait_ge(s.r_norm, 1)
            u_out(0)
            build_p(0)
            u_out(1)
            copy_t(0)
            build_m(0)
            phase_table(0)
            for m in range(KT):
                rotate(m)
                if m + 1 < KT:
                    build_p(m + 1)
                S = SLAB_OF["z", m]
                dve.wait_ge(s.w_used, S + 1)
                if m >= 2:
                    dve.wait_ge(z_out[m % 2], 16 * (m // 2))
                tt(st[:, m % 2, :], ps(S % 2), R[:], MUL).then_inc(s.z_ev, 1)
                if m >= 1:
                    combine(m - 1)
                dve.wait_ge(s.z_tanh, m + 1)
                stt(out=st[:, m % 2, :], in0=tz[:], scalar=1.0, in1=st[:, m % 2, :], op0=ADD,
                    op1=MUL).then_inc(s.zz, 1)
                if m + 2 < KT:
                    u_out(m + 2)
                if m + 1 < KT:
                    phase_table(m + 1)
                    copy_t(m + 1)
                    build_m(m + 1)
            for k in range(KT - 1):
                dve.wait_ge(s.y_hi, k + 1)
                tt(cols(lo0, k), cols(Y, k), cols(hi0, k).bitcast(F32), SUB).then_inc(s.y_lo, 1)
            combine(KT - 1)
            dve.wait_ge(s.y_hi, KT)
            tt(cols(lo0, KT - 1), cols(Y, KT - 1), cols(hi0, KT - 1).bitcast(F32), SUB).then_inc(s.y_lo, 1)

            def add_squares(m, to, sq, ready, before, done):
                if m > 0:
                    dve.wait_ge(ready, before + m + 1)
                    after(dve, s.acc, done + m - 1)
                    tt(to[:], to[:], sq[:, m % 2, :], ADD).then_inc(s.acc, 1)

            for m in range(KT):
                dve.wait_ge(s.w_used, S_GLU + 2 * m + 2)
                dve.wait_ge(s.glu_tanh, m + 1)
                y = tb[0][:, m % 2, :]
                stt(out=y, in0=tb[1][:, m % 2, :], scalar=1.0, in1=ps(2 * (m % 2) + 1), op0=ADD,
                    op1=MUL).then_inc(s.glu_y, 1)
                dve.wait_ge(s.glu_y, m + 1)
                if m == 0:
                    dve.wait_ge(s.zz_in, 16)
                after(dve, s.glu_hi, m - 1)
                stt(out=tb[2][:, m % 2, :], in0=y, scalar=0.25, in1=cols(zz, m), op0=MUL,
                    op1=MUL).then_inc(s.glu_y3, 1)
                dve.wait_ge(s.glu_hi, m + 1)
                tt(cols(lo1, m), tb[2][:, m % 2, :], cols(hi1, m).bitcast(F32), SUB).then_inc(s.glu_lo, 1)
                if m == 4:
                    for k in range(PK):
                        dve.wait_ge(s.p_hi, k + 1)
                        tt(plo[:, k, :], ps(4 + k), phi[:, k, :].bitcast(F32), SUB).then_inc(s.p_lo, 1)
            dve.wait_ge(s.xT_in, 16)
            for m in range(KT):
                dve.wait_ge(s.w_used, S_OUT + m + 1)
                tt(cols(xT, m), cols(xT, m), ps(4 + m % 2), ADD).then_inc(s.xa, 1)
                dve.wait_ge(s.xa_hi, m + 1)
                tt(cols(lo0, m), cols(xT, m), cols(hi0, m).bitcast(F32), SUB).then_inc(s.xa_lo, 1)
                add_squares(m, acc, tb[3], s.xa_sq, 0, 0)
            dve.wait_ge(s.r_norm, 2)
            dve.wait_ge(s.pr_ev, KT)
            for m in range(KT):
                dve.wait_ge(s.w_used, S_G0 + m + 1)
                tt(tb[0][:, m % 2, :], ps(4 + m % 2), R[:], MUL).then_inc(s.g_ev, 1)
                dve.wait_ge(s.g_tanh, m + 1)
                t = tb[1][:, m % 2, :]
                stt(out=t, in0=t, scalar=1.0, in1=cols(zz, m), op0=ADD, op1=MUL).then_inc(s.g_pr, 1)
                dve.wait_ge(s.g_pr, m + 1)
                if m >= 2:
                    dve.wait_ge(x1_out[m % 2], 16 * (m // 2))
                    dve.wait_ge(s.x1_sq, m - 1)
                stt(out=view(tb[2], (m % 2) * T, [[1, CH], [CH, NC]]),
                    in0=view(tb[1], (m % 2) * T, [[NC, CH], [1, NC]]), scalar=0.5,
                    in1=view(xT, m * T, [[NC, CH], [1, NC]]), op0=MUL, op1=ADD).then_inc(s.x1, 1)
                for hi, lo, g, hd, ld in ((hi1, lo1, V_KVG, s.n1_hi, s.n1_lo), (hi2, lo2, V_BG, s.n2_hi, s.n2_lo)):
                    dve.wait_ge(hd, m + 1)
                    stt(out=cols(lo, m), in0=tb[2][:, m % 2, :], scalar=vcol(g + m),
                        in1=cols(hi, m).bitcast(F32), op0=MUL, op1=SUB).then_inc(ld, 1)
                add_squares(m, acc, tb[3], s.x1_sq, 0, KT - 1)

            dve.wait_ge(s.r_norm, 3)
            for i in range(2):
                dve.wait_ge(x1_out[i], 16 * KT // 2)

            def project_ev(e):
                kind, m = HEAD_ORDER[e]
                dve.wait_ge(s.w_used, S_H + e + 1)
                if e >= 2:
                    k2, m2 = HEAD_ORDER[e - 2]
                    if k2 == "v":
                        dve.wait_ge(s.v_T, m2 + 1)
                    elif k2 == "z":
                        dve.wait_ge(s.sz, m2 + 1)
                    else:
                        dve.wait_ge(s.k_n, 2 * m2 + (k2 == "q") + 1)
                tt(ta[0][:, e % 2, :], ps(e % 2), R[:], MUL).then_inc(s.h_ev, 1)

            def project_n(e):
                kind, m = HEAD_ORDER[e]
                if kind in "kq":
                    n = 2 * m + (kind == "q")
                    dve.wait_ge(s.k_r, n + 1)
                    after(dve, s.k_lo, n)
                    stt(out=ta[2][:, e % 2, :], in0=ta[0][:, e % 2, :], scalar=vcol(V_KG if kind == "k" else V_QG),
                        in1=ta[1][:, e % 2, :], op0=MUL, op1=MUL).then_inc(s.k_n, 1)
                elif kind == "v":
                    dve.wait_ge(s.v_hi, m + 1)
                    tt(vl[:, m % 2, :], ps(7), vh[:, m % 2, :].bitcast(F32), SUB).then_inc(s.v_lo, 1)

            def project_lo(e):
                kind, m = HEAD_ORDER[e]
                if kind in "kq":
                    dve.wait_ge(s.k_hi, 2 * m + (kind == "q") + 1)
                    hi, lo = (kh, kl) if kind == "k" else (qh, ql)
                    tt(lo[:, m % 2, :], ta[2][:, e % 2, :], hi[:, m % 2, :].bitcast(F32), SUB).then_inc(s.k_lo, 1)

            def project_z(e):
                kind, m = HEAD_ORDER[e]
                if kind == "z":
                    dve.wait_ge(s.b_tanh, m + 1)
                    after(dve, s.o_ev, m - 1)
                    stt(out=sz[:, m % 2, :], in0=ta[1][:, e % 2, :], scalar=1.0, in1=ta[0][:, e % 2, :], op0=ADD,
                        op1=MUL).then_inc(s.sz, 1)

            def soft_in(j):
                m, I = divmod(j, QB)
                w = (I + 1) * P
                if I == 0:
                    dve.wait_ge(bias_in[m % 2], 16 * (m // 2 + 1))
                after(dve, s.at, j - 1)
                for c in range(2):
                    n = 2 * j + c
                    dve.wait_ge(s.sc, n + 1)
                    v.tensor_tensor_reduce(sco[c][:, j % 2, 0:w], ps(2 + c, w), bias[:, m % 2, T - w:T], 1.0,
                                           -3e38, ADD, ALU.max,
                                           stat[:, j % 2, 2 + c:3 + c]).then_inc(s.sc_read, 1)
                dve.wait_ge(s.sc_read, 2 * j + 2)
                ts(stat[:, j % 2, 4:6], stat[:, j % 2, 2:4], -1.0, None, MUL).then_inc(s.neg, 1)

            def soft_out(j):
                w = (j % QB + 1) * P
                dve.wait_ge(s.exp, 2 * j + 2)
                r = stat[:, j % 2, 8:10]
                link(v.reciprocal(r, stat[:, j % 2, 6:8]))
                link(tt(stat[:, j % 2, 10:11], stat[:, j % 2, 9:10], negl, MUL))
                link(ts(sco[0][:, j % 2, 0:w], sco[0][:, j % 2, 0:w], stat[:, j % 2, 8:9], None, MUL))
                stt(out=sco[0][:, j % 2, 0:w], in0=sco[1][:, j % 2, 0:w], scalar=stat[:, j % 2, 10:11],
                    in1=sco[0][:, j % 2, 0:w], op0=MUL, op1=ADD).then_inc(s.soft, 1)

            def at_lo(j):
                w = (j % QB + 1) * P
                dve.wait_ge(s.at_hi, j + 1)
                tt(atl[:, j % 2, 0:w], ps(4, w), ath[:, j % 2, 0:w].bitcast(F32), SUB).then_inc(s.at_lo, 1)

            def o_scale(m):
                dve.wait_ge(s.o_r, m + 1)
                for I in range(QB):
                    last = ts(on[:, I * P:(I + 1) * P], ps(5 + m % 2, P, I * P), oss[:, 8 + I:9 + I], None, MUL)
                last.then_inc(s.on, 1)

            def o_gate(m):
                dve.wait_ge(s.o_T, m + 1)
                dve.wait_ge(s.sz, m + 1)
                stt(out=on[:], in0=ps(5 + m % 2), scalar=vcol(V_SUB), in1=sz[:, m % 2, :], op0=MUL,
                    op1=MUL).then_inc(s.o_ev, 1)

            def o_lo_(m):
                dve.wait_ge(s.o_hi, m + 1)
                tt(cols(lo0, m), on[:], cols(hi0, m).bitcast(F32), SUB).then_inc(s.o_lo, 1)

            steps = H * QB
            slabs_h = len(HEAD_ORDER)
            for e in range(LEAD + steps + 4):
                j = e - LEAD
                if 1 <= e <= slabs_h:
                    project_ev(e - 1)
                if 0 <= j < steps:
                    soft_in(j)
                if 2 <= e <= slabs_h + 1:
                    project_n(e - 2)
                    project_lo(e - 2)
                if 0 <= j < steps:
                    soft_out(j)
                if e == slabs_h:
                    for k in range(PK):
                        dve.wait_ge(s.p_hi, PK + k + 1)
                        tt(plo2[:, k, :], ps((0, 7)[k]), phi2[:, k, :].bitcast(F32), SUB).then_inc(s.p_lo, 1)
                if 1 <= j <= steps:
                    at_lo(j - 1)
                if 1 <= e <= slabs_h:
                    project_z(e - 1)
                if j >= QB + 1 and (j - 1) % QB == 0:
                    o_scale((j - 1) // QB - 1)
                if j >= QB + 2 and (j - 2) % QB == 0:
                    o_gate((j - 2) // QB - 1)
                if j >= QB + 3 and (j - 3) % QB == 0:
                    o_lo_((j - 3) // QB - 1)

            dve.wait_ge(s.x1_in, 16)
            for m in range(KT):
                dve.wait_ge(s.w_used, S_BO + m + 1)
                tt(cols(x1b, m), cols(x1b, m), ps(4 + m % 2), ADD).then_inc(s.xa, 1)
                dve.wait_ge(s.xa_hi, KT + m + 1)
                tt(cols(lo1, m), cols(x1b, m), cols(hi1, m).bitcast(F32), SUB).then_inc(s.xa_lo, 1)
                add_squares(m, acc2, tc[3], s.xa_sq, KT, 2 * (KT - 1))
            dve.wait_ge(s.r_norm, 4)
            for m in range(KT):
                dve.wait_ge(s.w_used, S_G1 + m + 1)
                tt(tc[0][:, m % 2, :], ps(4 + m % 2), R[:], MUL).then_inc(s.g_ev, 1)
                dve.wait_ge(s.g_tanh, KT + m + 1)
                dve.wait_ge(s.pr2_ev, KT)
                t = tc[1][:, m % 2, :]
                stt(out=t, in0=t, scalar=1.0, in1=cols(pr2, m), op0=ADD, op1=MUL).then_inc(s.g_pr, 1)
                dve.wait_ge(s.g_pr, KT + m + 1)
                after(dve, s.out_T, m - 1)
                stt(out=tc[2][:, m % 2, :], in0=t, scalar=0.5, in1=cols(x1b, m), op0=MUL,
                    op1=ADD).then_inc(s.x2, 1)


_INS = ["x", "p", "a_norm_g", "a_w_in", "a_lam_re", "a_lam_im", "a_log_dt", "a_b_re", "a_b_im", "a_c_re",
        "a_c_im", "a_d", "a_w_glu", "a_w_out", "kv_norm_g", "w_k", "w_v", "k_norm_g", "b_norm_g", "b_w_in",
        "b_q_norm_g", "b_lam_q1", "b_lam_k1", "b_lam_q2", "b_lam_k2", "b_subln_g", "b_w_out", "rel_bias",
        "ple_w_proj", "ple_w_gate"]


def constants():
    c = np.zeros((P, C_END), np.float32)
    c[:, C_ID:C_ID + P] = np.eye(P)
    i = np.arange(ST)
    c[i, C_J1 + ST + i] = 1.0
    c[ST + i, C_J1 + i] = -1.0
    c[i, C_J2 + ST + i] = -1.0
    c[ST + i, C_J2 + i] = 1.0
    c[:, C_ONE:C_ONE + P] = 1.0
    c[:HD, C_BLK:C_BLK + HD] = 1.0
    c[HD:, C_BLK + HD:C_BLK + P] = 1.0
    rel = T - 1 - np.arange(REV)
    n = np.maximum(rel, 1).astype(np.float32)
    exact = BUCKETS // 2
    large = exact + (np.log(n / np.float32(exact)) / np.float32(math.log(128 / exact))
                     * np.float32(BUCKETS - exact)).astype(np.int32)
    bucket = np.where(rel < exact, rel, np.minimum(large, BUCKETS - 1))
    bucket = np.where(rel < 0, BUCKETS, bucket)
    c[bucket, C_HOT + np.arange(REV)] = 1.0
    c[:ST, C_SGN] = 1.0
    c[ST:, C_SGN] = -1.0
    return c


def kernel(**inputs):
    import concourse.bacc as _bacc
    from concourse.bass_utils import run_bass_kernel_spmd as _run

    nc = _bacc.Bacc("TRN2", target_bir_lowering=False, num_devices=1)
    arrays, args = {}, {}
    for name in _INS + ["consts"]:
        v = constants() if name == "consts" else np.ascontiguousarray(inputs[name])
        arrays[f"in_{name}"] = v
        args[name] = nc.dram_tensor(f"in_{name}", v.shape, mybir.dt.from_np(v.dtype), kind="ExternalInput").ap()
    out = nc.dram_tensor("out_x", (1, T, D), F32, kind="ExternalOutput").ap()
    build(nc, args, out)
    r = _run(nc, [arrays], core_ids=[0])
    return r.results[0]["out_x"]
```

```python
import math
from contextlib import ExitStack

import numpy as np
import concourse.bass as bass
from concourse import mybir

F32 = mybir.dt.float32
F32R = mybir.dt.float32r
ACT = mybir.ActivationFunctionType
ALU = mybir.AluOpType
AX = mybir.AxisListType

P = 128
D = 1024
T = 512
KT = D // P
CH = 8
NC = T // CH
G = 64
GC = 16
ST = 64
GT = P // GC
PADJ = 2 * CH - 1
H = 8
HD = 64
QB = T // P
PLE = 256
PK = PLE // P
EPS = 1e-6
LAM_INIT = 0.8 - 0.6 * math.exp(-0.3 * 1)
NEG = -1e30
BUCKETS = 32
REV = 640

RAW, RING = 2, 4

C_ID, C_J1, C_J2, C_ONE, C_BLK, C_HOT = 0, P, 2 * P, 3 * P, 4 * P, 5 * P
C_SGN = C_HOT + REV
C_END = C_SGN + 1

V_AG, V_D, V_KVG, V_BG, V_QG, V_KG, V_SUB, V_ROWS = 0, 8, 16, 24, 32, 33, 34, 35

TWO_PI = 2 * math.pi
PI_A = 6.28125
PI_B = float(np.float32(np.round((TWO_PI - PI_A) * 2 ** 20) / 2 ** 20))
PI_C = float(np.float32(TWO_PI - PI_A - PI_B))
MAGIC = 12582912.0

S_IN, S_GLU, S_P0, S_OUT, S_G0, S_H, S_P1, S_BO, S_G1, S_END = (
    0, 16, 32, 34, 42, 50, 82, 84, 92, 100)


N_PAR = 4 + 4 + 3 + 1 + 1
T_MOVES = ((0, 128, 0), (32, 32, 0), (64, 32, 32), (96, 32, 64), (64, 64, 0), (96, 32, 0))
T_COPIES = len(T_MOVES)


def in_order():
    order = [("u", 0), ("u", 1), ("u", 2), ("z", 0)]
    for m in range(KT):
        if m + 3 < KT:
            order.append(("u", m + 3))
        if m + 1 < KT:
            order.append(("z", m + 1))
    return order


IN_ORDER = in_order()
SLAB_OF = {x: i for i, x in enumerate(IN_ORDER)}


def head_order():
    order = [("k", 0), ("q", 0), ("v", 0)]
    for m in range(H):
        if m + 1 < H:
            order += [("k", m + 1), ("q", m + 1), ("v", m + 1)]
        order.append(("z", m))
    return order


HEAD_ORDER = head_order()
LEAD = 4


def build(nc, a, out):
    xd = nc.dram_tensor("xT_spill", (KT, P, T), F32, kind="Internal").ap()
    zd = nc.dram_tensor("gate_spill", (KT, P, T), F32, kind="Internal").ap()
    x1d = nc.dram_tensor("x1_spill", (KT, P, T), F32, kind="Internal").ap()
    ud = nc.dram_tensor("u_turn", (KT, P, T), F32, kind="Internal").ap()
    yd = nc.dram_tensor("y_turn", (KT, P, T), F32, kind="Internal").ap()
    bd = nc.dram_tensor("bias_rows", (H, P, REV), F32, kind="Internal").ap()

    def mk(name, shape, dt=F32):
        return nc.sbuf_tensor(name, shape, dt)

    with ExitStack() as keep:
        def sb(name, shape, dt=F32):
            return keep.enter_context(mk(name, shape, dt))

        def sem(name):
            return keep.enter_context(nc.semaphore(name))

        def sems(names):
            return [sem(name) for name in names.split()]

        raw = [sb(f"raw{i}", [P, D]) for i in range(RAW)]
        whi = [sb(f"whi{i}", [P, D], F32R) for i in range(RING)]
        wlo = [sb(f"wlo{i}", [P, D], F32R) for i in range(RING)]
        cst = sb("cst", [P, C_END])
        VT = sb("VT", [P, V_ROWS])
        R = sb("R", [P, T])
        small = sb("small", [P, 64])
        oss = small[:, 16:32]
        hi0 = sb("hi0", [P, KT, T], F32R)
        lo0 = sb("lo0", [P, KT, T], F32R)
        ident = cst[:, C_ID:C_ID + P]
        again = small[:, 32:40]
        epsc, negl, lamc = small[:, 0:1], small[:, 1:2], small[:, 2:6]

        with ExitStack() as s5:
            def sa(name, shape, dt=F32):
                return s5.enter_context(mk(name, shape, dt))
            Y = sa("Y", [P, KT, T])
            Pp = sa("Pp", [P, GT, PADJ, GC])
            Win = sa("Win", [P, GT, P])
            TT = sa("TT", [P, 2, GT, CH, GC])
            M = sa("M", [P, 2, GT, CH, GC])
            XB1 = sa("XB1", [P, G, GC])
            XB2 = sa("XB2", [P, G, GC])
            XC1 = sa("XC1", [P, G, GC])
            XC2 = sa("XC2", [P, G, GC])
            pw = [sa(f"pw{i}", [P, CH + 1, G]) for i in range(2)]
            gt = [sa(f"gt{i}", [P, CH + 1, G]) for i in range(2)]
            ft = [sa(f"ft{i}", [P, CH + 1, G]) for i in range(2)]
            r8 = sa("r8", [P, G])
            Ct = sa("Ct", [P, T])
            St = sa("St", [P, T])
            tmp = sa("tmp", [P, D])
            U = sa("U", [P, 4, GT, NC])
            h = sa("h", [P, 2, T])
            w1 = sa("w1", [P, T])
            w2 = sa("w2", [P, T])
            gs = sa("gs", [P, T])
            p1 = sa("p1", [P, T])
            p2 = sa("p2", [P, T])
            ysb = sa("ysb", [P, 2, T])
            yT = sa("yT", [P, 2, T])
            uT = sa("uT", [P, 4, T])
            st = sa("st", [P, 2, T])
            r8x = sa("r8x", [P, T])
            tz = sa("tz", [P, T])
        xrow = Y[:, :, :].rearrange("p a b -> p (a b)")
        pt = ysb[:, :, :].rearrange("p a b -> p (a b)")

        with ExitStack() as rest:
            def sc(name, shape, dt=F32, scope=rest):
                return scope.enter_context(mk(name, shape, dt))
            with ExitStack() as e:
                hi1 = sc("hi1", [P, KT, T], F32R, e)
            with ExitStack() as e:
                prow2 = sc("prow2", [P, QB, PLE], F32, e)
                phi2 = sc("phi2", [P, PK, T], F32R, e)
                plo2 = sc("plo2", [P, PK, T], F32R, e)
            sc("hi1_place", [P, KT, T], F32R)
            lo1 = sc("lo1", [P, KT, T], F32R)
            with ExitStack() as e:
                hi2 = sc("hi2", [P, KT, T], F32R, e)
                lo2 = sc("lo2", [P, KT, T], F32R, e)
            with ExitStack() as e:
                x1b = sc("x1b", [P, KT, T], F32, e)
                pr2 = sc("pr2", [P, KT, T], F32, e)
            sc("pair2_place", [P, 2, KT, T], F32R)
            with ExitStack() as e:
                zz = sc("zz", [P, KT, T], F32, e)
                xT = sc("xT", [P, KT, T], F32, e)
                prow = sc("prow", [P, QB, PLE], F32, e)
                phi = sc("phi", [P, PK, T], F32R, e)
                plo = sc("plo", [P, PK, T], F32R, e)
                tb = [sc(f"tb{i}", [P, 2, T], F32, e) for i in range(4)]
                acc = sc("acc", [P, T], F32, e)
            with ExitStack() as e:
                kh, kl, qh, ql, vh, vl = [sc(n, [P, 2, T], F32R, e) for n in ("kh", "kl", "qh", "ql", "vh", "vl")]
                ta = [sc(f"ta{i}", [P, 2, T], F32, e) for i in range(3)]
                sz = sc("sz", [P, 2, T], F32, e)
                bias = sc("bias", [P, 2, T], F32, e)
                sco = [sc(f"sco{c}", [P, 2, T], F32, e) for c in range(2)]
                ath = sc("ath", [P, 2, T], F32R, e)
                atl = sc("atl", [P, 2, T], F32R, e)
                on = sc("on", [P, T], F32, e)
                stat = sc("stat", [P, 2, 16], F32, e)
            with ExitStack() as e:
                tc = [sc(f"tc{i}", [P, 2, T], F32, e) for i in range(4)]
                acc2 = sc("acc2", [P, T], F32, e)
        bk = [keep.enter_context(nc.psum_tensor(f"bank{i}", [P, T], F32)) for i in range(8)]

        class s:
            x_in = sem("x_in")
            cst_in, par_in, b_in, hot_in, par_T, par_read = sems("cst_in par_in b_in hot_in par_T par_read")
            ag_in, ag_T, ag, lamv_in, c_in = sems("ag_in ag_T ag lamv_in c_in")
            dt, xr, mag, lam_dot, lam_e = sems("dt xr mag lam_dot lam_e")
            rr, sin, hot, rows_mm, rows_ev = sems("rr sin hot rows_mm rows_ev")
            rows_out, zeroed, dve_step = sems("rows_out zeroed dve_step")
            c_T, xc1, xc2, xc2_mm, xb1, xb2 = sems("c_T xc1 xc2 xc2_mm xb1 xb2")
            xb2_mm, r8 = sems("xb2_mm r8")
            w_hi, w_split, w_used = sems("w_hi w_split w_used")
            x_T, x_copied, x_hi, x_lo, x_sq, summed = sems("x_T x_copied x_hi x_lo x_sq summed")
            r_ln, r_norm = sems("r_ln r_norm")
            u_ev, u_out, z_ev, z_tanh, zz = sems("u_ev u_out z_ev z_tanh zz")
            p_built, p_T, win, t_mm, t_built, m_built = sems("p_built p_T win t_mm t_built m_built")
            ratio, ssm_w, rot, scan, p_rot, ssm_y = sems("ratio ssm_w rot scan p_rot ssm_y")
            y_ev, y_out, comb, gelu, y_hi, y_lo = sems("y_ev y_out comb gelu y_hi y_lo")
            w_sw, p_sw, h = sems("w_sw p_sw h_ready")
            cosine, pool_step, phases = sems("cosine pool_step phases")
            acc = sem("acc_ready")
            zz_in, xT_in, glu_tanh, glu_y, glu_y3, glu_hi = sems("zz_in xT_in glu_tanh glu_y glu_y3 glu_hi")
            glu_lo, p_in, p2_in, pT, p_hi, p_lo = sems("glu_lo p_in p2_in pT p_hi p_lo")
            pr_ev, pr2_mm, pr2_ev = sems("pr_ev pr2_mm pr2_ev")
            xa, xa_hi, xa_lo, xa_sq, g_ev, g_tanh = sems("xa xa_hi xa_lo xa_sq g_ev g_tanh")
            g_pr, x1, x1_sq, n1_hi, n1_lo, n2_hi = sems("g_pr x1 x1_sq n1_hi n1_lo n2_hi")
            n2_lo, x1_in, x2, out_T, out_ev = sems("n2_lo x1_in x2 out_T out_ev")
            h_ev, k_sq, k_bs, k_ln, k_r, k_n = sems("h_ev k_sq k_bs k_ln k_r k_n")
            k_hi, k_lo, v_T, v_hi, v_lo = sems("k_hi k_lo v_T v_hi v_lo")
            b_tanh, sz = sems("b_tanh sz")
            sc, sc_read, neg, exp, soft, at = sems("sc sc_read neg exp soft at")
            at_hi, at_lo, pv, o_sq, o_ln, o_r = sems("at_hi at_lo pv o_sq o_ln o_r")
            on, o_T, o_ev, o_hi, o_lo = sems("on o_T o_ev o_hi o_lo")
        raw_in = [sem(f"raw_in{i}") for i in range(RAW)]
        xs_out = [sem(f"xs_out{i}") for i in range(4)]
        u_in = [sem(f"u_in{i}") for i in range(4)]
        y_in = [sem(f"y_in{i}") for i in range(2)]
        z_out = [sem(f"z_out{i}") for i in range(2)]
        x1_out = [sem(f"x1_out{i}") for i in range(2)]
        bias_in = [sem(f"bias_in{i}") for i in range(2)]
        o_out = [sem(f"o_out{i}") for i in range(2)]

        def after(eng, which, n):
            if n > 0:
                eng.wait_ge(which, n)

        def view(t, off, dims, p0=0, np_=P):
            pitch = int(np.prod(t.shape[1:]))
            return bass.AP(t, p0 * pitch + off, [[pitch, np_]] + [list(d) for d in dims])

        def cols(t, m):
            return t[:, m, :]

        def ps(b, n=T, o=0):
            return bk[b][:, o:o + n]

        def vcol(r):
            return VT[:, r:r + 1]

        def powers_of(t, m, k0, step):
            return view(t, k0 * G + m * GT, [[1, GT], [step * G, CH], [0, GC]])

        def cmul(tt, link, A, B, t, dst, n, i, j):
            r, q = t
            d0, x0 = slice(dst, dst + n), slice(i, i + n)
            bc = [view(z, j * G, [[0, n], [1, G]]) for z in t]
            A, B = A[:, 0:n, :], B[:, 0:n, :]
            link(tt(A, r[:, x0, :], bc[0], ALU.mult))
            link(tt(B, q[:, x0, :], bc[1], ALU.mult))
            link(tt(r[:, d0, :], A, B, ALU.subtract))
            link(tt(A, r[:, x0, :], bc[1], ALU.mult))
            link(tt(B, q[:, x0, :], bc[0], ALU.mult))
            link(tt(q[:, d0, :], A, B, ALU.add))

        def powers(tt, link, A, B, t):
            for dst, n, j in ((2, 1, 1), (3, 2, 2), (5, 4, 4)):
                cmul(tt, link, A, B, t, dst, n, 1, j)

        def pt(i, n=1):
            return view(ysb, i * 64, [[1, 64 * n]])
        LR_, LI_, DT_, XR_, TH_, KQ_, RR_, SN_, SH_, CO_, MG_, T1_, T2_, FR_, FI_, DN_ = range(16)

        lam_v = view(yT, 448, [[64, 4], [1, 64]])
        block = keep.enter_context(nc.Block())

        @block.sync
        def _(sp):
            sent = [0]

            def slab_source(S):
                def w(t, c, n=P):
                    return t[:, c:c + n].rearrange("(k p) c -> p k c", p=P)
                if S < S_GLU:
                    kind, m = IN_ORDER[S]
                    return w(a["a_w_in"][0], m * P + (D if kind == "z" else 0))
                if S < S_P0:
                    m, half = divmod(S - S_GLU, 2)
                    return w(a["a_w_glu"][0], m * P + (0 if half else D))
                if S_H <= S < S_P1:
                    kind, m = HEAD_ORDER[S - S_H]
                    t = {"k": a["w_k"], "v": a["w_v"]}.get(kind, a["b_w_in"][0])
                    return w(t, m * P + (D if kind == "z" else 0))
                for base, end, t, c0, n in (
                        (S_P0, S_OUT, a["ple_w_proj"][0], 0, T), (S_OUT, S_G0, a["a_w_out"][0], 0, P),
                        (S_G0, S_H, a["ple_w_gate"][0], 0, P), (S_P1, S_BO, a["ple_w_proj"][1], 0, T),
                        (S_BO, S_G1, a["b_w_out"][0], 0, P), (S_G1, S_END, a["ple_w_gate"][1], 0, P)):
                    if base <= S < end:
                        return w(t, c0 + (S - base) * n, n)

            def slabs(upto):
                while sent[0] <= min(upto, S_END - 1):
                    S = sent[0]
                    after(sp, s.w_split, S - RAW + 1)
                    src = slab_source(S)
                    dst = raw[S % RAW][:].rearrange("p (k c) -> p k c", c=src.shape[2])
                    sp.dma_start(dst, src).then_inc(raw_in[S % RAW], 16)
                    sent[0] += 1

            def dma(dst, src, which=s.par_in):
                sp.dma_start(dst, src).then_inc(which, 16)
            sp.dma_start(cst[:], a["consts"]).then_inc(s.cst_in, 16)
            dma(view(yT, 2 * P, [[1, P]], p0=V_AG, np_=KT), a["a_norm_g"][0].rearrange("(k p) -> k p", p=P), s.ag_in)
            xv = a["x"][0].rearrange("(n s) d -> s n d", s=CH)
            for j in range(QB):
                for i in range(2):
                    sp.dma_start(xrow[i * NC:(i + 1) * NC, j * D:(j + 1) * D], xv[2 * j + i]).then_inc(s.x_in, 16)
            slabs(1)
            for i in range(2):
                for n, t in ((0, a["a_lam_re"][0]), (P, a["a_lam_im"][0])):
                    dma(view(yT, n + i * ST, [[1, ST]], np_=G), t)
                dma(view(yT, 2 * P + i * HD, [[1, HD]], p0=V_QG, np_=1), a["b_q_norm_g"])
                dma(view(yT, 2 * P + i * HD, [[1, HD]], p0=V_KG, np_=1), a["k_norm_g"].rearrange("(a n) -> a n", a=1))
            for r, t in ((V_D, a["a_d"][0]), (V_KVG, a["kv_norm_g"]), (V_BG, a["b_norm_g"][0])):
                dma(view(yT, 2 * P, [[1, P]], p0=r, np_=KT), t.rearrange("(k p) -> k p", p=P))
            dma(view(yT, 2 * P, [[1, P]], p0=V_SUB, np_=1), a["b_subln_g"])
            dma(view(yT, 384, [[1, G]]), bass.AP(a["a_log_dt"].tensor, 0, [[0, P], [1, G]]))
            for i, t in enumerate((a["a_c_re"][0], a["a_c_im"][0])):
                dma(view(M, i * ST, [[P, KT], [1, ST]]), t.rearrange("(k g) c p -> (g c) k p", k=KT), s.c_in)
            for i, t in enumerate((a["a_b_re"][0], a["a_b_im"][0])):
                dma(XB1[i * ST:(i + 1) * ST], t.rearrange("g p c -> p g c"), s.b_in)
            for i, n in enumerate(("b_lam_q1", "b_lam_k1", "b_lam_q2", "b_lam_k2")):
                dma(view(yT, 448 + i * 64, [[1, HD]]), bass.AP(a[n].tensor, 0, [[0, P], [1, HD]]), s.lamv_in)
            dma(small[0:BUCKETS, 8:16], a["rel_bias"], s.hot_in)
            for k in range(KT):
                sp.wait_ge(s.x_copied, k + 1)
                sp.dma_start(xd[k], uT[:, k % 4, :]).then_inc(xs_out[k % 4], 16)
            slabs(4)
            def turn_u(m):
                sp.wait_ge(s.u_ev, m + 1)
                sp.dma_start(ud[m], uT[:, m % 4, :]).then_inc(s.u_out, 16)
                sp.wait_ge(s.u_out, 16 * (m + 1))
                after(sp, s.ssm_y, m - 3)
                v = ud[m].rearrange("(g c) (s n) -> s c g n", c=GC, s=CH)
                for i in range(CH):
                    sp.dma_start(U[i * GC:(i + 1) * GC, m % 4, :, :], v[i]).then_inc(u_in[m % 4], 16)

            def turn_y(m):
                sp.wait_ge(s.y_ev, m + 1)
                sp.dma_start(yd[m], ysb[:, m % 2, :]).then_inc(s.y_out, 16)
                sp.wait_ge(s.y_out, 16 * (m + 1))
                after(sp, s.gelu, m - 1)
                v = yd[m].rearrange("(t c) (g n) -> g c t n", c=GC, g=GT)
                for i in range(GT):
                    sp.dma_start(yT[i * GC:(i + 1) * GC, m % 2, :].rearrange("p (t n) -> p t n", t=CH),
                                 v[i]).then_inc(y_in[m % 2], 16)

            def spill_z(m):
                sp.wait_ge(s.zz, m + 1)
                sp.dma_start(zd[m], st[:, m % 2, :]).then_inc(z_out[m % 2], 16)

            for m in range(3):
                slabs(m + 4)
                if m == 2:
                    sp.wait_ge(s.rows_ev, 2)
                    sp.dma_start(bd[:, :, 0:T], view(p1, 0, [[0, P], [1, T]], np_=H)).then_inc(s.rows_out, 16)
                    sp.dma_start(bd[:, :, T:REV], view(p2, 0, [[0, P], [1, REV - T]], np_=H)).then_inc(s.rows_out, 16)
                turn_u(m)
            for m in range(KT + 1):
                slabs(min(2 * m + 8, S_GLU + 1))
                if m >= 1:
                    turn_y(m - 1)
                if m + 3 < KT:
                    turn_u(m + 3)
                if m < KT - 2:
                    spill_z(m)
            spill_z(KT - 2)
            spill_z(KT - 1)
            slabs(S_GLU + 4)
            sp.wait_ge(s.y_lo, KT)
            for i in range(2):
                sp.wait_ge(z_out[i], 16 * KT // 2)
            sp.dma_start(zz[:], zd.rearrange("k p t -> p k t")).then_inc(s.zz_in, 16)
            sp.dma_start(xT[:], xd.rearrange("k p t -> p k t")).then_inc(s.xT_in, 16)
            pv = a["p"][0, 0].rearrange("(n s) d -> s n d", s=CH)
            for j in range(QB):
                for i in range(2):
                    sp.dma_start(prow[i * NC:(i + 1) * NC, j, :], pv[2 * j + i]).then_inc(s.p_in, 16)
            for m in range(KT):
                slabs(S_G0 + m + 5)
                sp.wait_ge(s.x1, m + 1)
                sp.dma_start(x1d[m], tb[2][:, m % 2, :]).then_inc(x1_out[m % 2], 16)
            sp.wait_ge(s.rows_out, 32)
            for m in range(H):
                slabs(S_H + 4 * m + 3)
                if m < 2:
                    sp.wait_ge(s.h_ev, 1)
                else:
                    sp.wait_ge(s.sc_read, 2 * QB * (m - 1))
                src = bass.AP(bd.tensor, m * P * REV + P - 1, [[REV - 1, P], [1, T]])
                sp.dma_start(bias[:, m % 2, :], src).then_inc(bias_in[m % 2], 16)
            slabs(S_H + 33)
            sp.wait_ge(s.w_used, S_H + 30)
            sp.dma_start(prow2[:], a["p"][1, 0].rearrange("(j p) d -> p j d", p=P)).then_inc(s.p2_in, 16)
            slabs(S_H + 35)
            sp.wait_ge(s.w_used, S_P1)
            for i in range(2):
                sp.wait_ge(x1_out[i], 16 * KT // 2)
            sp.dma_start(x1b[:], x1d.rearrange("k p t -> p k t")).then_inc(s.x1_in, 16)
            ov = out[0].rearrange("(j p) d -> p j d", p=P)
            for m in range(KT):
                slabs(S_G1 + m)
            for m in range(KT):
                sp.wait_ge(s.out_ev, m + 1)
                sp.dma_start(ov[:, :, m * P:(m + 1) * P],
                             tc[3][:, m % 2, :].rearrange("p (j c) -> p j c", c=P)).then_inc(o_out[m % 2], 16)
            for i in range(2):
                sp.wait_ge(o_out[i], 16 * KT // 2)

        @block.gpsimd
        def _(pool):
            nc.gpsimd.memset(Pp[:], 0.0).then_inc(s.zeroed, 1)
            nc.gpsimd.memset(TT[:], 0.0).then_inc(s.zeroed, 1)
            nc.gpsimd.memset(r8x[:], 0.0).then_inc(s.zeroed, 1)
            nc.gpsimd.memset(epsc, EPS).then_inc(s.zeroed, 1)

            def split(S):
                pool.wait_ge(raw_in[S % RAW], 16 * (S // RAW + 1))
                after(pool, s.w_used, S - RING + 1)
                nc.gpsimd.tensor_scalar(whi[S % RING][:], raw[S % RAW][:], 1.0, 0.0, ALU.mult,
                                        ALU.add).then_inc(s.w_hi, 1)
                pool.wait_ge(s.w_hi, S + 1)
                nc.gpsimd.tensor_tensor(wlo[S % RING][:], raw[S % RAW][:], whi[S % RING][:].bitcast(F32),
                                        ALU.subtract).then_inc(s.w_split, 1)

            done = [0]

            def link(ins):
                done[0] += 1
                ins.then_inc(s.pool_step, 1)
                pool.wait_ge(s.pool_step, done[0])

            tmp4 = view(Y, 6 * T, [[P, GT], [GC, CH], [1, GC]])

            def build_m(m):
                tt = nc.gpsimd.tensor_tensor
                if m == 0:
                    pool.wait_ge(s.r8, 1)
                    pool.wait_ge(s.xc2, 2)
                    pool.wait_ge(s.x_T, KT)
                after(pool, s.ssm_y, m - 1)
                o = view(M, (m % 2) * D, [[P, GT], [GC, CH], [1, GC]])
                x1 = view(XC1, m * P, [[GC, GT], [0, CH], [1, GC]])
                x2 = view(XC2, m * P, [[GC, GT], [0, CH], [1, GC]])
                after(pool, s.m_built, m)
                link(tt(tmp4, x2, powers_of(pw[1], m, 1, 1), ALU.mult))
                link(tt(o, x1, powers_of(pw[0], m, 1, 1), ALU.mult))
                tt(o, o, tmp4, ALU.add).then_inc(s.m_built, 1)

            def state(m):
                pool.wait_ge(s.p_sw, 2 * (m + 1))
                nc.gpsimd.tensor_tensor(h[:, m % 2, :], p1[:], h[:, m % 2, :], ALU.add).then_inc(s.h, 1)

            def phases():
                tt, ts = nc.gpsimd.tensor_tensor, nc.gpsimd.tensor_scalar
                A, B = [view(Y, 6 * T + i * T, [[G, 4], [1, G]]) for i in range(2)]
                def unit(t):
                    re, im, a_, b_ = t[0][:, 1, :], t[1][:, 1, :], A[:, 0, :], B[:, 0, :]
                    link(tt(a_, re, re, ALU.mult))
                    link(tt(b_, im, im, ALU.mult))
                    link(tt(a_, a_, b_, ALU.add))
                    link(ts(a_, a_, -0.5, 1.5, ALU.mult, ALU.add))
                    link(tt(re, re, a_, ALU.mult))
                    link(tt(im, im, a_, ALU.mult))

                pool.wait_ge(s.summed, KT)
                pool.wait_ge(s.x_T, KT)
                pool.wait_ge(s.cosine, 1)
                pool.wait_ge(s.cst_in, 16)
                for t in (gt, ft):
                    link(nc.gpsimd.memset(t[0][:, 0, :], 1.0))
                    link(nc.gpsimd.memset(t[1][:, 0, :], 0.0))
                link(ts(gt[0][:, 1, :], pt(CO_), 1.0, 0.0, ALU.mult, ALU.add))
                link(ts(gt[1][:, 1, :], pt(SN_), cst[:, C_SGN:C_SGN + 1], 0.0, ALU.mult, ALU.add))
                for _ in range(3):
                    cmul(tt, link, A, B, gt, 2, 1, 1, 1)
                    for t in gt:
                        link(ts(t[:, 1, :], t[:, 2, :], 1.0, 0.0, ALU.mult, ALU.add))
                unit(gt)
                powers(tt, link, A, B, gt)
                for i in range(2):
                    link(ts(ft[i][:, 1, :], gt[i][:, CH, :], 1.0, 0.0, ALU.mult, ALU.add))
                unit(ft)
                powers(tt, link, A, B, ft)
                nc.gpsimd.memset(view(w1, 0, [[1, T]]), 0.0).then_inc(s.phases, 1)

            phases_at = 4
            before = {7: [(build_m, 0)], 8: [(state, 0)]}
            for m in range(KT - 3):
                before[2 * m + 9] = [(build_m, m + 1)]
                before[2 * m + 10] = [(state, m + 1)]
            before[S_GLU + 2] = [(state, KT - 3), (build_m, KT - 2), (state, KT - 2), (build_m, KT - 1),
                                 (state, KT - 1)]
            for S in range(S_END):
                if S == phases_at:
                    phases()
                for part, m in before.get(S, ()):
                    part(m)
                split(S)

        @block.tensor
        def _(pe):
            mm = nc.tensor.matmul

            def exact(dst, wh, wl, xh, xl, first, last):
                mm(dst, wh, xh, start=first, stop=False)
                mm(dst, wh, xl, start=False, stop=False)
                return mm(dst, wl, xh, start=False, stop=last)

            def dense(S, xh, xl, b, ready, before=0, beside=None):
                pe.wait_ge(s.w_split, S + 1)
                for k in range(KT):
                    for r in ready:
                        pe.wait_ge(r, before + k + 1)
                    c = slice(k * P, (k + 1) * P)
                    last = exact(ps(b), whi[S % RING][:, c], wlo[S % RING][:, c], xh[:, k, :], xl[:, k, :],
                                 k == 0, k == KT - 1)
                    if k == KT - 1:
                        last.then_inc(s.w_used, 1)
                    if beside:
                        beside(k)

            def turn(b, src, np_=P, n=P, o=0):
                return nc.tensor.transpose(bk[b][0:n, o:o + np_], src, ident[0:np_, 0:np_])

            def sum_squares(b, sq, k, done, before=0):
                pe.wait_ge(done, before + k + 1)
                mm(ps(b), cst[:, C_ONE:C_ONE + P], sq, start=k == 0, stop=k == KT - 1).then_inc(s.summed, 1)

            def square_sum(b, t, n):
                pe.wait_ge(s.acc, n)
                mm(ps(b), cst[:, C_ONE:C_ONE + P], t[:], start=True, stop=True).then_inc(s.summed, 1)

            pe.wait_ge(s.cst_in, 16)
            pe.wait_ge(s.ag_in, 16)
            turn(4, view(yT, 2 * P, [[1, P]], np_=KT), np_=KT, o=3 * P).then_inc(s.ag_T, 1)
            for k in range(KT + 2):
                if k < KT:
                    after(pe, s.x_copied, k - 3)
                    if k == 0:
                        pe.wait_ge(s.x_in, 32 * QB)
                    for j in range(QB):
                        last = turn(k % 4, xrow[:, j * D + k * P:j * D + (k + 1) * P], o=j * P)
                    last.then_inc(s.x_T, 1)
                if k >= 2:
                    sum_squares(7, (w1, w2)[k % 2][:], k - 2, s.x_sq)

            pe.wait_ge(s.par_in, 16 * N_PAR)
            pe.wait_ge(s.ag, 1)
            turn(4, view(yT, 0, [[1, P]], np_=G), np_=G)
            turn(4, view(yT, P, [[1, P]], np_=G), np_=G, o=ST)
            turn(4, view(yT, 2 * P, [[1, P]], np_=V_ROWS), np_=V_ROWS, o=P).then_inc(s.par_T, 1)
            after(pe, s.x_copied, KT)
            dense(SLAB_OF["u", 0], hi0, lo0, 0, (s.x_hi, s.x_lo))
            pe.wait_ge(s.c_in, 32)
            for k in range(KT):
                last = turn(5 + k // 4, view(M, k * P, [[1, P]]), o=(k % 4) * P)
            last.then_inc(s.c_T, 1)
            pe.wait_ge(s.b_in, 32)
            for i in range(2):
                last = mm(ps(2 + i), cst[:, C_J1:C_J1 + P], view(XB1, i * T, [[1, T]]), start=True, stop=True)
            last.then_inc(s.xb2_mm, 1)
            dense(SLAB_OF["u", 1], hi0, lo0, 1, ())
            pe.wait_ge(s.xc1, 2)
            for i in range(2):
                last = mm(ps(5 + i), cst[:, C_J2:C_J2 + P], view(XC1, i * T, [[1, T]]), start=True, stop=True)
            last.then_inc(s.xc2_mm, 1)
            pe.wait_ge(s.u_ev, 1)
            dense(SLAB_OF["u", 2], hi0, lo0, 0, ())
            pe.wait_ge(s.xb1, 2)
            pe.wait_ge(s.xc2, 2)
            for i in range(2):
                last = mm(ps(5 + i), cst[:, C_J1:C_J1 + P], view(XB1, i * T, [[1, T]]), start=True, stop=True)
            last.then_inc(s.xb2_mm, 1)

            pe.wait_ge(s.u_ev, 2)
            dense(SLAB_OF["z", 0], hi0, lo0, 1, ())
            pe.wait_ge(s.par_read, 1)
            pe.wait_ge(s.hot, 1)
            mm(bk[4][0:H, 0:T], small[0:BUCKETS + 1, 8:16], cst[0:BUCKETS + 1, C_HOT:C_HOT + T],
               start=True, stop=True)
            pe.wait_ge(s.r_ln, 1)
            mm(bk[7][0:H, 0:REV - T], small[0:BUCKETS + 1, 8:16], cst[0:BUCKETS + 1, C_HOT + T:C_HOT + REV],
               start=True, stop=True).then_inc(s.rows_mm, 1)

            def turn_weights(m):
                pe.wait_ge(s.p_built, m + 1)
                after(pe, s.win, 2 * m)
                for g in range(GT):
                    last = turn(2 + g // 4, view(Pp, g * PADJ * GC, [[1, P]]), o=(g % 4) * P)
                last.then_inc(s.p_T, 1)

            def t_ready(m):
                after(pe, s.t_built, T_COPIES * m)

            def ssm_t(m, g):
                for i in range(2):
                    last = mm(ps(4, GC, (2 * g + i) * GC), view(Pp, g * PADJ * GC + (1 - i) * GC, [[1, P]]),
                              XC1[:, m * GT + g, :], start=True, stop=True)
                if g == GT - 1:
                    last.then_inc(s.t_mm, 1)

            def in_ready(m):
                pe.wait_ge(s.win, 2 * (m + 1))
                pe.wait_ge(u_in[m % 4], 16 * CH * (m // 4 + 1))
                after(pe, s.rot, m - 1)

            def ssm_in(m, g):
                last = mm(ps(5 + m % 2, NC, g * NC), Win[:, g, :], U[:, m % 4, g, :], start=True, stop=True)
                if g == GT - 1:
                    last.then_inc(s.ssm_w, 1)

            def ssm_out(m):
                pe.wait_ge(s.h, m + 1)
                pe.wait_ge(s.t_built, T_COPIES * (m + 1))
                pe.wait_ge(s.m_built, m + 1)
                after(pe, s.y_ev, m)
                for g in range(GT):
                    o = ps(7, NC, g * NC)
                    mm(o, view(TT, (m % 2) * D + g * P, [[1, P]]), U[:, m % 4, g, :], start=True, stop=False)
                    last = mm(o, view(M, (m % 2) * D + g * P, [[1, P]]), h[:, m % 2, g * NC:(g + 1) * NC],
                              start=False, stop=True)
                last.then_inc(s.ssm_y, 1)

            def project_in(S, beside=None):
                kind, m = IN_ORDER[S - 2]
                pe.wait_ge(s.u_ev if kind == "u" else s.z_ev, m + 1)
                dense(S, hi0, lo0, S % 2, (), beside=beside)

            turn_weights(0)
            pe.wait_ge(s.rows_ev, 2)
            for g in range(GT):
                ssm_t(0, g)
            turn_weights(1)
            in_ready(0)
            for g in range(GT):
                ssm_in(0, g)
            for m in range(KT):
                if m >= 1:
                    ssm_out(m - 1)
                for i, (part, ready) in enumerate(((ssm_t, t_ready), (ssm_in, in_ready))):
                    if m + 1 < KT:
                        ready(m + 1)
                    beside = (lambda g, part=part: part(m + 1, g)) if m + 1 < KT else None
                    if m + 3 < KT:
                        project_in(2 * m + 4 + i, beside)
                    elif beside:
                        for g in range(GT):
                            beside(g)
                if m + 2 < KT:
                    turn_weights(m + 2)
            project_in(S_GLU - 2)
            ssm_out(KT - 1)
            project_in(S_GLU - 1)

            def turn_p(rows, src, arrived, b):
                pe.wait_ge(arrived, rows)
                if arrived is s.p2_in:
                    pe.wait_ge(s.h_ev, len(HEAD_ORDER) - 1)
                    pe.wait_ge(s.v_lo, H)
                for k in range(PK):
                    for j in range(QB):
                        last = turn(b[k], src[:, j, k * P:(k + 1) * P], o=j * P)
                last.then_inc(s.pT, 1)

            for m in range(KT):
                if m < 2:
                    pe.wait_ge(s.z_ev, KT)
                else:
                    pe.wait_ge(s.glu_tanh, m - 1)
                    pe.wait_ge(s.glu_y, m - 1)
                dense(S_GLU + 2 * m, hi0, lo0, 2 * (m % 2), (s.y_hi, s.y_lo) if m == 0 else ())
                dense(S_GLU + 2 * m + 1, hi0, lo0, 2 * (m % 2) + 1, ())
                if m == 3:
                    turn_p(16 * 8, prow, s.p_in, (4, 5))

            def project(S, ph, pl, b, n):
                pe.wait_ge(s.w_split, S + 1)
                pe.wait_ge(s.p_hi, n)
                pe.wait_ge(s.p_lo, n)
                for o in range(4):
                    for k in range(PK):
                        c = slice(k * T + o * P, k * T + (o + 1) * P)
                        last = exact(ps(b + o), whi[S % RING][:, c], wlo[S % RING][:, c], ph[:, k, :],
                                     pl[:, k, :], k == 0, k == PK - 1)
                last.then_inc(s.w_used, 1)

            project(S_P0, phi, plo, 4, PK)
            pe.wait_ge(s.glu_tanh, KT)
            pe.wait_ge(s.glu_y, KT)
            project(S_P0 + 1, phi, plo, 0, PK)

            for m in range(KT):
                if m < 2:
                    pe.wait_ge(s.pr_ev, 4)
                else:
                    pe.wait_ge(s.xa, m - 1)
                dense(S_OUT + m, hi1, lo1, 4 + m % 2, (s.glu_hi, s.glu_lo) if m == 0 else ())
            for m in range(KT):
                pe.wait_ge(*((s.xa, KT - 1 + m) if m < 2 else (s.g_ev, m - 1)))
                dense(S_G0 + m, hi0, lo0, 4 + m % 2, (s.xa_hi, s.xa_lo) if m == 0 else ())
                if m == 0:
                    square_sum(6, acc, KT - 1)
            def project_head(e):
                kind, m = HEAD_ORDER[e]
                if e == 0:
                    pe.wait_ge(s.pr_ev, KT)
                else:
                    after(pe, s.h_ev, e - 1)
                xh, xl = (hi1, lo1) if kind in "kv" else (hi2, lo2)
                ready = (s.n1_hi, s.n1_lo) if e == 0 else (s.n2_hi, s.n2_lo) if e == 1 else ()
                dense(S_H + e, xh, xl, e % 2, ready)
                if e == 0:
                    square_sum(6, acc, 2 * (KT - 1))

            def after_project(e):
                kind, m = HEAD_ORDER[e]
                if kind == "z":
                    return
                if e > 0:
                    last_kind, n = [x for x in HEAD_ORDER[:e] if x[0] != "z"][-1]
                    if last_kind == "v":
                        pe.wait_ge(s.v_lo, n + 1)
                    else:
                        pe.wait_ge(s.k_ln, 2 * n + (last_kind == "q") + 1)
                if kind == "v":
                    pe.wait_ge(s.h_ev, e + 1)
                    for j in range(QB):
                        last = turn(7, ta[0][:, e % 2, j * P:(j + 1) * P], o=j * P)
                    last.then_inc(s.v_T, 1)
                else:
                    pe.wait_ge(s.k_sq, 2 * m + (kind == "q") + 1)
                    mm(ps(7), cst[:, C_BLK:C_BLK + P], ta[1][:, e % 2, :], start=True,
                       stop=True).then_inc(s.k_bs, 1)

            def scores(j):
                m, I = divmod(j, QB)
                if I == 0:
                    pe.wait_ge(s.k_lo, 2 * m + 2)
                for c in range(2):
                    n = 2 * j + c
                    after(pe, s.sc_read, n - 1)
                    r = slice(c * HD, (c + 1) * HD)
                    q = slice(I * P, (I + 1) * P)
                    w = (I + 1) * P
                    exact(ps(2 + c, w), qh[r, m % 2, q], ql[r, m % 2, q], kh[r, m % 2, 0:w], kl[r, m % 2, 0:w],
                          True, True).then_inc(s.sc, 1)

            def apply(j):
                m, I = divmod(j, QB)
                pe.wait_ge(s.soft, j + 1)
                after(pe, s.at_lo, j)
                for t in range(I + 1):
                    last = turn(4, sco[0][:, j % 2, t * P:(t + 1) * P], o=t * P)
                last.then_inc(s.at, 1)

            def values(j):
                m, I = divmod(j, QB)
                pe.wait_ge(s.at_lo, j + 1)
                if I == 0:
                    after(pe, s.o_ev, m - 1)
                    pe.wait_ge(s.v_lo, m + 1)
                for t in range(I + 1):
                    last = exact(ps(5 + m % 2, P, I * P), ath[:, j % 2, t * P:(t + 1) * P],
                                 atl[:, j % 2, t * P:(t + 1) * P], vh[:, m % 2, t * P:(t + 1) * P],
                                 vl[:, m % 2, t * P:(t + 1) * P], t == 0, t == I)
                last.then_inc(s.pv, 1)

            def turn_o(m):
                pe.wait_ge(s.on, m + 1)
                for I in range(QB):
                    last = turn(5 + m % 2, on[:, I * P:(I + 1) * P], o=I * P)
                last.then_inc(s.o_T, 1)

            def project_p2(i):
                S = S_P1 + i
                pe.wait_ge(s.w_split, S + 1)
                pe.wait_ge(s.p_hi, 2 * PK)
                pe.wait_ge(s.p_lo, 2 * PK)
                pe.wait_ge(s.h_ev, len(HEAD_ORDER))
                for o in range(4):
                    after(pe, s.pr2_ev, 4 * i + o - 1)
                    for k in range(PK):
                        c = slice(k * T + o * P, k * T + (o + 1) * P)
                        last = exact(ps(o % 2), whi[S % RING][:, c], wlo[S % RING][:, c], phi2[:, k, :],
                                     plo2[:, k, :], k == 0, k == PK - 1)
                    last.then_inc(*((s.w_used, 1) if o == 3 else (s.pr2_mm, 1)))

            steps = H * QB
            slabs_h = len(HEAD_ORDER)
            for e in range(LEAD + steps + 2):
                j = e - LEAD
                if e < slabs_h:
                    project_head(e)
                elif e - slabs_h in (1, 2):
                    project_p2(e - slabs_h - 1)
                if 1 <= e <= slabs_h:
                    after_project(e - 1)
                if e == slabs_h - 1:
                    turn_p(16, prow2, s.p2_in, (0, 7))
                if 0 <= j + 1 < steps:
                    scores(j + 1)
                if 0 <= j < steps:
                    apply(j)
                if 1 <= j <= steps:
                    values(j - 1)
                if j >= QB + 1 and (j - 1) % QB == 0:
                    turn_o((j - 1) // QB - 1)

            for m in range(KT):
                if m >= 2:
                    pe.wait_ge(s.xa, KT + m - 1)
                else:
                    pe.wait_ge(*((s.at_lo, steps) if m == 0 else (s.o_ev, H)))
                dense(S_BO + m, hi0, lo0, 4 + m % 2, (s.o_hi, s.o_lo) if m == 0 else ())
            for m in range(KT + 1):
                if m < KT:
                    pe.wait_ge(*((s.xa, 2 * KT - 1 + m) if m < 2 else (s.g_ev, KT + m - 1)))
                    dense(S_G1 + m, hi1, lo1, 4 + m % 2, (s.xa_hi, s.xa_lo) if m == 0 else (), KT)
                    if m == 0:
                        square_sum(6, acc2, 3 * (KT - 1))
                if m >= 1:
                    pe.wait_ge(s.x2, m)
                    if m >= 3:
                        pe.wait_ge(s.out_ev, m - 2)
                    else:
                        pe.wait_ge(s.pr2_ev, KT)
                    for j in range(QB):
                        last = turn((m - 1) % 2, tc[2][:, (m - 1) % 2, j * P:(j + 1) * P], o=j * P)
                    last.then_inc(s.out_T, 1)

        @block.scalar
        def _(act):
            fn = nc.scalar.activation
            act.wait_ge(s.ag, 1)
            for k in range(KT + 1):
                if k < KT:
                    act.wait_ge(s.x_T, k + 1)
                    fn(cols(hi0, k), ps(k % 4), ACT.Identity, scale=again[:, k:k + 1]).then_inc(s.x_hi, 1)
                if k >= 1:
                    act.wait_ge(s.x_copied, k)
                    after(act, s.summed, k - 2)
                    fn((w1, w2)[(k - 1) % 2][:], uT[:, (k - 1) % 4, :], ACT.Square).then_inc(s.x_sq, 1)
            act.wait_ge(s.par_in, 16 * N_PAR)
            fn(pt(DT_), view(yT, 384, [[1, G]]), ACT.Exp).then_inc(s.dt, 1)
            act.wait_ge(s.xr, 1)
            fn(pt(MG_), pt(XR_), ACT.Exp).then_inc(s.mag, 1)
            def inverse_rms(n, b, version):
                act.wait_ge(s.summed, n)
                fn(R[:], ps(b), ACT.Ln, scale=1.0 / D, bias=epsc).then_inc(s.r_ln, 1)
                act.wait_ge(s.r_ln, version)
                fn(R[:], R[:], ACT.Exp, scale=-0.5).then_inc(s.r_norm, 1)

            act.wait_ge(s.zeroed, 4)
            inverse_rms(KT, 7, 1)
            act.wait_ge(s.rr, 1)
            fn(pt(SN_), pt(RR_), ACT.Sin).then_inc(s.sin, 1)
            fn(pt(SH_), pt(RR_), ACT.Sin, scale=0.5).then_inc(s.sin, 1)
            act.wait_ge(s.xc2_mm, 1)
            for i in range(2):
                fn(view(XC2, i * T, [[1, T]]), ps(5 + i), ACT.Copy).then_inc(s.xc2, 1)
            act.wait_ge(s.xb2_mm, 2)
            for i in range(2):
                fn(view(XB2, i * T, [[1, T]]), ps(5 + i), ACT.Copy).then_inc(s.xb2, 1)
            act.wait_ge(s.lam_dot, 2)
            fn(small[:, 4:6], small[:, 2:4], ACT.Exp).then_inc(s.lam_e, 1)
            act.wait_ge(s.rows_mm, 1)
            fn(p1[0:H, :], bk[4][0:H, 0:T], ACT.Copy).then_inc(s.rows_ev, 1)
            fn(p2[0:H, 0:REV - T], bk[7][0:H, 0:REV - T], ACT.Copy).then_inc(s.rows_ev, 1)
            
            def scan_ratio(m):
                if m == 0:
                    act.wait_ge(s.r8, 1)
                after(act, s.scan, m)
                fn(view(r8x, 1, [[NC, GT], [1, NC - 1]]), view(r8, m * GT, [[1, GT], [0, NC - 1]]),
                   ACT.Copy).then_inc(s.ratio, 1)

            def input_weights(m):
                act.wait_ge(s.p_T, m + 1)
                after(act, s.ssm_w, m)
                for i in range(2):
                    fn(Win[:, 4 * i:4 * i + 4, :], ps(2 + i).rearrange("p (g s) -> p g s", g=4),
                       ACT.Copy).then_inc(s.win, 1)

            def copy_t(m):
                act.wait_ge(s.t_mm, m + 1)
                after(act, s.ssm_y, m - 1)
                for src, n, dst in T_MOVES:
                    t0 = CH - 2 - 2 * ((src - dst) // 32)
                    fn(view(TT, (m % 2) * D + t0 * GC, [[P, GT], [1, 2 * GC]], p0=dst, np_=n),
                       bass.AP(bk[4], src * T, [[T, n], [2 * GC, GT], [1, 2 * GC]]), ACT.Copy).then_inc(s.t_built, 1)

            def exchange_w(m):
                act.wait_ge(s.ssm_w, m + 1)
                after(act, s.rot, m)
                for i in range(2):
                    fn(w2[ST * i:ST * (i + 1), :], bk[5 + m % 2][ST * (1 - i):ST * (2 - i), :],
                       ACT.Copy).then_inc(s.w_sw, 1)

            def exchange_p(m):
                act.wait_ge(s.p_rot, m + 1)
                after(act, s.ssm_y, m - 1)
                for i in range(2):
                    fn(h[ST * i:ST * (i + 1), m % 2, :], p2[ST * (1 - i):ST * (2 - i), :], ACT.Copy).then_inc(s.p_sw, 1)

            def gate(m):
                act.wait_ge(s.z_ev, m + 1)
                after(act, s.zz, m)
                fn(tz[:], st[:, m % 2, :], ACT.Tanh, scale=0.5).then_inc(s.z_tanh, 1)

            def gelu(m):
                act.wait_ge(s.comb, m + 1)
                fn(Y[:, m, :], yT[:, m % 2, :], ACT.Gelu_apprx_tanh).then_inc(s.gelu, 1)

            act.wait_ge(s.zeroed, 4)
            scan_ratio(0)
            input_weights(0)
            copy_t(0)
            exchange_w(0)
            for m in range(KT + 1):
                if 1 <= m < KT:
                    exchange_w(m)
                if m + 1 < KT:
                    input_weights(m + 1)
                if m >= 1:
                    act.wait_ge(s.ssm_y, m)
                    if m >= 3:
                        act.wait_ge(s.y_out, 16 * (m - 2))
                    fn(ysb[:, (m - 1) % 2, :], ps(7), ACT.Copy).then_inc(s.y_ev, 1)
                if m < KT:
                    exchange_p(m)
                if m < KT - 2:
                    gate(m)
                if m + 1 < KT:
                    scan_ratio(m + 1)
                    copy_t(m + 1)
                if 1 <= m < KT:
                    if m == KT - 1:
                        act.wait_ge(s.m_built, KT)
                    gelu(m - 1)
            gate(KT - 2)
            gate(KT - 1)
            act.wait_ge(s.w_used, S_GLU)
            for k in range(KT):
                if k == KT - 1:
                    gelu(k)
                act.wait_ge(s.gelu, k + 1)
                fn(cols(hi0, k), cols(Y, k), ACT.Copy).then_inc(s.y_hi, 1)

            def split_p(ph, psb):
                for k in range(PK):
                    fn(ph[:, k, :], ps(psb[k]), ACT.Copy).then_inc(s.p_hi, 1)

            for m in range(KT + 1):
                if m < KT:
                    act.wait_ge(s.w_used, S_GLU + 2 * m + 1)
                    after(act, s.glu_y, m - 1)
                    if m == 0:
                        act.wait_ge(s.y_lo, KT)
                    fn(tb[1][:, m % 2, :], ps(2 * (m % 2)), ACT.Tanh, scale=0.5).then_inc(s.glu_tanh, 1)
                if m >= 1:
                    act.wait_ge(s.glu_y3, m)
                    fn(cols(hi1, m - 1), tb[2][:, (m - 1) % 2, :], ACT.Copy).then_inc(s.glu_hi, 1)
                if m == 4:
                    act.wait_ge(s.pT, 1)
                    split_p(phi, (4, 5))
            for i in range(2):
                act.wait_ge(s.w_used, S_P0 + i + 1)
                for o in range(4):
                    fn(cols(zz, 4 * i + o), ps(4 * (1 - i) + o), ACT.Copy).then_inc(s.pr_ev, 1)
            for m in range(KT):
                act.wait_ge(s.xa, m + 1)
                fn(cols(hi0, m), cols(xT, m), ACT.Copy).then_inc(s.xa_hi, 1)
                if m >= 3:
                    act.wait_ge(s.acc, m - 2)
                fn(acc[:] if m == 0 else tb[3][:, m % 2, :], cols(xT, m), ACT.Square).then_inc(s.xa_sq, 1)
            inverse_rms(KT + 1, 6, 2)
            for m in range(KT):
                act.wait_ge(s.g_ev, m + 1)
                after(act, s.g_pr, m - 1)
                fn(tb[1][:, m % 2, :], tb[0][:, m % 2, :], ACT.Tanh, scale=0.5).then_inc(s.g_tanh, 1)
                act.wait_ge(s.x1, m + 1)
                fn(cols(hi1, m), tb[2][:, m % 2, :], ACT.Identity, scale=vcol(V_KVG + m)).then_inc(s.n1_hi, 1)
                fn(cols(hi2, m), tb[2][:, m % 2, :], ACT.Identity, scale=vcol(V_BG + m)).then_inc(s.n2_hi, 1)
                if m == 0:
                    act.wait_ge(s.summed, KT + 1)
                if m >= 3:
                    act.wait_ge(s.acc, KT - 1 + m - 2)
                fn(acc[:] if m == 0 else tb[3][:, m % 2, :], tb[2][:, m % 2, :], ACT.Square).then_inc(s.x1_sq, 1)
            inverse_rms(KT + 2, 6, 3)

            def project_first(e):
                kind, m = HEAD_ORDER[e]
                if kind == "v":
                    return
                act.wait_ge(s.h_ev, e + 1)
                for last_kind, n in [x for x in HEAD_ORDER[e % 2:e:2] if x[0] != "v"][-1:]:
                    if last_kind == "z":
                        act.wait_ge(s.sz, n + 1)
                    else:
                        act.wait_ge(s.k_n, 2 * n + (last_kind == "q") + 1)
                if kind == "z":
                    fn(ta[1][:, e % 2, :], ta[0][:, e % 2, :], ACT.Tanh, scale=0.5).then_inc(s.b_tanh, 1)
                else:
                    fn(ta[1][:, e % 2, :], ta[0][:, e % 2, :], ACT.Square).then_inc(s.k_sq, 1)

            def project_second(e):
                kind, m = HEAD_ORDER[e]
                n = 2 * m + (kind == "q")
                if kind in "kq":
                    act.wait_ge(s.k_bs, n + 1)
                    t = ta[1][:, e % 2, :]
                    fn(t, ps(7), ACT.Ln, scale=1.0 / HD, bias=epsc).then_inc(s.k_ln, 1)
                    act.wait_ge(s.k_ln, n + 1)
                    fn(t, t, ACT.Exp, scale=-0.5).then_inc(s.k_r, 1)
                elif kind == "v":
                    act.wait_ge(s.v_T, m + 1)
                    after(act, s.pv, QB * (m - 1))
                    fn(vh[:, m % 2, :], ps(7), ACT.Copy).then_inc(s.v_hi, 1)

            def project_hi(e):
                kind, m = HEAD_ORDER[e]
                if kind in "kq":
                    act.wait_ge(s.k_n, 2 * m + (kind == "q") + 1)
                    after(act, s.sc, 2 * QB * (m - 1))
                    fn((kh if kind == "k" else qh)[:, m % 2, :], ta[2][:, e % 2, :], ACT.Copy).then_inc(s.k_hi, 1)

            def exps(j):
                w = (j % QB + 1) * P
                act.wait_ge(s.neg, j + 1)
                for c in range(2):
                    e = sco[c][:, j % 2, 0:w]
                    fn(e, e, ACT.Exp, bias=stat[:, j % 2, 4 + c:5 + c],
                       accum_out=stat[:, j % 2, 6 + c:7 + c]).then_inc(s.exp, 1)

            def at_hi(j):
                w = (j % QB + 1) * P
                act.wait_ge(s.at, j + 1)
                after(act, s.pv, j - 1)
                fn(ath[:, j % 2, 0:w], ps(4, w), ACT.Copy).then_inc(s.at_hi, 1)

            def o_norm(m):
                act.wait_ge(s.pv, QB * (m + 1))
                after(act, s.o_lo, m)
                for I in range(QB):
                    fn(on[:, I * P:(I + 1) * P], ps(5 + m % 2, P, I * P), ACT.Square,
                       accum_out=oss[:, I:I + 1]).then_inc(s.o_sq, 1)
                act.wait_ge(s.o_sq, QB * (m + 1))
                fn(oss[:, 4:8], oss[:, 0:4], ACT.Ln, scale=1.0 / P, bias=epsc).then_inc(s.o_ln, 1)
                act.wait_ge(s.o_ln, m + 1)
                fn(oss[:, 8:12], oss[:, 4:8], ACT.Exp, scale=-0.5).then_inc(s.o_r, 1)

            def o_hi(m):
                act.wait_ge(s.o_ev, m + 1)
                fn(cols(hi0, m), on[:], ACT.Copy).then_inc(s.o_hi, 1)

            steps = H * QB
            slabs_h = len(HEAD_ORDER)
            for e in range(LEAD + steps + 3):
                j = e - LEAD
                if 1 <= e <= slabs_h:
                    project_first(e - 1)
                if 2 <= e <= slabs_h + 1:
                    project_second(e - 2)
                if 0 <= j < steps:
                    exps(j)
                if 2 <= e <= slabs_h + 1:
                    project_hi(e - 2)
                if e == slabs_h:
                    act.wait_ge(s.pT, 2)
                    split_p(phi2, (0, 7))
                if 1 <= j <= steps:
                    at_hi(j - 1)
                if e - slabs_h in (1, 2):
                    i = e - slabs_h - 1
                    for o in range(4):
                        act.wait_ge(*((s.w_used, S_P1 + i + 1) if o == 3 else (s.pr2_mm, 3 * i + o + 1)))
                        fn(cols(pr2, 4 * i + o), ps(o % 2), ACT.Copy).then_inc(s.pr2_ev, 1)
                if j >= QB + 1 and (j - 1) % QB == 0:
                    o_norm((j - 1) // QB - 1)
                if j >= QB + 2 and (j - 2) % QB == 0:
                    o_hi((j - 2) // QB - 1)

            for m in range(KT):
                act.wait_ge(s.xa, KT + m + 1)
                fn(cols(hi1, m), cols(x1b, m), ACT.Copy).then_inc(s.xa_hi, 1)
                if m >= 3:
                    act.wait_ge(s.acc, 2 * (KT - 1) + m - 2)
                fn(acc2[:] if m == 0 else tc[3][:, m % 2, :], cols(x1b, m), ACT.Square).then_inc(s.xa_sq, 1)
            inverse_rms(KT + 3, 6, 4)
            for m in range(KT + 1):
                if m < KT:
                    act.wait_ge(s.g_ev, KT + m + 1)
                    after(act, s.g_pr, KT + m - 1)
                    fn(tc[1][:, m % 2, :], tc[0][:, m % 2, :], ACT.Tanh, scale=0.5).then_inc(s.g_tanh, 1)
                if m >= 1:
                    n = m - 1
                    act.wait_ge(s.out_T, n + 1)
                    if n >= 2:
                        act.wait_ge(o_out[n % 2], 16 * (n // 2))
                    fn(tc[3][:, n % 2, :], ps(n % 2), ACT.Copy).then_inc(s.out_ev, 1)

        @block.vector
        def _(dve):
            v = nc.vector
            tt, ts, stt, cp = v.tensor_tensor, v.tensor_scalar, v.scalar_tensor_tensor, v.tensor_copy
            MUL, ADD, SUB = ALU.mult, ALU.add, ALU.subtract
            steps_done = [0]

            def link(ins):
                steps_done[0] += 1
                ins.then_inc(s.dve_step, 1)
                dve.wait_ge(s.dve_step, steps_done[0])

            dve.wait_ge(s.ag_T, 1)
            cp(again, bk[4][:, 3 * P:3 * P + KT]).then_inc(s.ag, 1)
            dve.wait_ge(s.ag, 1)
            for k in range(KT):
                dve.wait_ge(s.x_hi, k + 1)
                if k >= 4:
                    dve.wait_ge(xs_out[k % 4], 16)
                    dve.wait_ge(s.x_sq, k - 3)
                cp(uT[:, k % 4, :], ps(k % 4)).then_inc(s.x_copied, 1)
                dve.wait_ge(s.x_copied, k + 1)
                stt(out=cols(lo0, k), in0=uT[:, k % 4, :], scalar=again[:, k:k + 1], in1=cols(hi0, k).bitcast(F32),
                    op0=MUL, op1=SUB).then_inc(s.x_lo, 1)

            dve.wait_ge(s.par_T, 1)
            link(cp(pt(LR_), bk[4][:, 0:ST]))
            link(cp(pt(LI_), bk[4][:, ST:P]))
            cp(VT[:], bk[4][:, P:P + V_ROWS]).then_inc(s.par_read, 1)
            dve.wait_ge(s.par_read, 1)
            link(ts(vcol(V_QG), vcol(V_QG), HD ** -0.5, None, MUL))
            link(ts(vcol(V_SUB), vcol(V_SUB), 0.5 * (1 - LAM_INIT), None, MUL))
            dve.wait_ge(s.dt, 1)
            tt(pt(XR_), pt(LR_), pt(DT_), MUL).then_inc(s.xr, 1)
            link(tt(pt(TH_), pt(LI_), pt(DT_), MUL))
            link(ts(pt(KQ_), pt(TH_), 1 / TWO_PI, MAGIC, MUL, ADD))
            link(ts(pt(KQ_), pt(KQ_), -MAGIC, None, ADD))
            link(stt(out=pt(RR_), in0=pt(KQ_), scalar=-PI_A, in1=pt(TH_), op0=MUL, op1=ADD))
            link(stt(out=pt(RR_), in0=pt(KQ_), scalar=-PI_B, in1=pt(RR_), op0=MUL, op1=ADD))
            link(stt(out=pt(RR_), in0=pt(KQ_), scalar=-PI_C, in1=pt(RR_), op0=MUL, op1=ADD))
            ts(pt(RR_), pt(RR_), 3.1415925, -3.1415925, ALU.min, ALU.max).then_inc(s.rr, 1)
            dve.wait_ge(s.c_T, 1)
            dve.wait_ge(s.cst_in, 16)
            sgn = cst[:, C_SGN:C_SGN + 1]
            for h in range(2):
                ts(view(XC1, h * T, [[1, T]]), ps(5 + h), sgn, None, MUL).then_inc(s.xc1, 1)
            dve.wait_ge(s.lamv_in, 64)
            for i in range(2):
                v.tensor_tensor_reduce(view(tmp, i * 64, [[1, 64]]), lam_v[:, 2 * i, :], lam_v[:, 2 * i + 1, :],
                                       1.0, 0.0, MUL, ADD, small[:, 2 + i:3 + i]).then_inc(s.lam_dot, 1)
            dve.wait_ge(s.hot_in, 16)
            v.memset(small[BUCKETS:BUCKETS + 1, 8:16], NEG).then_inc(s.hot, 1)

            def u_out(m):
                S = SLAB_OF["u", m]
                dve.wait_ge(s.w_used, S + 1)
                if m < 4:
                    dve.wait_ge(xs_out[m], 32)
                else:
                    dve.wait_ge(s.comb, m - 3)
                tt(uT[:, m % 4, :], ps(S % 2), R[:], MUL).then_inc(s.u_ev, 1)

            dve.wait_ge(s.r_norm, 1)
            u_out(0)
            dve.wait_ge(s.sin, 2)
            dve.wait_ge(s.mag, 1)
            link(tt(pt(CO_), pt(SH_), pt(SH_), MUL))
            ts(pt(CO_), pt(CO_), -2.0, 1.0, MUL, ADD).then_inc(s.cosine, 1)
            dve.wait_ge(s.cosine, 1)
            re, im = pw
            link(v.memset(re[:, 0, :], 1.0))
            link(v.memset(im[:, 0, :], 0.0))
            link(tt(re[:, 1, :], pt(MG_), pt(CO_), MUL))
            link(tt(im[:, 1, :], pt(MG_), pt(SN_), MUL))
            link(ts(pt(T1_), re[:, 1, :], -1.0, None, ADD))
            link(tt(pt(DN_), pt(LR_), pt(LR_), MUL))
            link(tt(pt(T2_), pt(LI_), pt(LI_), MUL))
            link(tt(pt(DN_), pt(DN_), pt(T2_), ADD))
            link(v.reciprocal(pt(DN_), pt(DN_)))
            link(tt(pt(FR_), pt(T1_), pt(LR_), MUL))
            link(tt(pt(T2_), im[:, 1, :], pt(LI_), MUL))
            link(tt(pt(FR_), pt(FR_), pt(T2_), ADD))
            link(tt(pt(FR_), pt(FR_), pt(DN_), MUL))
            link(tt(pt(FI_), im[:, 1, :], pt(LR_), MUL))
            link(tt(pt(T2_), pt(T1_), pt(LI_), MUL))
            link(tt(pt(FI_), pt(FI_), pt(T2_), SUB))
            link(tt(pt(FI_), pt(FI_), pt(DN_), MUL))

            powers(tt, link, view(tmp, 0, [[G, 4], [1, G]]), view(tmp, 4 * G, [[G, 4], [1, G]]), pw)
            u_out(1)
            link(tt(pt(MG_), pt(MG_), pt(MG_), MUL))
            link(tt(pt(MG_), pt(MG_), pt(MG_), MUL))
            tt(r8[:], pt(MG_), pt(MG_), MUL).then_inc(s.r8, 1)
            dve.wait_ge(s.xb2_mm, 1)
            dve.wait_ge(s.b_in, 32)
            for h in range(2):
                gsl = slice(h * G // 2, (h + 1) * G // 2)
                x1 = XB1[:, gsl, :]
                x2 = XB2[:, gsl, :]
                fr = view(ysb, FR_ * 64 + h * G // 2, [[1, G // 2], [0, GC]])
                fi = view(ysb, FI_ * 64 + h * G // 2, [[1, G // 2], [0, GC]])
                link(tt(x2, ps(2 + h).rearrange("p (g c) -> p g c", c=GC), fi, MUL))
                link(tt(x1, x1, fr, MUL))
                tt(x1, x1, x2, ADD).then_inc(s.xb1, 1)
            dve.wait_ge(s.zeroed, 4)
            tmp4 = view(tmp, 0, [[P, GT], [GC, CH], [1, GC]])

            def build_p(m):
                after(dve, s.t_mm, m)
                if m == 0:
                    dve.wait_ge(s.xb2, 2)
                o = view(Pp, 0, [[PADJ * GC, GT], [GC, CH], [1, GC]])
                x1 = view(XB1, m * P, [[GC, GT], [0, CH], [1, GC]])
                x2 = view(XB2, m * P, [[GC, GT], [0, CH], [1, GC]])
                link(tt(tmp4, x2, powers_of(pw[1], m, CH - 1, -1), MUL))
                link(tt(o, x1, powers_of(pw[0], m, CH - 1, -1), MUL))
                tt(o, o, tmp4, ADD).then_inc(s.p_built, 1)

            def phase_table(m):
                o = [[NC, GT], [8, 8], [1, 8]]
                fr, fi = [view(t, m * GT, [[1, GT], [G, 8], [0, 8]]) for t in ft]
                gr, gi = [view(t, m * GT, [[1, GT], [0, 8], [G, 8]]) for t in gt]
                C, S_, A, B = view(Ct, 0, o), view(St, 0, o), view(tmp, 0, o), view(tmp, T, o)
                if m > 0:
                    dve.wait_ge(s.p_rot, m)
                else:
                    dve.wait_ge(s.phases, 1)
                dve.wait_ge(s.p_built, min(m + 2, KT))
                link(tt(A, fr, gr, MUL))
                link(tt(B, fi, gi, MUL))
                link(tt(C, A, B, SUB))
                link(tt(A, fr, gi, MUL))
                link(tt(B, fi, gr, MUL))
                link(tt(S_, A, B, ADD))

            def rotate(m):
                cut = [[NC, GT], [1, NC - 1]]
                A, B = view(w1, 1, cut), view(w2, 0, cut)
                C, S_ = view(Ct, 1, cut), view(St, 1, cut)
                dve.wait_ge(s.w_sw, 2 * (m + 1))
                after(dve, s.scan, m)
                link(tt(A, bass.AP(bk[5 + m % 2], 0, [[T, P]] + cut), C, MUL))
                link(tt(B, B, S_, MUL))
                tt(A, A, B, ADD).then_inc(s.rot, 1)
                dve.wait_ge(s.rot, m + 1)
                dve.wait_ge(s.ratio, m + 1)
                v.tensor_tensor_scan(gs[:], r8x[:], w1[:], 0.0, MUL, ADD).then_inc(s.scan, 1)
                dve.wait_ge(s.scan, m + 1)
                after(dve, s.h, m)
                if m == 0:
                    dve.wait_ge(s.rows_out, 32)
                link(tt(p1[:], gs[:], Ct[:], MUL))
                tt(p2[:], gs[:], St[:], MUL).then_inc(s.p_rot, 1)

            def combine(m):
                dve.wait_ge(y_in[m % 2], 16 * GT * (m // 2 + 1))
                stt(out=yT[:, m % 2, :], in0=uT[:, m % 4, :], scalar=vcol(V_D + m), in1=yT[:, m % 2, :],
                    op0=MUL, op1=ADD).then_inc(s.comb, 1)

            def gate(m):
                S = SLAB_OF["z", m]
                dve.wait_ge(s.w_used, S + 1)
                if m >= 2:
                    dve.wait_ge(z_out[m % 2], 16 * (m // 2))
                tt(st[:, m % 2, :], ps(S % 2), R[:], MUL).then_inc(s.z_ev, 1)

            def gate_out(m):
                dve.wait_ge(s.z_tanh, m + 1)
                stt(out=st[:, m % 2, :], in0=tz[:], scalar=1.0, in1=st[:, m % 2, :], op0=ADD,
                    op1=MUL).then_inc(s.zz, 1)

            build_p(0)
            build_p(1)
            u_out(2)
            phase_table(0)
            link(tt(small[:, 1:2], small[:, 5:6], small[:, 4:5], SUB))
            link(ts(small[:, 1:2], small[:, 1:2], -LAM_INIT, None, ADD))
            for m in range(KT):
                rotate(m)
                if m < KT - 2:
                    gate(m)
                if m + 2 < KT:
                    build_p(m + 2)
                if m < KT - 2:
                    gate_out(m)
                if m >= 1:
                    combine(m - 1)
                if m + 3 < KT:
                    u_out(m + 3)
                if m + 1 < KT:
                    phase_table(m + 1)
            for m in range(KT - 2, KT):
                gate(m)
                gate_out(m)
            for k in range(KT - 1):
                dve.wait_ge(s.y_hi, k + 1)
                tt(cols(lo0, k), cols(Y, k), cols(hi0, k).bitcast(F32), SUB).then_inc(s.y_lo, 1)
            combine(KT - 1)
            dve.wait_ge(s.y_hi, KT)
            tt(cols(lo0, KT - 1), cols(Y, KT - 1), cols(hi0, KT - 1).bitcast(F32), SUB).then_inc(s.y_lo, 1)

            def add_squares(m, to, sq, ready, before, done):
                if m > 0:
                    dve.wait_ge(ready, before + m + 1)
                    after(dve, s.acc, done + m - 1)
                    tt(to[:], to[:], sq[:, m % 2, :], ADD).then_inc(s.acc, 1)

            for m in range(KT):
                dve.wait_ge(s.w_used, S_GLU + 2 * m + 2)
                dve.wait_ge(s.glu_tanh, m + 1)
                y = tb[0][:, m % 2, :]
                stt(out=y, in0=tb[1][:, m % 2, :], scalar=1.0, in1=ps(2 * (m % 2) + 1), op0=ADD,
                    op1=MUL).then_inc(s.glu_y, 1)
                dve.wait_ge(s.glu_y, m + 1)
                if m == 0:
                    dve.wait_ge(s.zz_in, 16)
                after(dve, s.glu_hi, m - 1)
                stt(out=tb[2][:, m % 2, :], in0=y, scalar=0.25, in1=cols(zz, m), op0=MUL,
                    op1=MUL).then_inc(s.glu_y3, 1)
                dve.wait_ge(s.glu_hi, m + 1)
                tt(cols(lo1, m), tb[2][:, m % 2, :], cols(hi1, m).bitcast(F32), SUB).then_inc(s.glu_lo, 1)
                if m == 4:
                    for k in range(PK):
                        dve.wait_ge(s.p_hi, k + 1)
                        tt(plo[:, k, :], ps(4 + k), phi[:, k, :].bitcast(F32), SUB).then_inc(s.p_lo, 1)
            dve.wait_ge(s.xT_in, 16)
            for m in range(KT):
                dve.wait_ge(s.w_used, S_OUT + m + 1)
                tt(cols(xT, m), cols(xT, m), ps(4 + m % 2), ADD).then_inc(s.xa, 1)
                dve.wait_ge(s.xa_hi, m + 1)
                tt(cols(lo0, m), cols(xT, m), cols(hi0, m).bitcast(F32), SUB).then_inc(s.xa_lo, 1)
                add_squares(m, acc, tb[3], s.xa_sq, 0, 0)
            dve.wait_ge(s.r_norm, 2)
            dve.wait_ge(s.pr_ev, KT)
            for m in range(KT):
                dve.wait_ge(s.w_used, S_G0 + m + 1)
                tt(tb[0][:, m % 2, :], ps(4 + m % 2), R[:], MUL).then_inc(s.g_ev, 1)
                dve.wait_ge(s.g_tanh, m + 1)
                t = tb[1][:, m % 2, :]
                stt(out=t, in0=t, scalar=1.0, in1=cols(zz, m), op0=ADD, op1=MUL).then_inc(s.g_pr, 1)
                dve.wait_ge(s.g_pr, m + 1)
                if m >= 2:
                    dve.wait_ge(x1_out[m % 2], 16 * (m // 2))
                    dve.wait_ge(s.x1_sq, m - 1)
                stt(out=view(tb[2], (m % 2) * T, [[1, CH], [CH, NC]]),
                    in0=view(tb[1], (m % 2) * T, [[NC, CH], [1, NC]]), scalar=0.5,
                    in1=view(xT, m * T, [[NC, CH], [1, NC]]), op0=MUL, op1=ADD).then_inc(s.x1, 1)
                for hi, lo, g, hd, ld in ((hi1, lo1, V_KVG, s.n1_hi, s.n1_lo), (hi2, lo2, V_BG, s.n2_hi, s.n2_lo)):
                    dve.wait_ge(hd, m + 1)
                    stt(out=cols(lo, m), in0=tb[2][:, m % 2, :], scalar=vcol(g + m),
                        in1=cols(hi, m).bitcast(F32), op0=MUL, op1=SUB).then_inc(ld, 1)
                add_squares(m, acc, tb[3], s.x1_sq, 0, KT - 1)

            dve.wait_ge(s.r_norm, 3)
            for i in range(2):
                dve.wait_ge(x1_out[i], 16 * KT // 2)

            def project_ev(e):
                kind, m = HEAD_ORDER[e]
                dve.wait_ge(s.w_used, S_H + e + 1)
                if e >= 2:
                    k2, m2 = HEAD_ORDER[e - 2]
                    if k2 == "v":
                        dve.wait_ge(s.v_T, m2 + 1)
                    elif k2 == "z":
                        dve.wait_ge(s.sz, m2 + 1)
                    else:
                        dve.wait_ge(s.k_n, 2 * m2 + (k2 == "q") + 1)
                tt(ta[0][:, e % 2, :], ps(e % 2), R[:], MUL).then_inc(s.h_ev, 1)

            def project_n(e):
                kind, m = HEAD_ORDER[e]
                if kind in "kq":
                    n = 2 * m + (kind == "q")
                    dve.wait_ge(s.k_r, n + 1)
                    after(dve, s.k_lo, n)
                    stt(out=ta[2][:, e % 2, :], in0=ta[0][:, e % 2, :], scalar=vcol(V_KG if kind == "k" else V_QG),
                        in1=ta[1][:, e % 2, :], op0=MUL, op1=MUL).then_inc(s.k_n, 1)
                elif kind == "v":
                    dve.wait_ge(s.v_hi, m + 1)
                    tt(vl[:, m % 2, :], ps(7), vh[:, m % 2, :].bitcast(F32), SUB).then_inc(s.v_lo, 1)

            def project_lo(e):
                kind, m = HEAD_ORDER[e]
                if kind in "kq":
                    dve.wait_ge(s.k_hi, 2 * m + (kind == "q") + 1)
                    hi, lo = (kh, kl) if kind == "k" else (qh, ql)
                    tt(lo[:, m % 2, :], ta[2][:, e % 2, :], hi[:, m % 2, :].bitcast(F32), SUB).then_inc(s.k_lo, 1)

            def project_z(e):
                kind, m = HEAD_ORDER[e]
                if kind == "z":
                    dve.wait_ge(s.b_tanh, m + 1)
                    after(dve, s.o_ev, m - 1)
                    stt(out=sz[:, m % 2, :], in0=ta[1][:, e % 2, :], scalar=1.0, in1=ta[0][:, e % 2, :], op0=ADD,
                        op1=MUL).then_inc(s.sz, 1)

            def soft_in(j):
                m, I = divmod(j, QB)
                w = (I + 1) * P
                if I == 0:
                    dve.wait_ge(bias_in[m % 2], 16 * (m // 2 + 1))
                after(dve, s.at, j - 1)
                for c in range(2):
                    n = 2 * j + c
                    dve.wait_ge(s.sc, n + 1)
                    v.tensor_tensor_reduce(sco[c][:, j % 2, 0:w], ps(2 + c, w), bias[:, m % 2, T - w:T], 1.0,
                                           -3e38, ADD, ALU.max,
                                           stat[:, j % 2, 2 + c:3 + c]).then_inc(s.sc_read, 1)
                dve.wait_ge(s.sc_read, 2 * j + 2)
                ts(stat[:, j % 2, 4:6], stat[:, j % 2, 2:4], -1.0, None, MUL).then_inc(s.neg, 1)

            def soft_out(j):
                w = (j % QB + 1) * P
                dve.wait_ge(s.exp, 2 * j + 2)
                r = stat[:, j % 2, 8:10]
                link(v.reciprocal(r, stat[:, j % 2, 6:8]))
                link(tt(stat[:, j % 2, 10:11], stat[:, j % 2, 9:10], negl, MUL))
                link(ts(sco[0][:, j % 2, 0:w], sco[0][:, j % 2, 0:w], stat[:, j % 2, 8:9], None, MUL))
                stt(out=sco[0][:, j % 2, 0:w], in0=sco[1][:, j % 2, 0:w], scalar=stat[:, j % 2, 10:11],
                    in1=sco[0][:, j % 2, 0:w], op0=MUL, op1=ADD).then_inc(s.soft, 1)

            def at_lo(j):
                w = (j % QB + 1) * P
                dve.wait_ge(s.at_hi, j + 1)
                tt(atl[:, j % 2, 0:w], ps(4, w), ath[:, j % 2, 0:w].bitcast(F32), SUB).then_inc(s.at_lo, 1)

            def o_scale(m):
                dve.wait_ge(s.o_r, m + 1)
                for I in range(QB):
                    last = ts(on[:, I * P:(I + 1) * P], ps(5 + m % 2, P, I * P), oss[:, 8 + I:9 + I], None, MUL)
                last.then_inc(s.on, 1)

            def o_gate(m):
                dve.wait_ge(s.o_T, m + 1)
                dve.wait_ge(s.sz, m + 1)
                stt(out=on[:], in0=ps(5 + m % 2), scalar=vcol(V_SUB), in1=sz[:, m % 2, :], op0=MUL,
                    op1=MUL).then_inc(s.o_ev, 1)

            def o_lo_(m):
                dve.wait_ge(s.o_hi, m + 1)
                tt(cols(lo0, m), on[:], cols(hi0, m).bitcast(F32), SUB).then_inc(s.o_lo, 1)

            steps = H * QB
            slabs_h = len(HEAD_ORDER)
            for e in range(LEAD + steps + 4):
                j = e - LEAD
                if 1 <= e <= slabs_h:
                    project_ev(e - 1)
                if 0 <= j < steps:
                    soft_in(j)
                if 2 <= e <= slabs_h + 1:
                    project_n(e - 2)
                    project_lo(e - 2)
                if 0 <= j < steps:
                    soft_out(j)
                if e == slabs_h:
                    for k in range(PK):
                        dve.wait_ge(s.p_hi, PK + k + 1)
                        tt(plo2[:, k, :], ps((0, 7)[k]), phi2[:, k, :].bitcast(F32), SUB).then_inc(s.p_lo, 1)
                if 1 <= j <= steps:
                    at_lo(j - 1)
                if 1 <= e <= slabs_h:
                    project_z(e - 1)
                if j >= QB + 1 and (j - 1) % QB == 0:
                    o_scale((j - 1) // QB - 1)
                if j >= QB + 2 and (j - 2) % QB == 0:
                    o_gate((j - 2) // QB - 1)
                if j >= QB + 3 and (j - 3) % QB == 0:
                    o_lo_((j - 3) // QB - 1)

            dve.wait_ge(s.x1_in, 16)
            for m in range(KT):
                dve.wait_ge(s.w_used, S_BO + m + 1)
                tt(cols(x1b, m), cols(x1b, m), ps(4 + m % 2), ADD).then_inc(s.xa, 1)
                dve.wait_ge(s.xa_hi, KT + m + 1)
                tt(cols(lo1, m), cols(x1b, m), cols(hi1, m).bitcast(F32), SUB).then_inc(s.xa_lo, 1)
                add_squares(m, acc2, tc[3], s.xa_sq, KT, 2 * (KT - 1))
            dve.wait_ge(s.r_norm, 4)
            for m in range(KT):
                dve.wait_ge(s.w_used, S_G1 + m + 1)
                tt(tc[0][:, m % 2, :], ps(4 + m % 2), R[:], MUL).then_inc(s.g_ev, 1)
                dve.wait_ge(s.g_tanh, KT + m + 1)
                dve.wait_ge(s.pr2_ev, KT)
                t = tc[1][:, m % 2, :]
                stt(out=t, in0=t, scalar=1.0, in1=cols(pr2, m), op0=ADD, op1=MUL).then_inc(s.g_pr, 1)
                dve.wait_ge(s.g_pr, KT + m + 1)
                after(dve, s.out_T, m - 1)
                stt(out=tc[2][:, m % 2, :], in0=t, scalar=0.5, in1=cols(x1b, m), op0=MUL,
                    op1=ADD).then_inc(s.x2, 1)


_INS = ["x", "p", "a_norm_g", "a_w_in", "a_lam_re", "a_lam_im", "a_log_dt", "a_b_re", "a_b_im", "a_c_re",
        "a_c_im", "a_d", "a_w_glu", "a_w_out", "kv_norm_g", "w_k", "w_v", "k_norm_g", "b_norm_g", "b_w_in",
        "b_q_norm_g", "b_lam_q1", "b_lam_k1", "b_lam_q2", "b_lam_k2", "b_subln_g", "b_w_out", "rel_bias",
        "ple_w_proj", "ple_w_gate"]


def constants():
    c = np.zeros((P, C_END), np.float32)
    c[:, C_ID:C_ID + P] = np.eye(P)
    i = np.arange(ST)
    c[i, C_J1 + ST + i] = 1.0
    c[ST + i, C_J1 + i] = -1.0
    c[i, C_J2 + ST + i] = -1.0
    c[ST + i, C_J2 + i] = 1.0
    c[:, C_ONE:C_ONE + P] = 1.0
    c[:HD, C_BLK:C_BLK + HD] = 1.0
    c[HD:, C_BLK + HD:C_BLK + P] = 1.0
    rel = T - 1 - np.arange(REV)
    n = np.maximum(rel, 1).astype(np.float32)
    exact = BUCKETS // 2
    large = exact + (np.log(n / np.float32(exact)) / np.float32(math.log(128 / exact))
                     * np.float32(BUCKETS - exact)).astype(np.int32)
    bucket = np.where(rel < exact, rel, np.minimum(large, BUCKETS - 1))
    bucket = np.where(rel < 0, BUCKETS, bucket)
    c[bucket, C_HOT + np.arange(REV)] = 1.0
    c[:ST, C_SGN] = 1.0
    c[ST:, C_SGN] = -1.0
    return c


def kernel(**inputs):
    import concourse.bacc as _bacc
    from concourse.bass_utils import run_bass_kernel_spmd as _run

    nc = _bacc.Bacc("TRN2", target_bir_lowering=False, num_devices=1)
    arrays, args = {}, {}
    for name in _INS + ["consts"]:
        v = constants() if name == "consts" else np.ascontiguousarray(inputs[name])
        arrays[f"in_{name}"] = v
        args[name] = nc.dram_tensor(f"in_{name}", v.shape, mybir.dt.from_np(v.dtype), kind="ExternalInput").ap()
    out = nc.dram_tensor("out_x", (1, T, D), F32, kind="ExternalOutput").ap()
    build(nc, args, out)
    r = _run(nc, [arrays], core_ids=[0])
    return r.results[0]["out_x"]
```
